# Optimizing a Trainium2 kernel written in Bass

```python
import jax, jax.numpy as jnp
from jax import lax
import numpy as np

D_MODEL = 1024
BATCH = 1
SEQ = 1024
DEPTH = 2

CTX_LEN = 256
GRID_W = 64
EXPAND = 2
D_INNER = EXPAND * D_MODEL
D_A = D_INNER // 2
D_B = D_INNER - D_A
N_HEADS_A = 4
HEAD_DIM_A = D_A // N_HEADS_A
N_GROUPS_B = 4
GROUP_B = D_B // N_GROUPS_B
N_GROUPS_C = 4
GROUP_C = D_INNER // N_GROUPS_C
POOL_WINDOWS = (2, 4, 8, 16)
CONV_W = 3
CHUNK = 64
N_GATES = 4 * N_HEADS_A
W_IN_EVEN = 5 * D_A + 2 * D_B + N_GATES
W_IN_ODD = 2 * D_INNER
EPS = 1e-6

kernel_name = 'hybrid_mlstm_fourier_pool_dit'

f32 = jnp.float32

def _rmsnorm(a, g):
    af = a.astype(f32)
    af = af * lax.rsqrt(jnp.mean(af * af, axis=-1, keepdims=True) + EPS)
    return (af * g.astype(f32)).astype(a.dtype)

def _short_conv(u, w):
    T = u.shape[1]
    pad = CONV_W // 2
    up = jnp.pad(u, ((0, 0), (pad, CONV_W - 1 - pad), (0, 0)))
    out = w[0] * up[:, 0:T]
    for j in range(1, CONV_W):
        out = out + w[j] * up[:, j:j + T]
    return out

def _mlstm_chunked(q, k, v, ig, lf, state):
    B, H, T, Dh = q.shape
    nc = T // CHUNK

    def to_chunks(a):
        return jnp.moveaxis(a.reshape(a.shape[:2] + (nc, CHUNK) + a.shape[3:]), 2, 0)

    mask = jnp.tril(jnp.ones((CHUNK, CHUNK), dtype=bool))

    def step(carry, inp):
        C, n, m = carry
        qc, kc, vc, ic, fc = inp
        b = jnp.cumsum(fc, axis=-1)
        dm = b[..., :, None] - b[..., None, :] + ic[..., None, :]
        dm = jnp.where(mask, dm, -jnp.inf)
        m_inter = b + m[..., None]
        m_t = jnp.maximum(jnp.max(dm, axis=-1), m_inter)
        s = jnp.einsum('bhtd,bhsd->bhts', qc, kc) * jnp.exp(dm - m_t[..., None])
        inter = jnp.exp(m_inter - m_t)
        num = jnp.einsum('bhts,bhsd->bhtd', s, vc) + inter[..., None] * jnp.einsum('bhtd,bhde->bhte', qc, C)
        den = jnp.sum(s, axis=-1) + inter * jnp.einsum('bhtd,bhd->bht', qc, n)
        h = num / jnp.maximum(jnp.abs(den), jnp.exp(-m_t))[..., None]
        b_end = b[..., -1]
        w_s = b_end[..., None] - b + ic
        m_new = jnp.maximum(b_end + m, jnp.max(w_s, axis=-1))
        decay = jnp.exp(b_end + m - m_new)
        ws = jnp.exp(w_s - m_new[..., None])
        C_new = decay[..., None, None] * C + jnp.einsum('bhs,bhsd,bhse->bhde', ws, kc, vc)
        n_new = decay[..., None] * n + jnp.einsum('bhs,bhsd->bhd', ws, kc)
        return (C_new, n_new, m_new), h

    final, hs = lax.scan(step, state, (to_chunks(q), to_chunks(k), to_chunks(v), to_chunks(ig), to_chunks(lf)))
    h = jnp.moveaxis(hs, 0, 2).reshape(B, H, T, Dh)
    return h, final

def _to_heads(a):
    B, T, _ = a.shape
    return a.reshape(B, T, N_HEADS_A, HEAD_DIM_A).transpose(0, 2, 1, 3).astype(f32)

def _project_even(h, win, gate_b, conv_qk):
    B, T, _ = h.shape
    p = h @ win
    qk = jax.nn.silu(_short_conv(p[..., :2 * D_A], conv_qk))
    q = _to_heads(qk[..., :D_A]) * (HEAD_DIM_A ** -0.5)
    k = _to_heads(qk[..., D_A:])
    v = _to_heads(p[..., 2 * D_A:3 * D_A])
    o = p[..., 3 * D_A:4 * D_A]
    z_a = p[..., 4 * D_A:5 * D_A]
    u_b = p[..., 5 * D_A:5 * D_A + D_B]
    z_b = p[..., 5 * D_A + D_B:5 * D_A + 2 * D_B]
    g = (p[..., 5 * D_A + 2 * D_B:] + gate_b).astype(f32)
    g = g.reshape(B, T, 4, N_HEADS_A).transpose(2, 0, 3, 1)
    gates = (g[0], jax.nn.log_sigmoid(g[1]), g[2], jax.nn.log_sigmoid(g[3]))
    return (q, k, v), gates, (o, z_a, u_b, z_b)

def _mlstm_bidir(qkv_c, gates_c, qkv_x, gates_x):
    B, H, _, Dh = qkv_c[0].shape
    zero = (jnp.zeros((B, H, Dh, Dh), f32), jnp.zeros((B, H, Dh), f32), jnp.zeros((B, H), f32))

    def flip(a):
        return jnp.flip(a, axis=2)

    hc_f, st_f = _mlstm_chunked(*qkv_c, gates_c[0], gates_c[1], zero)
    hx_f, _ = _mlstm_chunked(*qkv_x, gates_x[0], gates_x[1], st_f)
    hc_b, st_b = _mlstm_chunked(*map(flip, qkv_c), flip(gates_c[2]), flip(gates_c[3]), zero)
    hx_b, _ = _mlstm_chunked(*map(flip, qkv_x), flip(gates_x[2]), flip(gates_x[3]), st_b)
    return hc_f + flip(hc_b), hx_f + flip(hx_b)

def _fourier_mix(u, fw):
    B, T, _ = u.shape
    ug = u.astype(f32).reshape(B, T, N_GROUPS_B, GROUP_B)
    y = jnp.fft.fft2(ug, axes=(1, 3), norm='ortho').real
    return jnp.einsum('btgc,gcd->btgd', y, fw.astype(f32)).reshape(B, T, D_B)

def _even_out(h, extra, head_g, fw, wout, dtype):
    o, z_a, u_b, z_b = extra
    B, H, T, Dh = h.shape
    h = jax.nn.sigmoid(o.astype(f32)).reshape(B, T, H, Dh) * h.transpose(0, 2, 1, 3)
    h = h * lax.rsqrt(jnp.mean(h * h, axis=-1, keepdims=True) + EPS)
    y_a = h.reshape(B, T, D_A) * head_g.astype(f32) * jax.nn.silu(z_a.astype(f32))
    y_b = _fourier_mix(u_b, fw) * jax.nn.silu(z_b.astype(f32))
    y = jnp.concatenate([y_a, y_b], axis=-1).astype(dtype)
    return y @ wout

def _box_mean(u, axis, w):
    n = u.shape[axis]
    pads = [(1, 0) if a == axis else (0, 0) for a in range(u.ndim)]
    P = jnp.pad(jnp.cumsum(u, axis=axis), pads)
    idx = jnp.arange(n)
    lo = jnp.clip(idx - w // 2, 0, n)
    hi = jnp.clip(idx + w - w // 2, 0, n)
    s = jnp.take(P, hi, axis=axis) - jnp.take(P, lo, axis=axis)
    cnt = (hi - lo).astype(u.dtype).reshape((n,) + (1,) * (u.ndim - axis - 1))
    return s / cnt

def _pool_mix(u, pool_w, scale, rows):
    B, T, _ = u.shape
    parts = []
    for g, w in enumerate(POOL_WINDOWS):
        ug = u[..., g * GROUP_C:(g + 1) * GROUP_C].astype(f32)
        if rows is None:
            m = _box_mean(ug, 1, w)
        else:
            grid = ug.reshape(B, rows, GRID_W, GROUP_C)
            m = _box_mean(_box_mean(grid, 1, w), 2, w).reshape(B, T, GROUP_C)
        parts.append(m - ug)
    y = jnp.stack(parts, axis=2)
    y = jnp.einsum('btgc,gcd->btgd', y, pool_w.astype(f32)).reshape(B, T, D_INNER)
    return y * scale.astype(f32)

def _odd_branch(h, win, pool_w, scale, wout, rows):
    p = h @ win
    y = _pool_mix(p[..., :D_INNER], pool_w, scale, rows) * jax.nn.silu(p[..., D_INNER:].astype(f32))
    return y.astype(h.dtype) @ wout

def setup_inputs(seed: int = 0) -> dict:
    key = jax.random.key(seed)
    ks = jax.random.split(key, 20)
    n_even = (DEPTH + 1) // 2
    n_odd = DEPTH // 2
    nrm = jax.random.normal
    x = nrm(ks[0], (BATCH, SEQ, D_MODEL), f32)
    c = nrm(ks[1], (BATCH, D_MODEL), f32)
    ctx = nrm(ks[2], (BATCH, CTX_LEN, D_MODEL), f32)
    c_ctx = nrm(ks[3], (D_MODEL,), f32)
    ada_w = nrm(ks[4], (DEPTH, D_MODEL, 3 * D_MODEL), f32) * (0.5 * D_MODEL ** -0.5)
    ada_b = 0.02 * nrm(ks[5], (DEPTH, 3 * D_MODEL), f32)
    norm_g = 1.0 + 0.1 * nrm(ks[6], (DEPTH, D_MODEL), f32)
    win_even = nrm(ks[7], (n_even, D_MODEL, W_IN_EVEN), f32) * (D_MODEL ** -0.5)
    i_bias = 0.1 * nrm(ks[8], (n_even, 2, N_HEADS_A), f32)
    f_bias = jnp.linspace(3.0, 6.0, N_HEADS_A, dtype=f32) + 0.1 * nrm(ks[9], (n_even, 2, N_HEADS_A), f32)
    gate_b_even = jnp.stack([i_bias[:, 0], f_bias[:, 0], i_bias[:, 1], f_bias[:, 1]], axis=1).reshape(n_even, N_GATES)
    conv_qk_even = nrm(ks[10], (n_even, CONV_W, 2 * D_A), f32) * (CONV_W ** -0.5)
    head_norm_even = 1.0 + 0.1 * nrm(ks[11], (n_even, D_A), f32)
    fourier_w_even = nrm(ks[12], (n_even, N_GROUPS_B, GROUP_B, GROUP_B), f32) * (GROUP_B ** -0.5)
    wout_even = nrm(ks[13], (n_even, D_INNER, D_MODEL), f32) * (D_INNER ** -0.5)
    win_odd = nrm(ks[14], (n_odd, D_MODEL, W_IN_ODD), f32) * (D_MODEL ** -0.5)
    pool_w_odd = nrm(ks[15], (n_odd, N_GROUPS_C, GROUP_C, GROUP_C), f32) * (GROUP_C ** -0.5)
    pool_scale_odd = 1.0 + 0.1 * nrm(ks[16], (n_odd, D_INNER), f32)
    wout_odd = nrm(ks[17], (n_odd, D_INNER, D_MODEL), f32) * (D_INNER ** -0.5)
    final_g = 1.0 + 0.1 * nrm(ks[18], (D_MODEL,), f32)
    return {'x': x, 'c': c, 'ctx': ctx, 'c_ctx': c_ctx, 'ada_w': ada_w, 'ada_b': ada_b, 'norm_g': norm_g,
            'win_even': win_even, 'gate_b_even': gate_b_even, 'conv_qk_even': conv_qk_even,
            'head_norm_even': head_norm_even, 'fourier_w_even': fourier_w_even, 'wout_even': wout_even,
            'win_odd': win_odd, 'pool_w_odd': pool_w_odd, 'pool_scale_odd': pool_scale_odd,
            'wout_odd': wout_odd, 'final_g': final_g}

def reference(x, c, ctx, c_ctx, ada_w, ada_b, norm_g, win_even, gate_b_even, conv_qk_even,
              head_norm_even, fourier_w_even, wout_even, win_odd, pool_w_odd, pool_scale_odd,
              wout_odd, final_g):
    rows = x.shape[1] // GRID_W
    for l in range(DEPTH):
        even = (l % 2 == 0)
        ctx_out = l < DEPTH - 1
        mod_x = jax.nn.silu(c) @ ada_w[l] + ada_b[l]
        shift_x, scale_x, gate_x = jnp.split(mod_x[:, None, :], 3, axis=-1)
        hx = _rmsnorm(x, norm_g[l]) * (1 + scale_x) + shift_x
        if even or ctx_out:
            mod_c = jax.nn.silu(c_ctx) @ ada_w[l] + ada_b[l]
            shift_c, scale_c, gate_c = jnp.split(mod_c, 3, axis=-1)
            hc = _rmsnorm(ctx, norm_g[l]) * (1 + scale_c) + shift_c
        if even:
            e = l // 2
            qkv_x, gates_x, extra_x = _project_even(hx, win_even[e], gate_b_even[e], conv_qk_even[e])
            qkv_c, gates_c, extra_c = _project_even(hc, win_even[e], gate_b_even[e], conv_qk_even[e])
            h_c, h_x = _mlstm_bidir(qkv_c, gates_c, qkv_x, gates_x)
            y_x = _even_out(h_x, extra_x, head_norm_even[e], fourier_w_even[e], wout_even[e], x.dtype)
            if ctx_out:
                y_c = _even_out(h_c, extra_c, head_norm_even[e], fourier_w_even[e], wout_even[e], ctx.dtype)
        else:
            o = l // 2
            y_x = _odd_branch(hx, win_odd[o], pool_w_odd[o], pool_scale_odd[o], wout_odd[o], rows)
            if ctx_out:
                y_c = _odd_branch(hc, win_odd[o], pool_w_odd[o], pool_scale_odd[o], wout_odd[o], None)
        x = x + gate_x * y_x
        if ctx_out:
            ctx = ctx + gate_c * y_c
    return _rmsnorm(x, final_g)


_drawn_inputs = setup_inputs


def setup_inputs(seed=0):
    import zlib

    import numpy as np

    out = dict(_drawn_inputs(seed))
    spreads = {}
    factors = {'ctx': 4.536, 'c_ctx': 2.78, 'head_norm_even': 4.202, 'pool_scale_odd': 2.984}
    for name, (base, spread) in spreads.items():
        noise = np.random.default_rng([zlib.crc32(name.encode()), seed]).standard_normal(out[name].shape)
        drawn = base * np.exp(spread * noise) if base else spread * noise
        out[name] = __import__('jax').numpy.asarray(drawn.astype(out[name].dtype))
    for name, factor in factors.items():
        out[name] = (out[name] * factor).astype(out[name].dtype)
    return out
```

```python
from contextlib import ExitStack

import numpy as np

import concourse.bass as bass
from concourse import mybir

F32 = mybir.dt.float32
F32R = mybir.dt.float32r
ALU = mybir.AluOpType
ACT = mybir.ActivationFunctionType

P = 128
D = 1024
KB = D // P
T = 1024
TC = 256
HALF = 512
HEADS = 4
DH = 256
GROUPS = 4
GRID_W = 64
GRID_H = T // GRID_W
WINDOWS = (2, 4, 8, 16)
EPS = 1e-6
CHUNK = 128
NCC, NCX = TC // CHUNK, T // CHUNK
NCH = NCC + NCX
BIG = 1e30
RADIX = 4
TF = T // RADIX

HEAD_UNITS = [1] * 10 + [4, 4]
FOUR_UNITS = [1] * 4 + [4, 4]
POOL_UNITS = [1] * 4 + [2, 2] + [1] * 4 + [2] * 4
CREDIT = 8
STEP_CREDIT = 96


class Steps:

    def __init__(self, sem, base, names, times=1):
        self.sem, self.base, self.names, self.times = sem, base, list(names), times
        self.index = {n: i for i, n in enumerate(self.names)}
        assert len(self.index) == len(self.names)
        self.next = 0

    def at(self, name, i=0):
        return self.base + i * len(self.names) + self.index[name] + 1

    @property
    def end(self):
        return self.base + self.times * len(self.names)

    def done(self, ins, name):
        assert self.names[self.next % len(self.names)] == name, (name, self.names[self.next % len(self.names)])
        self.next += 1
        ins.then_inc(self.sem, 1)


def nat_chunk(direction, j):
    if direction == 0:
        return j
    return NCC - 1 - j if j < NCC else NCC + NCX - 1 - (j - NCC)


def program(nc, x, c, ctx_in, c_ctx, ada_w, ada_b, norm_g, win_even, gate_b, conv_qk, head_norm, fourier_w,
            wout_even, win_odd, pool_w, pool_scale, wout_odd, final_g, tab_ident, tab_mask, tab_ct, tab_ns,
            tab_cc, tab_cs, tab_inv, out):
    stack = ExitStack()
    with stack:
        def sem(name):
            return stack.enter_context(nc.semaphore(name))

        cursor = [-(-nc.sbuf_base // 64) * 64]

        def at(name, shape, dt, offset):
            return nc.alloc_sbuf_tensor_at(name, shape, dt, offset=offset)

        def size(shape):
            return -(-int(np.prod(shape[1:])) * 4 // 32) * 32

        def fixed(name, shape, dt=F32):
            t = at(name, shape, dt, cursor[0])
            cursor[0] += size(shape)
            return t

        class Region:
            def __init__(self, start):
                self.at = start

            def __call__(self, name, shape, dt=F32):
                t = at(name, shape, dt, self.at)
                self.at += size(shape)
                assert self.at <= nc.sbuf_usable_end, (name, self.at)
                return t

        ident = fixed("ident", [P, P])
        ones = fixed("ones", [P, P])
        mask = fixed("mask", [P, 2, CHUNK])
        zero = fixed("zero", [P, 1])
        eps = fixed("eps", [P, 1])
        seed = fixed("seed", [P, 4])
        vec = fixed("vec", [P, 176])
        mod = fixed("mod", [P, 2, 24, 2])
        gain = fixed("gain", [P, 3, KB])
        cols = fixed("cols", [P, 3, NCH, 8])
        chunk_sc = fixed("chunk_sc", [P, 8, 2, NCH])
        w_raw = [fixed(f"w_raw{i}", [P, D]) for i in range(2)]
        w_hi = [fixed(f"w_hi{i}", [P, D], F32R) for i in range(2)]
        w_lo = [fixed(f"w_lo{i}", [P, D], F32R) for i in range(2)]
        h_hi = fixed("h_hi", [P, KB, T], F32R)
        h_lo = fixed("h_lo", [P, KB, T], F32R)
        resid = fixed("resid", [P, KB, T])
        arena = cursor[0]

        ADA_B, NORM_G, FINAL_G, HEAD_G, POOL_S, C_VEC, CONV = 0, 48, 64, 72, 80, 96, P

        r = Region(arena)
        hc_hi = r("hc_hi", [P, KB, TC], F32R)
        hc_lo = r("hc_lo", [P, KB, TC], F32R)
        after_ctx = r.at
        tok = [r(f"tok{i}", [P, D]) for i in range(2)]
        xc_t = r("xc_t", [P, KB, TC])
        n_sq = [r(f"n_sq{i}", [P, HALF]) for i in range(2)]
        n_t = [r(f"n_t{i}", [P, HALF]) for i in range(2)]
        n_h = [r(f"n_h{i}", [P, HALF]) for i in range(2)]
        n_rs = r("n_rs", [P, HALF])
        ada_buf = r("ada_buf", [P, 8, 512])
        vrow = r("vrow", [P, 2, P])
        c_silu = r("c_silu", [P, KB, 2])
        mrow = [r(f"mrow{i}", [2, 512]) for i in range(2)]
        r = Region(after_ctx)
        g_w = r("g_w", [P, KB, 2, P])
        g_wh = r("g_wh", [P, KB, 2, P], F32R)
        g_wl = r("g_wl", [P, KB, 2, P], F32R)
        g_in = r("g_in", [P, KB, 16])
        g_i = r("g_i", [64, TC + T])
        g_f = r("g_f", [64, TC + T])
        g_e = r("g_e", [64, TC + T])
        g_b = r("g_b", [64, TC + T])
        g_small = r("g_small", [64, 3, NCH])
        g_bias = r("g_bias", [64, 2])
        r = Region(after_ctx)
        g_g = r("g_g", [64, TC + T])
        g_d = r("g_d", [64, TC + T])
        g_nat = r("g_nat", [64, TC + T])
        g_s = r("g_s", [64, TC + T])
        assert r.at <= after_ctx + 3 * size([P, KB, 2, P])
        r = Region(after_ctx)
        q_t = r("q_t", [P, 2, T])
        kk = r.at
        k_t = r("k_t", [P, 2, TC + T])
        k_tok = r("k_tok", [P, NCH, DH])
        v_tok = r("v_tok", [P, NCH, DH + 1])
        cst = r("cst", [P, 2, 2, DH + 1])
        gg = r.at
        g_bc = r("g_bc", [P, 2, T])
        hh = r.at
        h_tok = r("h_tok", [P, NCX, DH])
        kw = [r(f"kw{d}", [P, DH]) for d in range(2)]
        qi = [r(f"qi{d}", [P, 2, CHUNK]) for d in range(2)]
        pr = [r(f"pr{d}", [P, CHUNK]) for d in range(2)]
        ee = [r(f"ee{d}", [P, CHUNK]) for d in range(2)]
        it = [r(f"it{d}", [P, CHUNK]) for d in range(2)]
        dn = r("dn", [P, 2, 4])
        r = Region(kk)
        yh2 = r("yh2", [P, 2, T], F32R)
        yl2 = r("yl2", [P, 2, T], F32R)
        r = Region(gg)
        ev_a = [r(f"ev_a{i}", [P, T]) for i in range(2)]
        r = Region(hh)
        cb = r("cb", [P, T + 2])
        cbc = r("cbc", [P, TC + 2])
        cv = r("cv", [P, TC + T])
        r = Region(arena)
        pq = r("pq", [P, 2, RADIX, 2 * DH])
        fd = r("fd", [P, 2, RADIX, TF])
        f_tmp = r("f_tmp", [P, 2, 2, TF])
        f_b = r("f_b", [P, 2 * DH])
        ct = r("ct", [P, 2, T])
        ns = r("ns", [P, 2, T])
        cfsf = r("cfsf", [P, 2, 2 * DH])
        ccs = r("ccs", [P, 2, 2, DH])
        fw = r("fw", [P, 2, DH])
        ev_f = [r(f"ev_f{i}", [P, T]) for i in range(2)]
        yh_f = r("yh_f", [P, 2, T], F32R)
        yl_f = r("yl_f", [P, 2, T], F32R)
        r = Region(arena)
        u_f = r("u_f", [P, 2, T])
        r = Region(arena + size([P, 2, RADIX, 2 * DH]))
        y_f = r("y_f", [P, 2, T])
        r = Region(arena)
        u_p = r("u_p", [P, 4, T])
        yh_p = r("yh_p", [P, 4, T], F32R)
        yl_p = r("yl_p", [P, 4, T], F32R)
        pt = [r(f"pt{i}", [P, 2048]) for i in range(2)]
        inv = r("inv", [P, T])
        r2 = Region(arena + 3 * size([P, 4, T]) + 2 * size([P, 2048]) + size([P, T]))
        ev_p = [r2(f"ev_p{i}", [P, T]) for i in range(2)]
        r = Region(arena)
        m_sq = [r(f"m_sq{i}", [P, HALF]) for i in range(2)]
        m_t = [r(f"m_t{i}", [P, HALF]) for i in range(2)]
        m_h = [r(f"m_h{i}", [P, HALF]) for i in range(2)]
        m_rs = r("m_rs", [P, HALF])
        o_tok = [r(f"o_tok{i}", [P, D]) for i in range(2)]

        ps = [stack.enter_context(nc.psum_tensor(f"ps{i}", [P, 2, HALF], F32)) for i in range(4)]

        g_dram = nc.dram_tensor("g_scratch", [8, TC + T], F32)
        s_dram = nc.dram_tensor("s_scratch", [8, 2 * NCH], F32)

        w_landed = [sem("w_landed0"), sem("w_landed1")]
        w_high = sem("w_high")
        w_ready = sem("w_ready")
        unit_done = sem("unit_done")
        unit_out = sem("unit_out")
        ctx_out = sem("ctx_out")
        pe_step, act_step, dve_step = sem("pe_step"), sem("act_step"), sem("dve_step")
        rows_clear = sem("rows_clear")
        bias_clear = sem("bias_clear")
        c_const = sem("c_const")
        c_vec = sem("c_vec")
        c_tok = [sem("c_tok0"), sem("c_tok1")]
        c_ada = sem("c_ada")
        c_gate = sem("c_gate")
        c_rows = sem("c_rows")
        c_bc = sem("c_bc")
        c_gbc = sem("c_gbc")
        c_four = sem("c_four")
        c_fw = sem("c_fw")
        c_inv = sem("c_inv")
        c_out = [sem("c_out0"), sem("c_out1")]

        DIRS = (0, 1)
        norm_x = [f"n{h}" for h in range(2)]

        def norm_names(tag):
            return {"pe": [f"{tag}sum"],
                    "act": [f"{tag}sq{k}" for k in range(KB)] + [f"{tag}std"]
                    + [f"{tag}h{k}" for k in range(KB)] + [f"{tag}hi{k}" for k in range(KB)],
                    "dve": [f"{tag}rs"] + [f"{tag}t{k}" for k in range(KB)] + [f"{tag}lo{k}" for k in range(KB)]}

        pos = {"pe": STEP_CREDIT, "act": STEP_CREDIT, "dve": STEP_CREDIT}
        sems = {"pe": pe_step, "act": act_step, "dve": dve_step}

        def stage(names, times=1):
            out_ = {}
            for e in ("pe", "act", "dve"):
                s = Steps(sems[e], pos[e], names.get(e, []), times)
                pos[e] = s.end
                out_[e] = s
            return out_

        NT = T // P
        st_vec = stage({"pe": ["vecT"], "act": ["silu_c"], "dve": ["vec"]})
        st_tok = stage({"pe": ["t0", "t1"], "act": ["c0", "c1"]}, NT // 2)
        st_tokc = stage({"pe": ["t0", "t1"], "act": ["c0", "c1"]})
        st_ada = stage({"pe": ["mm", "tr"], "act": ["row"], "dve": ["col"]}, 12)
        st_gain = stage({"dve": ["gain"]})

        def norm_stage(tag):
            a = [f"sq{k}" for k in range(KB)] + ["std"]
            for k in range(KB):
                a += [f"h{k}", f"hi{k}"]
            v = ["rs"]
            for k in range(KB):
                v.append(f"t{k}")
                if k >= 1:
                    v.append(f"lo{k - 1}")
            v.append(f"lo{KB - 1}")
            return stage({"pe": [f"s{k}" for k in range(KB)], "act": a, "dve": v})

        st_n0 = [norm_stage("x0"), norm_stage("x1"), norm_stage("c")]
        st_gate = stage({"pe": ["gates", "colsA", "colsW", "colsE"],
                         "act": ["ln", "w", "em"],
                         "dve": ["w_lo", "f", "G", "g_nat", "a_nat", "w_in", "w_nat", "e_in", "e_nat", "cols"]})

        head_act, head_dve, head_pe = [], [], []
        head_pe += ["vT0", "vT1"]
        for n in ("q0", "q1", "k0", "k1"):
            head_dve.append(f"conv_{n}")
            head_act.append(f"silu_{n}")
            if n == "k0":
                head_dve.append("vtok0")
            if n == "k1":
                head_dve.append("vtok1")
        head_pe += ["kT0", "kT1"]
        head_dve += ["ktok0", "ktok1"]
        for j in range(NCH):
            for d in DIRS:
                if j >= NCC:
                    head_pe.append(f"S{j}{d}")
                    head_dve.append(f"E{j}{d}")
                    head_act += [f"D{j}{d}", f"I{j}{d}"]
                    head_dve += [f"P{j}{d}", f"Q{j}{d}"]
                    head_pe.append(f"N{j}{d}")
                if j < NCH - 1:
                    head_dve.append(f"kw{j}{d}")
                    head_pe.append(f"U{j}{d}")
                if j >= NCC:
                    head_dve.append(f"h{j}{d}")
                if j < NCH - 1:
                    head_dve.append(f"C{j}{d}")
        head_pe += ["hT0", "hT1"]
        head_dve += ["hf0", "hf1", "o0", "o1"]
        head_act += ["sq0", "sq1"]
        head_pe += ["hsum"]
        head_act += ["hstd"]
        head_dve += ["hrs", "z0", "z1"]
        head_act += ["yh0", "yh1"]
        head_dve += ["yl0", "yl1"] + [f"acc{m}" for m in range(KB)]
        st_head = stage({"pe": head_pe, "act": head_act, "dve": head_dve}, HEADS)

        st_four = stage({
            "pe": ["cf", "V0", "V1", "V2", "V3", "V4", "V5", "V6", "V7", "Y0", "Y1"],
            "act": ["cf", "y0", "y1", "yh0", "yh1"],
            "dve": ["fold", "V0", "V1", "V2", "V3", "V4", "V5", "V6", "V7", "z0", "z1", "yl0", "yl1"]
            + [f"acc{m}" for m in range(KB)]}, GROUPS)
        st_n1 = [norm_stage("x0"), norm_stage("x1")]
        st_pool = stage({
            "act": [f"ph{m}" for m in range(4)] + [f"yh{m}" for m in range(4)],
            "dve": [f"p{m}" for m in range(4)] + [f"pl{m}" for m in range(4)] + [f"z{m}" for m in range(4)]
            + [f"yl{m}" for m in range(4)] + [f"acc{m}" for m in range(KB)]}, GROUPS)
        st_n2 = [norm_stage("x0"), norm_stage("x1")]
        st_end = stage({"pe": ["t0", "t1"], "act": ["c0", "c1"]}, NT // 2)

        HU, FU, PU = sum(HEAD_UNITS), sum(FOUR_UNITS), sum(POOL_UNITS)
        U_FOUR = HEADS * HU
        U_POOL = U_FOUR + GROUPS * FU
        B_FOUR = HEADS * len(HEAD_UNITS)
        B_POOL = B_FOUR + GROUPS * len(FOUR_UNITS)

        we = win_even[0].rearrange("(k p) m -> p k m", p=P)
        wo = win_odd[0].rearrange("(k p) m -> p k m", p=P)
        woe = wout_even[0].rearrange("(k p) m -> p k m", p=P)
        woo = wout_odd[0].rearrange("(k p) m -> p k m", p=P)
        pw = pool_w[0].rearrange("g (k p) m -> p (g k) m", p=P)
        ada_v = ada_w.rearrange("l (k p) (b m) -> p l k b m", p=P, m=512)

        def bcast(dram, offset, n):
            a = dram[:].rearrange("a b -> (a b)")
            return a[bass.ds(offset, n)].partition_broadcast(P)

        def bcast_ap(dram, g):
            return dram.rearrange("a b -> (a b)")[bass.ds(g * T, T)].partition_broadcast(P)

        def accumulate(act, u, ev, layer, SD, i, last):
            for m in range(KB):
                act.wait_ge(unit_done, u + m + 1 + CREDIT)
                act.wait_ge(dve_step, SD.at(f"acc{m - 2}" if m >= 2 else
                                            f"{last}{(m if last == 'z' and layer == 0 else m + 2)}", i))
                act.activation(ev[m % 2][:], ps[m % 2][:].rearrange("p a b -> p (a b)"), ACT.Identity,
                               scale=mod[:, layer, 16 + m, 0:1], bias=zero[:]).then_inc(unit_out, 1)

        def gather(dve, dst, i):
            for n, bank in enumerate((ps[2][:, 1, :], ps[3][:, 0, :], ps[3][:, 1, :])):
                cnt = min(4, NCH - 4 * n)
                ins = dve.tensor_copy(dst[:, 4 * n:4 * n + cnt, i * P:(i + 1) * P],
                                      bank[:, 0:cnt * P].rearrange("p (c f) -> p c f", f=P))
            return ins

        def add_up(dve, u, ev, SD, i):
            for m in range(KB):
                dve.wait_ge(unit_out, u + m + 1 + CREDIT)
                SD.done(dve.tensor_tensor(resid[:, m, :], resid[:, m, :], ev[m % 2][:], ALU.add), f"acc{m}")

        block = stack.enter_context(nc.Block())

        @block.sync
        def _(sp):
            sp.dma_start(ident[:], tab_ident).then_inc(c_const, 16)
            sp.dma_start(mask[:], tab_mask).then_inc(c_const, 16)
            sp.wait_ge(rows_clear, 1)
            rows = lambda a: a.rearrange("(k p) -> k p", p=P)
            for t, a0, n, src in ((0, ADA_B, 48, ada_b.rearrange("l (k p) -> (l k) p", p=P)),
                                  (0, NORM_G, 16, norm_g.rearrange("l (k p) -> (l k) p", p=P)),
                                  (0, FINAL_G, 8, rows(final_g)), (0, HEAD_G, 8, rows(head_norm[0])),
                                  (0, POOL_S, 16, rows(pool_scale[0])),
                                  (0, C_VEC, 8, rows(c[0])), (0, C_VEC + 8, 8, rows(c_ctx)),
                                  (1, 0, 48, conv_qk[0].rearrange("j (k p) -> (j k) p", p=P))):
                sp.dma_start(vrow[a0:a0 + n, t, :], src).then_inc(c_vec, 16)
            with sp.Fori(0, NT // 2) as i:
                for j in range(2):
                    sp.wait_ge(pe_step, st_tok["pe"].at(f"t{j}", i - 1))
                    sp.dma_start(tok[j][:], x[0, bass.ds((2 * i + j) * P, P), :]).then_inc(c_tok[j], 16)
            for j in range(2):
                sp.wait_ge(pe_step, st_tok["pe"].at(f"t{j}", NT // 2 - 1))
                sp.dma_start(tok[j][:], ctx_in[0, j * P:(j + 1) * P, :]).then_inc(c_tok[j], 16)
            for lay in range(2):
                with sp.Fori(0, 6) as i:
                    sp.wait_ge(pe_step, st_ada["pe"].at("mm", i + 6 * lay - 1))
                    sp.dma_start(ada_buf[:], ada_v[:, lay, :, bass.ds(i, 1), :].rearrange("p k b m -> p k (b m)")
                                 ).then_inc(c_ada, 16)
            sp.wait_ge(dve_step, st_n0[2]["dve"].end)
            sp.dma_start(g_in[:], we[:, :, 7 * D:7 * D + 16]).then_inc(c_gate, 16)
            sp.wait_ge(bias_clear, 1)
            for kind in range(2):
                for d in range(2):
                    row = 2 * d + kind
                    sp.dma_start(g_bias[32 * d:32 * d + 4, kind:kind + 1],
                                 gate_b[0, 4 * row:4 * row + 4].rearrange("(r o) -> r o", o=1)).then_inc(c_gate, 16)

            def load(b, j, src, k):
                sp.wait_ge(w_ready, b - 1 + CREDIT)
                sp.dma_start(w_raw[j % 2][:].rearrange("p (k m) -> p k m", k=k), src).then_inc(w_landed[j % 2], 16)

            with sp.Fori(0, HEADS) as h:
                b = h * len(HEAD_UNITS)
                for n, part in enumerate((0, 2, 1, 3, 4)):
                    for i in range(2):
                        load(b + 2 * n + i, i, we[:, :, bass.ds(h * DH + part * D + i * P, P)], KB)
                for i in range(2):
                    load(b + 10 + i, i, woe[:, bass.ds(2 * h, 2), i * 512:(i + 1) * 512], 2)
            with sp.Fori(0, GROUPS) as g:
                b = g * len(FOUR_UNITS) + B_FOUR
                for n, part in enumerate((5, 6)):
                    for i in range(2):
                        load(b + 2 * n + i, i, we[:, :, bass.ds(g * DH + part * D + i * P, P)], KB)
                for i in range(2):
                    load(b + 4 + i, i, woe[:, bass.ds(2 * g + 8, 2), i * 512:(i + 1) * 512], 2)
            with sp.Fori(0, GROUPS) as g:
                b = g * len(POOL_UNITS) + B_POOL
                for i in range(4):
                    load(b + i, i, wo[:, :, bass.ds(g * 512 + i * P, P)], KB)
                for i in range(2):
                    load(b + 4 + i, i, pw[:, bass.ds(4 * g, 4), i * 256:(i + 1) * 256], 4)
                for i in range(4):
                    load(b + 6 + i, i, wo[:, :, bass.ds(g * 512 + 2 * D + i * P, P)], KB)
                for i in range(4):
                    load(b + 10 + i, i, woo[:, bass.ds(4 * g, 4), i * 256:(i + 1) * 256], 4)
            for i in range(NT // 2):
                for j in range(2):
                    sp.wait_ge(act_step, st_end["act"].at(f"c{j}", i))
                    sp.dma_start(out[0, (2 * i + j) * P:(2 * i + j + 1) * P, :], o_tok[j][:]).then_inc(c_out[j], 16)
            for j in range(2):
                sp.wait_ge(c_out[j], 16 * (NT // 2))

        @block.gpsimd
        def _(pool):
            pool.memset(ones[:], 1.0).then_inc(act_step, STEP_CREDIT)
            pool.memset(eps[:], EPS).then_inc(dve_step, STEP_CREDIT)
            pool.memset(zero[:], 0.0).then_inc(unit_done, CREDIT)
            for n, (counter, start) in enumerate(((w_ready, CREDIT), (unit_out, CREDIT), (pe_step, STEP_CREDIT),
                                                  (ctx_out, 1))):
                pool.memset(seed[:, n:n + 1], 0.0).then_inc(counter, start)
            pool.drain()

            def split(base, i, units, loops_before):
                ubase, bbase = base
                per, nb = sum(units), len(units)
                for j in range(nb):
                    before = sum(units[:j - 1]) if j >= 1 else -units[-1]
                    s = j % 2
                    pool.wait_ge(w_landed[s], 16 * (i * (nb // 2) + (bbase + j) // 2 + 1))
                    pool.wait_ge(unit_done, i * per + ubase + before + CREDIT)
                    pool.tensor_tensor(w_hi[s][:], w_raw[s][:], zero[:].to_broadcast([P, D]), ALU.add
                                       ).then_inc(w_high, 1)
                    pool.wait_ge(w_high, i * nb + bbase + j + 1)
                    pool.tensor_tensor(w_lo[s][:], w_raw[s][:], w_hi[s][:].bitcast(F32), ALU.subtract
                                       ).then_inc(w_ready, 1)

            with pool.Fori(0, HEADS) as i:
                split((0, 0), i, HEAD_UNITS, 0)
            with pool.Fori(0, GROUPS) as i:
                split((U_FOUR, B_FOUR), i, FOUR_UNITS, 0)
            with pool.Fori(0, GROUPS) as i:
                split((U_POOL, B_POOL), i, POOL_UNITS, 0)

        @block.tensor
        def _(pe):
            def three(dst, ah, al, bh, bl, start, stop):
                pe.matmul(dst, ah, bh, start=start, stop=False)
                pe.matmul(dst, ah, bl, start=False, stop=False)
                return pe.matmul(dst, al, bh, start=False, stop=stop)

            pe.wait_ge(c_const, 32)
            pe.wait_ge(c_vec, 8 * 16)
            pe.transpose(ps[0][:, 0, 0:P], vrow[:, 0, :], ident[:])
            st_vec["pe"].done(pe.transpose(ps[0][:, 0, P:2 * P], vrow[:, 1, :], ident[:]), "vecT")

            def token_tile(st, i, j, landed):
                pe.wait_ge(c_tok[j], landed)
                pe.wait_ge(act_step, st["act"].at(f"c{j}", i - 1) if st is st_tok
                           else st_tok["act"].at(f"c{j}", NT // 2 - 1))
                for k in range(KB):
                    m = pe.transpose(ps[2 + j][:, k // 4, (k % 4) * P:(k % 4 + 1) * P],
                                     tok[j][:, k * P:(k + 1) * P], ident[:])
                st["pe"].done(m, f"t{j}")

            with pe.Fori(0, NT // 2) as i:
                for j in range(2):
                    token_tile(st_tok, i, j, 16 * i + 16)
            for j in range(2):
                token_tile(st_tokc, 0, j, 16 * (NT // 2) + 16)

            pe.wait_ge(act_step, st_vec["act"].at("silu_c"))
            with pe.Fori(0, 12) as i:
                pe.wait_ge(c_ada, 16 * i + 16)
                pe.wait_ge(act_step, st_ada["act"].at("row", i - 1))
                for k in range(KB):
                    m = pe.matmul(ps[0][0:2, 0, :], c_silu[:, k, :], ada_buf[:, k, :], start=(k == 0), stop=(k == KB - 1))
                st_ada["pe"].done(m, "mm")
                pe.wait_ge(act_step, st_ada["act"].at("row", i))
                pe.wait_ge(dve_step, st_ada["dve"].at("col", i - 1))
                for n in range(4):
                    m = pe.matmul(ps[1][:, 0, 2 * n:2 * n + 2], mrow[0][:, n * P:(n + 1) * P], ident[0:2, 0:2],
                                  start=True, stop=True)
                st_ada["pe"].done(m, "tr")

            def norm(st, bank, n, sq):
                for k in range(KB):
                    pe.wait_ge(act_step, st["act"].at(f"sq{k}"))
                    st["pe"].done(pe.matmul(bank[:, 0, 0:n], ones[:], sq[k % 2][:, 0:n],
                                            start=(k == 0), stop=(k == KB - 1)), f"s{k}")

            for s, st in enumerate(st_n0):
                norm(st, ps[2], TC if s == 2 else HALF, n_sq)

            pe.wait_ge(dve_step, st_gate["dve"].at("w_lo"))
            for kind, bank in ((0, ps[0]), (1, ps[1])):
                for half in range(2):
                    for k in range(KB):
                        s = slice(half * HALF, (half + 1) * HALF)
                        three(bank[:, half, :], g_wh[:, k, kind, :], g_wl[:, k, kind, :], h_hi[:, k, s], h_lo[:, k, s],
                              k == 0, k == KB - 1)
                for k in range(KB):
                    m = three(ps[3][:, kind, 0:TC], g_wh[:, k, kind, :], g_wl[:, k, kind, :], hc_hi[:, k, :],
                              hc_lo[:, k, :], k == 0, k == KB - 1)
            st_gate["pe"].done(m, "gates")
            for n, (name, src, want) in enumerate((("colsA", g_nat, "a_nat"), ("colsW", g_s, "w_nat"),
                                                   ("colsE", g_e, "e_nat"))):
                pe.wait_ge(dve_step, st_gate["dve"].at(want))
                for ch in range(NCH):
                    bank = (ps[0], ps[1], ps[3])[n]
                    m = pe.transpose(bank[:, ch // 8, (ch % 8) * 64:(ch % 8) * 64 + 64],
                                     src[:, ch * CHUNK:(ch + 1) * CHUNK], ident[0:64, 0:64])
                st_gate["pe"].done(m, name)

            def begin(b, u):
                pe.wait_ge(w_ready, b + 1 + CREDIT)

            def unit(s, u, lhs, rhs, ks, more=None):
                pe.wait_ge(unit_out, u - 1 + CREDIT)
                bank = ps[s]
                for half in range(2):
                    for k in ks:
                        m = three(bank[:, half, :], *lhs(k), rhs[0][:, k, half * HALF:(half + 1) * HALF],
                                  rhs[1][:, k, half * HALF:(half + 1) * HALF], k == ks[0], k == ks[-1])
                m.then_inc(unit_done, 1)

            def wide(s, m0, width):
                return lambda k: (w_hi[s][:, k * width + m0:k * width + m0 + P],
                                  w_lo[s][:, k * width + m0:k * width + m0 + P])

            pe.wait_ge(dve_step, st_gate["dve"].end)
            with pe.Fori(0, HEADS) as h:
                b, u = h * len(HEAD_UNITS), h * HU
                SA, SD, SP_ = st_head["act"], st_head["dve"], st_head["pe"]

                def project(n, context=None):
                    begin(b + n, u + n)
                    if context is not None:
                        pe.wait_ge(ctx_out, h * 4 + context + 1)
                        for k in range(KB):
                            three(ps[2][:, 0, 0:TC], *wide(n % 2, 0, P)(k), hc_hi[:, k, :], hc_lo[:, k, :],
                                  k == 0, k == KB - 1)
                    unit(n % 2, u + n, wide(n % 2, 0, P), (h_hi, h_lo), range(KB))

                pe.wait_ge(dve_step, SD.at("hrs", h - 1))
                project(0)
                project(1)
                project(2, 0)
                project(3, 1)
                project(4, 2)

                def turn(src, i, name):
                    for ch in range(NCH):
                        col = ch * P
                        bank = (ps[2][:, 1, :], ps[3][:, 0, :], ps[3][:, 1, :])[col // HALF]
                        m = pe.transpose(bank[:, col % HALF:col % HALF + P], src[:, i, ch * P:(ch + 1) * P], ident[:])
                    SP_.done(m, name)

                pe.wait_ge(ctx_out, h * 4 + 3)
                pe.wait_ge(unit_out, u + 4 + CREDIT)
                turn(k_t, 0, "vT0")
                project(5, 3)
                pe.wait_ge(dve_step, SD.at("vtok0", h))
                turn(k_t, 1, "vT1")
                pe.wait_ge(act_step, SA.at("silu_k1", h))
                pe.wait_ge(dve_step, SD.at("vtok1", h))
                turn(k_t, 0, "kT0")
                pe.wait_ge(dve_step, SD.at("ktok0", h))
                turn(k_t, 1, "kT1")
                pe.wait_ge(dve_step, SD.at("ktok1", h))
                for j in range(NCH):
                    for d in DIRS:
                        n = nat_chunk(d, j)
                        t = (n - NCC) * CHUNK
                        if j >= NCC:
                            s_b, n_b = ps[0][:, d, 0:CHUNK], ps[1][:, d, 0:DH + 1]
                            if j > NCC:
                                pe.wait_ge(dve_step, SD.at(f"P{j - 1}{d}", h))
                            else:
                                pe.wait_ge(unit_out, u + 6 + CREDIT)
                            for i in range(2):
                                m = pe.matmul(s_b, k_t[:, i, n * CHUNK:(n + 1) * CHUNK], q_t[:, i, t:t + CHUNK],
                                              start=(i == 0), stop=(i == 1))
                            SP_.done(m, f"S{j}{d}")
                            pe.wait_ge(dve_step, SD.at(f"Q{j}{d}", h))
                            if j > NCC:
                                pe.wait_ge(dve_step, SD.at(f"h{j - 1}{d}", h))
                            pe.matmul(n_b, pr[d][:], v_tok[:, n, :], start=True, stop=False)
                            pe.matmul(n_b, qi[d][:, 0, :], cst[:, d, 0, :], start=False, stop=False)
                            SP_.done(pe.matmul(n_b, qi[d][:, 1, :], cst[:, d, 1, :], start=False, stop=True),
                                     f"N{j}{d}")
                        if j < NCH - 1:
                            pe.wait_ge(dve_step, SD.at(f"kw{j}{d}", h))
                            if j > 0:
                                pe.wait_ge(dve_step, SD.at(f"C{j - 1}{d}", h))
                            for i in range(2):
                                m = pe.matmul(ps[2 + d][:, i, 0:DH + 1], kw[d][:, i * P:(i + 1) * P], v_tok[:, n, :],
                                              start=True, stop=True)
                            SP_.done(m, f"U{j}{d}")
                for i in range(2):
                    pe.wait_ge(dve_step, SD.at(f"h{NCH - 1}1", h))
                    for n in range(NCX):
                        m = pe.transpose(ps[2 + i][:, n // 4, (n % 4) * P:(n % 4 + 1) * P],
                                         h_tok[:, n, i * P:(i + 1) * P], ident[:])
                    SP_.done(m, f"hT{i}")
                project(6)
                project(7)
                for half in range(2):
                    for i in range(2):
                        pe.wait_ge(act_step, SA.at(f"sq{i}", h))
                        if half == 0 and i == 0:
                            pe.wait_ge(dve_step, SD.at("hf1", h))
                        m = pe.matmul(ps[2][:, half, :], ones[:], k_t[:, i, half * HALF:(half + 1) * HALF],
                                      start=(i == 0), stop=(i == 1))
                SP_.done(m, "hsum")
                project(8)
                project(9)
                for n in range(2):
                    begin(b + 10 + n, 0)
                    if n == 0:
                        pe.wait_ge(dve_step, SD.at("yl1", h))
                    for m4 in range(4):
                        unit(m4 % 2, u + 10 + 4 * n + m4, wide(n, m4 * P, 512), (yh2, yl2), range(2))

            with pe.Fori(0, GROUPS) as g:
                b, u = g * len(FOUR_UNITS) + B_FOUR, g * FU + U_FOUR
                SA, SD, SP_ = st_four["act"], st_four["dve"], st_four["pe"]
                pe.wait_ge(c_fw, 16 * g + 16)
                pe.wait_ge(c_four, 64)
                pe.wait_ge(dve_step, SD.at("V7", g - 1))
                pe.wait_ge(act_step, SA.at("y1", g - 1))
                for f in range(2):
                    for i in range(2):
                        for k in range(2):
                            m = pe.matmul(ps[2][:, i, f * DH:(f + 1) * DH], ccs[:, f, k, i * P:(i + 1) * P], fw[:, k, :],
                                          start=(k == 0), stop=(k == 1))
                SP_.done(m, "cf")
                for n in range(2):
                    begin(b + n, 0)
                    unit(n, u + n, wide(n, 0, P), (h_hi, h_lo), range(KB))
                pe.wait_ge(dve_step, SD.at("fold", g))
                pe.wait_ge(act_step, SA.at("cf", g))
                for n, (arr, tb) in enumerate(((0, 0), (0, 1), (2, 0), (2, 1), (3, 0), (1, 0), (3, 1), (1, 1))):
                    bank = ps[2 + (n % 4) // 2][:, n % 2, :]
                    if n >= 4:
                        pe.wait_ge(dve_step, SD.at(f"V{n - 4}", g))
                    for ch in range(2):
                        m = pe.matmul(bank, fd[:, ch, arr, tb * P:(tb + 1) * P], cfsf[:, ch, :],
                                      start=(ch == 0), stop=(ch == 1))
                    SP_.done(m, f"V{n}")
                for i in range(2):
                    pe.wait_ge(dve_step, SD.at("V7", g))
                    for rr in range(RADIX):
                        dst = ps[2 + i][:, rr // 2, (rr % 2) * TF:(rr % 2 + 1) * TF]
                        for tb in range(2):
                            for z, tab in ((0, ct), (1, ns)):
                                m = pe.matmul(dst, pq[:, tb, rr, z * DH + i * P:z * DH + (i + 1) * P],
                                              tab[:, tb, rr * TF:(rr + 1) * TF], start=(tb == 0 and z == 0),
                                              stop=(tb == 1 and z == 1))
                    SP_.done(m, f"Y{i}")
                for n in range(2):
                    begin(b + 2 + n, 0)
                    unit(n, u + 2 + n, wide(n, 0, P), (h_hi, h_lo), range(KB))
                for n in range(2):
                    begin(b + 4 + n, 0)
                    if n == 0:
                        pe.wait_ge(dve_step, SD.at("yl1", g))
                    for m4 in range(4):
                        unit(m4 % 2, u + 4 + 4 * n + m4, wide(n, m4 * P, 512), (yh_f, yl_f), range(2))

            for st in st_n1:
                norm(st, ps[2], HALF, m_sq)

            pe.wait_ge(dve_step, st_n1[1]["dve"].end)
            with pe.Fori(0, GROUPS) as g:
                b, u = g * len(POOL_UNITS) + B_POOL, g * PU + U_POOL
                SA, SD = st_pool["act"], st_pool["dve"]
                for n in range(4):
                    begin(b + n, 0)
                    unit(n % 2, u + n, wide(n % 2, 0, P), (h_hi, h_lo), range(KB))
                for n in range(2):
                    begin(b + 4 + n, 0)
                    if n == 0:
                        pe.wait_ge(dve_step, SD.at("pl3", g))
                    for m2 in range(2):
                        unit(m2, u + 4 + 2 * n + m2, wide(n, m2 * P, 256), (yh_p, yl_p), range(4))
                for n in range(4):
                    begin(b + 6 + n, 0)
                    unit(n % 2, u + 8 + n, wide(n % 2, 0, P), (h_hi, h_lo), range(KB))
                for n in range(4):
                    begin(b + 10 + n, 0)
                    if n == 0:
                        pe.wait_ge(dve_step, SD.at("yl3", g))
                    for m2 in range(2):
                        unit(m2, u + 12 + 2 * n + m2, wide(n % 2, m2 * P, 256), (yh_p, yl_p), range(4))

            for st in st_n2:
                norm(st, ps[2], HALF, m_sq)
            pe.wait_ge(dve_step, st_n2[1]["dve"].end)
            for i in range(NT // 2):
                for j in range(2):
                    pe.wait_ge(act_step, st_end["act"].at(f"c{j}", i - 1))
                    for k in range(KB):
                        m = pe.transpose(ps[2 + j][:, k // 4, (k % 4) * P:(k % 4 + 1) * P],
                                         resid[:, k, (2 * i + j) * P:(2 * i + j + 1) * P], ident[:])
                    st_end["pe"].done(m, f"t{j}")

        @block.scalar
        def _(act):
            def flat(bank):
                return bank[:].rearrange("p a b -> p (a b)")

            act.wait_ge(dve_step, st_vec["dve"].at("vec"))
            st_vec["act"].done(act.activation(c_silu[:].rearrange("p k s -> p s k"),
                                              vec[:, C_VEC:C_VEC + 16].rearrange("p (s k) -> p s k", s=2),
                                              ACT.Silu), "silu_c")
            with act.Fori(0, NT // 2) as i:
                for j in range(2):
                    act.wait_ge(pe_step, st_tok["pe"].at(f"t{j}", i))
                    st_tok["act"].done(act.copy(resid[:, :, bass.ds((2 * i + j) * P, P)],
                                                flat(ps[2 + j]).rearrange("p (k t) -> p k t", k=KB)), f"c{j}")
            for j in range(2):
                act.wait_ge(pe_step, st_tokc["pe"].at(f"t{j}"))
                st_tokc["act"].done(act.copy(xc_t[:, :, j * P:(j + 1) * P],
                                             flat(ps[2 + j]).rearrange("p (k t) -> p k t", k=KB)), f"c{j}")
            with act.Fori(0, 12) as i:
                act.wait_ge(pe_step, st_ada["pe"].at("mm", i))
                act.wait_ge(pe_step, st_ada["pe"].at("tr", i - 1))
                st_ada["act"].done(act.copy(mrow[0][:], ps[0][0:2, 0, :]), "row")

            def norm(st, bank, src, n, width, sq, t_, h_, rs, gain_col, bias_col, hi):
                s = slice(n * HALF, n * HALF + width)
                for k in range(KB):
                    if k >= 2:
                        act.wait_ge(pe_step, st["pe"].at(f"s{k - 2}"))
                    st["act"].done(act.activation(sq[k % 2][:, 0:width], src[:, k, s], ACT.Square), f"sq{k}")
                act.wait_ge(pe_step, st["pe"].at(f"s{KB - 1}"))
                st["act"].done(act.activation(rs[:, 0:width], bank[:, 0, 0:width], ACT.Sqrt, scale=1.0 / D,
                                              bias=eps[:]), "std")
                for k in range(KB):
                    act.wait_ge(dve_step, st["dve"].at(f"t{k}"))
                    if k >= 2:
                        act.wait_ge(dve_step, st["dve"].at(f"lo{k - 2}"))
                    if bias_col is None:
                        st["act"].done(act.activation(src[:, k, s], t_[k % 2][:, 0:width], ACT.Copy), f"h{k}")
                        st["act"].done(act.activation(h_[k % 2][:, 0:1], t_[k % 2][:, 0:1], ACT.Copy), f"hi{k}")
                    else:
                        st["act"].done(act.activation(h_[k % 2][:, 0:width], t_[k % 2][:, 0:width], ACT.Identity,
                                                      scale=gain_col(k), bias=bias_col(k)), f"h{k}")
                        act.wait_ge(act_step, st["act"].at(f"h{k}"))
                        st["act"].done(act.activation(hi[:, k, s], h_[k % 2][:, 0:width], ACT.Copy), f"hi{k}")

            act.wait_ge(dve_step, st_gain["dve"].at("gain"))
            act.wait_ge(act_step, st_tokc["act"].end)
            for n in range(2):
                norm(st_n0[n], ps[2], resid, n, HALF, n_sq, n_t, n_h, n_rs,
                     lambda k: gain[:, 0, k:k + 1], lambda k: mod[:, 0, k, 0:1], h_hi)
            norm(st_n0[2], ps[2], xc_t, 0, TC, n_sq, n_t, n_h, n_rs,
                 lambda k: gain[:, 1, k:k + 1], lambda k: mod[:, 0, k, 1:2], hc_hi)

            SG = st_gate
            act.wait_ge(dve_step, SG["dve"].at("f"))
            act.activation(g_e[:], g_f[:], ACT.Abs)
            act.drain()
            act.activation(g_e[:], g_e[:], ACT.Exp, scale=-1.0)
            act.drain()
            SG["act"].done(act.activation(g_e[:], g_e[:], ACT.Ln, bias=1.0), "ln")
            act.wait_ge(dve_step, SG["dve"].at("w_in"))
            SG["act"].done(act.activation(g_i[:], g_i[:], ACT.Exp), "w")
            act.wait_ge(dve_step, SG["dve"].at("e_in"))
            SG["act"].done(act.activation(g_f[:], g_f[:], ACT.Exp, scale=-1.0), "em")

            act.activation(g_small[:, 1, :], g_small[:, 1, :], ACT.Exp)
            act.drain()
            for d in range(2):
                act.dma_start(g_dram[4 * d:4 * d + 4, :], g_b[32 * d:32 * d + 4, :]).then_inc(c_rows, 16)
                act.dma_start(s_dram[4 * d:4 * d + 4, :], g_small[32 * d:32 * d + 4, 0:2, :]).then_inc(c_rows, 16)
            act.wait_ge(c_rows, 64)
            act.dma_start(chunk_sc[:].rearrange("p a b c -> p (a b c)"),
                          bcast(s_dram, 0, 16 * NCH)).then_inc(c_bc, 16)

            act.wait_ge(dve_step, SG["dve"].end)
            with act.Fori(0, HEADS) as h:
                u = h * HU
                SA, SD, SPE = st_head["act"], st_head["dve"], st_head["pe"]
                act.wait_ge(unit_done, u + CREDIT)
                act.wait_ge(dve_step, SD.at("acc7", h - 1))
                for d in range(2):
                    act.dma_start(g_bc[:, d, :], bcast(g_dram, (h + 4 * d) * (TC + T) + TC, T)).then_inc(c_gbc, 16)
                for n, name in enumerate(("q0", "q1", "v0", "v1", "k0", "k1")):
                    i = n % 2
                    act.wait_ge(unit_done, u + 1 + n + CREDIT)
                    if name[0] == "v":
                        act.copy(k_t[:, i, 0:TC], ps[2][:, 0, 0:TC]).then_inc(ctx_out, 1)
                        act.copy(k_t[:, i, TC:TC + T], flat(ps[i])).then_inc(unit_out, 1)
                        continue
                    before = {"q1": "q0", "k0": "q1", "k1": "k0"}.get(name)
                    if before:
                        act.wait_ge(dve_step, SD.at(f"conv_{before}", h))
                    if name[0] == "k":
                        act.copy(cbc[:, 1:TC + 1], ps[2][:, 0, 0:TC]).then_inc(ctx_out, 1)
                    act.copy(cb[:, 1:T + 1], flat(ps[i])).then_inc(unit_out, 1)
                    act.wait_ge(dve_step, SD.at(f"conv_{name}", h))
                    if name[0] == "q":
                        ins = act.activation(q_t[:, i, :], cv[:, TC:TC + T], ACT.Silu)
                    else:
                        act.wait_ge(pe_step, SPE.at(f"vT{i}", h))
                        ins = act.activation(k_t[:, i, :], cv[:], ACT.Silu)
                    SA.done(ins, f"silu_{name}")
                act.wait_ge(c_gbc, 32 * h + 32)
                act.wait_ge(c_bc, 16)
                for j in range(NCC, NCH):
                    for d in DIRS:
                        t = (nat_chunk(d, j) - NCC) * CHUNK
                        if j > NCC:
                            act.wait_ge(dve_step, SD.at(f"Q{j - 1}{d}", h))
                        act.wait_ge(dve_step, SD.at(f"E{j}{d}", h))
                        SA.done(act.activation(ee[d][:], ee[d][:], ACT.Exp, scale=-1.0), f"D{j}{d}")
                        SA.done(act.activation(it[d][:], g_bc[:, d, t:t + CHUNK], ACT.Exp, scale=-1.0,
                                               bias=chunk_sc[:, bass.ds(h + 4 * d, 1), 0, j:j + 1].rearrange(
                                                   "p a b -> p (a b)")), f"I{j}{d}")
                for i in range(2):
                    act.wait_ge(unit_done, u + 7 + i + CREDIT)
                    if i == 0:
                        act.wait_ge(act_step, SA.at(f"I{NCH - 1}1", h))
                    act.activation(ev_a[i][:], flat(ps[i]), ACT.Sigmoid).then_inc(unit_out, 1)
                for i in range(2):
                    act.wait_ge(dve_step, SD.at(f"o{i}", h))
                    SA.done(act.activation(k_t[:, i, 0:T], q_t[:, i, :], ACT.Square), f"sq{i}")
                act.wait_ge(pe_step, SPE.at("hsum", h))
                act.wait_ge(dve_step, SD.at("o1", h))
                SA.done(act.activation(ev_a[0][:], flat(ps[2]), ACT.Sqrt, scale=1.0 / DH, bias=eps[:]), "hstd")
                for i in range(2):
                    act.wait_ge(unit_done, u + 9 + i + CREDIT)
                    if i == 0:
                        act.wait_ge(dve_step, SD.at("hrs", h))
                    act.activation(ev_a[i][:], flat(ps[i]), ACT.Silu).then_inc(unit_out, 1)
                for i in range(2):
                    act.wait_ge(dve_step, SD.at(f"z{i}", h))
                    SA.done(act.activation(yh2[:, i, :], q_t[:, i, :], ACT.Copy), f"yh{i}")
                accumulate(act, u + 10, ev_a, 0, SD, h, "z")

            act.wait_ge(dve_step, st_head["dve"].end)
            act.dma_start(ct[:], tab_ct.rearrange("(b p) m -> p b m", p=P)).then_inc(c_four, 16)
            act.dma_start(ns[:], tab_ns.rearrange("(b p) m -> p b m", p=P)).then_inc(c_four, 16)
            act.dma_start(ccs[:, 0], tab_cc.rearrange("(b p) m -> p b m", p=P)).then_inc(c_four, 16)
            act.dma_start(ccs[:, 1], tab_cs.rearrange("(b p) m -> p b m", p=P)).then_inc(c_four, 16)
            with act.Fori(0, GROUPS) as g:
                u = g * FU + U_FOUR
                SA, SD, SPE = st_four["act"], st_four["dve"], st_four["pe"]
                act.wait_ge(pe_step, SPE.at("cf", g - 1))
                act.dma_start(fw[:], fourier_w[0, bass.ds(g, 1)].rearrange("g (k p) m -> p (g k) m", p=P)
                              ).then_inc(c_fw, 16)
                act.wait_ge(pe_step, SPE.at("cf", g))
                SA.done(act.copy(cfsf[:], ps[2][:]), "cf")
                for i in range(2):
                    act.wait_ge(unit_done, u + 1 + i + CREDIT)
                    act.copy(u_f[:, i, :], flat(ps[i])).then_inc(unit_out, 1)
                for i in range(2):
                    act.wait_ge(pe_step, SPE.at(f"Y{i}", g))
                    SA.done(act.copy(y_f[:, i, :].rearrange("p (m r) -> p r m", r=RADIX),
                                     flat(ps[2 + i]).rearrange("p (r m) -> p r m", r=RADIX)), f"y{i}")
                for i in range(2):
                    act.wait_ge(unit_done, u + 3 + i + CREDIT)
                    if i == 0:
                        act.wait_ge(dve_step, SD.at("acc7", g - 1))
                    act.activation(ev_f[i][:], flat(ps[i]), ACT.Silu).then_inc(unit_out, 1)
                for i in range(2):
                    act.wait_ge(dve_step, SD.at(f"z{i}", g))
                    SA.done(act.activation(yh_f[:, i, :], y_f[:, i, :], ACT.Copy), f"yh{i}")
                accumulate(act, u + 4, ev_f, 0, SD, g, "z")

            act.wait_ge(dve_step, st_four["dve"].end)
            for n in range(2):
                norm(st_n1[n], ps[2], resid, n, HALF, m_sq, m_t, m_h, m_rs,
                     lambda k: gain[:, 2, k:k + 1], lambda k: mod[:, 1, k, 0:1], h_hi)
            act.wait_ge(dve_step, st_n1[1]["dve"].end)

            with act.Fori(0, GROUPS) as g:
                u = g * PU + U_POOL
                SA, SD = st_pool["act"], st_pool["dve"]
                act.wait_ge(dve_step, SD.at("acc7", g - 1))
                act.dma_start(inv[:], bcast_ap(tab_inv, g)).then_inc(c_inv, 16)
                for m in range(4):
                    act.wait_ge(unit_done, u + 1 + m + CREDIT)
                    act.copy(u_p[:, m, :], flat(ps[m % 2])).then_inc(unit_out, 1)
                for m in range(4):
                    act.wait_ge(dve_step, SD.at(f"p{m}", g))
                    SA.done(act.activation(yh_p[:, m, :], u_p[:, m, :], ACT.Copy), f"ph{m}")
                for m in range(4):
                    act.wait_ge(unit_done, u + 5 + m + CREDIT)
                    if m == 0:
                        act.wait_ge(dve_step, SD.at("pl3", g))
                    act.activation(u_p[:, m, :], flat(ps[m % 2]), ACT.Identity,
                                   scale=vec[:, bass.ds(4 * g + POOL_S + m, 1)], bias=zero[:]).then_inc(unit_out, 1)
                for m in range(4):
                    act.wait_ge(unit_done, u + 9 + m + CREDIT)
                    if m >= 2:
                        act.wait_ge(dve_step, SD.at(f"z{m - 2}", g))
                    act.activation(ev_p[m % 2][:], flat(ps[m % 2]), ACT.Silu).then_inc(unit_out, 1)
                    act.wait_ge(dve_step, SD.at(f"z{m}", g))
                    SA.done(act.activation(yh_p[:, m, :], u_p[:, m, :], ACT.Copy), f"yh{m}")
                accumulate(act, u + 12, ev_p, 1, SD, g, "z")

            act.wait_ge(dve_step, st_pool["dve"].end)
            for n in range(2):
                norm(st_n2[n], ps[2], resid, n, HALF, m_sq, m_t, m_h, m_rs, None, None, None)
            for i in range(NT // 2):
                for j in range(2):
                    act.wait_ge(pe_step, st_end["pe"].at(f"t{j}", i))
                    if i:
                        act.wait_ge(c_out[j], 16 * i)
                    st_end["act"].done(act.copy(o_tok[j][:], flat(ps[2 + j])), f"c{j}")

        @block.vector
        def _(dve):
            def flat(bank):
                return bank[:].rearrange("p a b -> p (a b)")

            dve.memset(vrow[:], 0.0).then_inc(rows_clear, 1)
            dve.wait_ge(pe_step, st_vec["pe"].at("vecT"))
            st_vec["dve"].done(dve.tensor_copy(vec[:], ps[0][:, 0, 0:176]), "vec")
            with dve.Fori(0, 12) as i:
                dve.wait_ge(pe_step, st_ada["pe"].at("tr", i))
                st_ada["dve"].done(dve.tensor_copy(
                    mod[:].rearrange("p l b s -> p (l b s)")[:, bass.ds(i * 8, 8)], ps[1][:, 0, 0:8]), "col")
            dve.drain()
            bias = vec[:, ADA_B:ADA_B + 48].rearrange("p (l b) -> p l b", l=2)
            for s in range(2):
                dve.tensor_tensor(mod[:, :, :, s], mod[:, :, :, s], bias, ALU.add)
            dve.drain()
            for n, (lay, s) in enumerate(((0, 0), (0, 1), (1, 0))):
                ins = dve.scalar_tensor_tensor(gain[:, n, :], mod[:, lay, 8:16, s], 1.0,
                                               vec[:, NORM_G + 8 * lay:NORM_G + 8 * lay + 8], ALU.add, ALU.mult)
            st_gain["dve"].done(ins, "gain")

            def norm(st, src, n, width, t_, h_, rs, hi, lo, last=False):
                s = slice(n * HALF, n * HALF + width)
                dve.wait_ge(act_step, st["act"].at("std"))
                st["dve"].done(dve.reciprocal(rs[:, 0:width], rs[:, 0:width]), "rs")
                dve.wait_ge(dve_step, st["dve"].at("rs"))

                def low(k):
                    dve.wait_ge(act_step, st["act"].at(f"hi{k}"))
                    if last:
                        st["dve"].done(dve.tensor_copy(h_[k % 2][:, 1:2], h_[k % 2][:, 0:1]), f"lo{k}")
                    else:
                        st["dve"].done(dve.tensor_tensor(lo[:, k, s], h_[k % 2][:, 0:width], hi[:, k, s].bitcast(F32),
                                                         ALU.subtract), f"lo{k}")

                for k in range(KB):
                    if last:
                        if k >= 2:
                            dve.wait_ge(act_step, st["act"].at(f"hi{k - 2}"))
                        ins = dve.scalar_tensor_tensor(t_[k % 2][:, 0:width], src[:, k, s],
                                                       vec[:, FINAL_G + k:FINAL_G + k + 1], rs[:, 0:width],
                                                       ALU.mult, ALU.mult)
                    else:
                        if k >= 2:
                            dve.wait_ge(act_step, st["act"].at(f"h{k - 2}"))
                        ins = dve.tensor_tensor(t_[k % 2][:, 0:width], src[:, k, s], rs[:, 0:width], ALU.mult)
                    st["dve"].done(ins, f"t{k}")
                    if k >= 1:
                        low(k - 1)
                low(KB - 1)

            for n in range(2):
                norm(st_n0[n], resid, n, HALF, n_t, n_h, n_rs, h_hi, h_lo)
            norm(st_n0[2], xc_t, 0, TC, n_t, n_h, n_rs, hc_hi, hc_lo)

            SG = st_gate
            dve.wait_ge(dve_step, st_n0[2]["dve"].end)
            dve.memset(g_bias[:], 0.0).then_inc(bias_clear, 1)
            dve.memset(g_w[:], 0.0)
            dve.wait_ge(c_gate, 16 * 5)
            dve.drain()
            for kind in range(2):
                for d in range(2):
                    row = 2 * d + kind
                    dve.tensor_copy(g_w[:, :, kind, 32 * d:32 * d + 4], g_in[:, :, 4 * row:4 * row + 4])
            dve.drain()
            dve.tensor_copy(g_wh[:], g_w[:])
            dve.drain()
            SG["dve"].done(dve.tensor_tensor(g_wl[:], g_w[:], g_wh[:].bitcast(F32), ALU.subtract), "w_lo")
            dve.wait_ge(pe_step, SG["pe"].at("gates"))
            for kind, dst, bank in ((0, g_i, ps[0]), (1, g_f, ps[1])):
                bc = slice(kind, kind + 1)
                dve.tensor_scalar(dst[0:32, 0:TC], ps[3][0:32, kind, 0:TC], g_bias[0:32, bc], None, ALU.add)
                dve.tensor_scalar(dst[0:32, TC:TC + T], flat(bank)[0:32], g_bias[0:32, bc], None, ALU.add)
                dve.tensor_scalar(dst[32:64, 0:TC], ps[3][32:64, kind, 0:TC][:, ::-1], g_bias[32:64, bc], None, ALU.add)
                ins = dve.tensor_scalar(dst[32:64, TC:TC + T], flat(bank)[32:64][:, ::-1], g_bias[32:64, bc], None,
                                        ALU.add)
            SG["dve"].done(ins, "f")
            dve.memset(g_s[:], 1.0)
            dve.memset(g_d[:], 0.0)
            dve.memset(g_small[:], 0.0)
            dve.drain()
            dve.memset(g_s[:, ::CHUNK], 0.0)
            dve.wait_ge(act_step, SG["act"].at("ln"))
            dve.scalar_tensor_tensor(g_f[:], g_f[:], 0.0, g_e[:], ALU.min, ALU.subtract)
            dve.drain()
            dve.tensor_tensor_scan(g_b[:], g_s[:], g_f[:], 0.0, ALU.mult, ALU.add)
            dve.drain()
            dve.tensor_tensor(g_i[:], g_i[:], g_b[:], ALU.subtract)
            dve.tensor_copy(g_d[:, CHUNK::CHUNK], g_b[:, CHUNK - 1:TC + T - CHUNK:CHUNK])
            dve.drain()
            SG["dve"].done(dve.tensor_tensor_scan(g_g[:], g_d[:], g_i[:], 0.0, ALU.add, ALU.max), "G")
            dve.wait_ge(dve_step, SG["dve"].at("G"))

            def natural(dst, src):
                dve.tensor_copy(dst[0:32, :], src[0:32, :])
                dve.tensor_copy(dst[32:64, 0:TC], src[32:64, 0:TC][:, ::-1])
                return dve.tensor_copy(dst[32:64, TC:TC + T], src[32:64, TC:TC + T][:, ::-1])

            ch = lambda a: a[:].rearrange("p (c t) -> p c t", t=CHUNK)
            SG["dve"].done(natural(g_nat, g_i), "g_nat")
            dve.tensor_tensor(g_small[:, 0, 1:NCH], g_g[:, CHUNK - 1:TC + T - CHUNK:CHUNK],
                              g_b[:, CHUNK - 1:TC + T - CHUNK:CHUNK], ALU.add)
            dve.tensor_copy(g_small[:, 2, :], g_g[:, CHUNK - 1::CHUNK])
            dve.drain()
            SG["dve"].done(dve.tensor_tensor(g_small[:, 1, :], g_small[:, 0, :], g_small[:, 2, :], ALU.subtract),
                           "a_nat")
            SG["dve"].done(dve.tensor_tensor(ch(g_i), ch(g_i),
                                             g_small[:, 2, :].unsqueeze(2).to_broadcast([64, NCH, CHUNK]),
                                             ALU.subtract), "w_in")
            dve.tensor_tensor(g_f[:], g_b[:], g_g[:], ALU.add)
            dve.drain()
            dve.wait_ge(act_step, SG["act"].at("w"))
            SG["dve"].done(natural(g_s, g_i), "w_nat")
            SG["dve"].done(natural(g_b, g_g), "e_in")
            dve.wait_ge(act_step, SG["act"].at("em"))
            SG["dve"].done(natural(g_e, g_f), "e_nat")
            dve.wait_ge(c_bc, 16)
            dve.drain()
            for n, (name, bank) in enumerate((("colsA", ps[0]), ("colsW", ps[1]), ("colsE", ps[3]))):
                dve.wait_ge(pe_step, SG["pe"].at(name))
                for lo_, hi_ in ((0, 8), (8, NCH)):
                    dve.tensor_copy(
                        cols[:, n, lo_:hi_, :].rearrange("p c (d r) -> p c d r", d=2),
                        bank[:, lo_ // 8, 0:(hi_ - lo_) * 64].rearrange("p (c d r) -> p c d r", d=2, r=32)[:, :, :, 0:4])
            dve.drain()
            dve.tensor_scalar(cols[:, 1], cols[:, 1], float(DH) ** -0.5, None, ALU.mult)
            SG["dve"].done(dve.tensor_copy(dn[:, 0, 0:1], zero[:]), "cols")
            dve.drain()

            dve.wait_ge(c_const, 32)
            with dve.Fori(0, HEADS) as h:
                u = h * HU
                SA, SD, SPE = st_head["act"], st_head["dve"], st_head["pe"]
                sc = float(DH) ** -0.5
                dve.memset(cb[:, 0:T + 2:T + 1], 0.0)
                dve.memset(cbc[:, 0:TC + 2:TC + 1], 0.0)
                for n, name in enumerate(("q0", "q1", "k0", "k1")):
                    if n == 0:
                        dve.drain()
                    wcol = lambda tap: vec[:, bass.ds(2 * h + (CONV + 16 * tap + 8 * (n // 2) + n % 2), 1)]
                    dve.wait_ge(unit_out, u + (1, 2, 5, 6)[n] + CREDIT)
                    if n:
                        dve.wait_ge(act_step, SA.at(f"silu_{('q0', 'q1', 'k0')[n - 1]}", h))
                    parts = [(cb, T, slice(TC, TC + T))]
                    if n >= 2:
                        parts.append((cbc, TC, slice(0, TC)))
                    for src, w, dst in parts:
                        dve.tensor_scalar(cv[:, dst], src[:, 0:w], wcol(0), None, ALU.mult)
                    dve.drain()
                    for src, w, dst in parts:
                        dve.scalar_tensor_tensor(cv[:, dst], src[:, 1:w + 1], wcol(1), cv[:, dst], ALU.mult, ALU.add)
                    dve.drain()
                    for src, w, dst in parts:
                        ins = dve.scalar_tensor_tensor(cv[:, dst], src[:, 2:w + 2], wcol(2), cv[:, dst], ALU.mult,
                                                       ALU.add)
                    SD.done(ins, f"conv_{name}")
                    if n >= 2:
                        dve.wait_ge(pe_step, SPE.at(f"vT{n - 2}", h))
                        SD.done(gather(dve, v_tok, n - 2), f"vtok{n - 2}")
                dve.memset(v_tok[:, :, DH:DH + 1], 1.0)
                dve.memset(cst[:], 0.0)
                for i in range(2):
                    dve.wait_ge(pe_step, SPE.at(f"kT{i}", h))
                    SD.done(gather(dve, k_tok, i), f"ktok{i}")
                dve.wait_ge(c_gbc, 32 * h + 32)
                dve.wait_ge(dve_step, SD.at("ktok1", h))
                col = lambda arr, n, d: cols[:, arr, n, bass.ds(h + 4 * d, 1)]
                for j in range(NCH):
                    for d in DIRS:
                        n = nat_chunk(d, j)
                        t = (n - NCC) * CHUNK
                        if j >= NCC:
                            if j > NCC:
                                dve.wait_ge(pe_step, SPE.at(f"N{j - 1}{d}", h))
                            SD.done(dve.scalar_tensor_tensor(ee[d][:], g_bc[:, d, t:t + CHUNK], col(0, n, d),
                                                             mask[:, d, :], ALU.subtract, ALU.add), f"E{j}{d}")
                            dve.wait_ge(pe_step, SPE.at(f"S{j}{d}", h))
                            dve.wait_ge(act_step, SA.at(f"D{j}{d}", h))
                            SD.done(dve.scalar_tensor_tensor(pr[d][:], ps[0][:, d, 0:CHUNK], sc, ee[d][:], ALU.mult,
                                                             ALU.mult), f"P{j}{d}")
                            dve.wait_ge(act_step, SA.at(f"I{j}{d}", h))
                            SD.done(dve.tensor_tensor(qi[d][:], q_t[:, :, t:t + CHUNK],
                                                      it[d][:].unsqueeze(1).to_broadcast([P, 2, CHUNK]), ALU.mult),
                                    f"Q{j}{d}")
                        if j < NCH - 1:
                            if j > 0:
                                dve.wait_ge(pe_step, SPE.at(f"U{j - 1}{d}", h))
                            SD.done(dve.tensor_scalar(kw[d][:], k_tok[:, n, :], col(1, n, d), None, ALU.mult),
                                    f"kw{j}{d}")
                        if j >= NCC:
                            nb = ps[1][:, d, :]
                            dve.wait_ge(pe_step, SPE.at(f"N{j}{d}", h))
                            dve.tensor_scalar(dn[:, d, 0:1], nb[:, DH:DH + 1], -1.0, None, ALU.mult)
                            dve.drain()
                            dve.tensor_tensor(dn[:, d, 1:2], dn[:, d, 0:1], nb[:, DH:DH + 1], ALU.max)
                            dve.drain()
                            dve.tensor_tensor(dn[:, d, 2:3], dn[:, d, 1:2], col(2, n, d), ALU.max)
                            dve.drain()
                            dve.reciprocal(dn[:, d, 3:4], dn[:, d, 2:3])
                            dve.drain()
                            hs = h_tok[:, n - NCC, :]
                            if j - NCC < NCX // 2:
                                ins = dve.tensor_scalar(hs, nb[:, 0:DH], dn[:, d, 3:4], None, ALU.mult)
                            else:
                                ins = dve.scalar_tensor_tensor(hs, nb[:, 0:DH], dn[:, d, 3:4], hs, ALU.mult, ALU.add)
                            SD.done(ins, f"h{j}{d}")
                        if j < NCH - 1:
                            dve.wait_ge(pe_step, SPE.at(f"U{j}{d}", h))
                            dec = chunk_sc[:, bass.ds(h + 4 * d, 1), 1, j:j + 1].rearrange("p a b -> p (a b)")
                            for i in range(2):
                                ins = dve.scalar_tensor_tensor(cst[:, d, i, :], cst[:, d, i, :], dec,
                                                               ps[2 + d][:, i, 0:DH + 1], ALU.mult, ALU.add)
                            SD.done(ins, f"C{j}{d}")
                            dve.drain()
                for i in range(2):
                    dve.wait_ge(pe_step, SPE.at(f"hT{i}", h))
                    SD.done(dve.tensor_copy(q_t[:, i, :], flat(ps[2 + i])), f"hf{i}")
                dve.wait_ge(dve_step, SD.at("hf1", h))
                for i in range(2):
                    dve.wait_ge(unit_out, u + 7 + i + CREDIT)
                    SD.done(dve.tensor_tensor(q_t[:, i, :], q_t[:, i, :], ev_a[i][:], ALU.mult), f"o{i}")
                dve.wait_ge(act_step, SA.at("hstd", h))
                dve.reciprocal(ev_a[0][:], ev_a[0][:])
                dve.drain()
                for i in range(2):
                    ins = dve.tensor_tensor(q_t[:, i, :], q_t[:, i, :], ev_a[0][:], ALU.mult)
                SD.done(ins, "hrs")
                dve.wait_ge(dve_step, SD.at("hrs", h))
                for i in range(2):
                    dve.wait_ge(unit_out, u + 9 + i + CREDIT)
                    SD.done(dve.scalar_tensor_tensor(q_t[:, i, :], q_t[:, i, :],
                                                     vec[:, bass.ds(2 * h + HEAD_G + i, 1)], ev_a[i][:],
                                                     ALU.mult, ALU.mult), f"z{i}")
                for i in range(2):
                    dve.wait_ge(act_step, SA.at(f"yh{i}", h))
                    SD.done(dve.tensor_tensor(yl2[:, i, :], q_t[:, i, :], yh2[:, i, :].bitcast(F32), ALU.subtract),
                            f"yl{i}")
                add_up(dve, u + 10, ev_a, SD, h)

            with dve.Fori(0, GROUPS) as g:
                u = g * FU + U_FOUR
                SA, SD, SPE = st_four["act"], st_four["dve"], st_four["pe"]
                dve.wait_ge(unit_out, u + 2 + CREDIT)
                uq = lambda q: u_f[:].rearrange("p c (q t) -> p c q t", q=RADIX)[:, :, q, :]
                dve.tensor_tensor(f_tmp[:, :, 0, :], uq(0), uq(2), ALU.add)
                dve.tensor_tensor(f_tmp[:, :, 1, :], uq(1), uq(3), ALU.add)
                dve.tensor_tensor(fd[:, :, 1, :], uq(0), uq(2), ALU.subtract)
                dve.tensor_tensor(fd[:, :, 3, :], uq(1), uq(3), ALU.subtract)
                dve.drain()
                dve.tensor_tensor(fd[:, :, 0, :], f_tmp[:, :, 0, :], f_tmp[:, :, 1, :], ALU.add)
                SD.done(dve.tensor_tensor(fd[:, :, 2, :], f_tmp[:, :, 0, :], f_tmp[:, :, 1, :], ALU.subtract), "fold")
                lo_, hi_ = slice(0, DH), slice(DH, 2 * DH)
                for n, (arr, tb) in enumerate(((0, 0), (0, 1), (2, 0), (2, 1), (3, 0), (1, 0), (3, 1), (1, 1))):
                    bank = ps[2 + (n % 4) // 2][:, n % 2, :]
                    if n > 4:
                        dve.drain()
                    dve.wait_ge(pe_step, SPE.at(f"V{n}", g))
                    if arr in (0, 2):
                        ins = dve.tensor_copy(pq[:, tb, arr, :], bank)
                    elif arr == 3:
                        ins = dve.tensor_copy(f_b[:], bank)
                    else:
                        dve.tensor_tensor(pq[:, tb, 1, lo_], bank[:, lo_], f_b[:, hi_], ALU.subtract)
                        dve.tensor_tensor(pq[:, tb, 1, hi_], bank[:, hi_], f_b[:, lo_], ALU.add)
                        dve.tensor_tensor(pq[:, tb, 3, lo_], bank[:, lo_], f_b[:, hi_], ALU.add)
                        ins = dve.tensor_tensor(pq[:, tb, 3, hi_], bank[:, hi_], f_b[:, lo_], ALU.subtract)
                    SD.done(ins, f"V{n}")
                for i in range(2):
                    dve.wait_ge(unit_out, u + 4 + i - 1 + CREDIT)
                    dve.wait_ge(act_step, SA.at(f"y{i}", g))
                    SD.done(dve.tensor_tensor(y_f[:, i, :], y_f[:, i, :], ev_f[i][:], ALU.mult), f"z{i}")
                for i in range(2):
                    dve.wait_ge(act_step, SA.at(f"yh{i}", g))
                    SD.done(dve.tensor_tensor(yl_f[:, i, :], y_f[:, i, :], yh_f[:, i, :].bitcast(F32), ALU.subtract),
                            f"yl{i}")
                add_up(dve, u + 4, ev_f, SD, g)

            dve.drain()
            for n in range(2):
                norm(st_n1[n], resid, n, HALF, m_t, m_h, m_rs, h_hi, h_lo)
            dve.drain()

            for g, win in enumerate(WINDOWS):
                u = g * PU + U_POOL
                SA, SD = st_pool["act"], st_pool["dve"]
                half = win // 2
                for m in range(4):
                    dve.wait_ge(unit_out, u + 1 + m + CREDIT)
                    if m == 0:
                        dve.wait_ge(c_inv, 16 * g + 16)
                    rows_n = GRID_H + win - 1
                    a, bbuf = pt[0], pt[1]
                    rv = lambda t_: t_[:, 0:rows_n * GRID_W]
                    dve.memset(a[:, 0:half * GRID_W], 0.0)
                    if win - 1 - half:
                        dve.memset(a[:, (half + GRID_H) * GRID_W:rows_n * GRID_W], 0.0)
                    dve.tensor_copy(a[:, half * GRID_W:half * GRID_W + T], u_p[:, m, :])
                    dve.drain()
                    step, left = 1, rows_n
                    while step < win:
                        left -= step
                        dve.tensor_tensor(bbuf[:, 0:left * GRID_W], a[:, 0:left * GRID_W],
                                          a[:, step * GRID_W:(step + left) * GRID_W], ALU.add)
                        dve.drain()
                        a, bbuf = bbuf, a
                        step *= 2
                    assert left == GRID_H
                    cw = GRID_W + win - 1
                    bv = bbuf[:, 0:GRID_H * cw].rearrange("p (r c) -> p r c", c=cw)
                    dve.memset(bv[:, :, 0:half], 0.0)
                    if win - 1 - half:
                        dve.memset(bv[:, :, half + GRID_W:cw], 0.0)
                    dve.tensor_copy(bv[:, :, half:half + GRID_W],
                                    a[:, 0:T].rearrange("p (r c) -> p r c", c=GRID_W))
                    dve.drain()
                    a, bbuf = bbuf, a
                    step, left = 1, cw
                    while step < win:
                        left -= step
                        av = a[:, 0:GRID_H * cw].rearrange("p (r c) -> p r c", c=cw)
                        ov = bbuf[:, 0:GRID_H * cw].rearrange("p (r c) -> p r c", c=cw)
                        dve.tensor_tensor(ov[:, :, 0:left], av[:, :, 0:left], av[:, :, step:step + left], ALU.add)
                        dve.drain()
                        a, bbuf = bbuf, a
                        step *= 2
                    av = a[:, 0:GRID_H * cw].rearrange("p (r c) -> p r c", c=cw)[:, :, 0:GRID_W]
                    dve.tensor_tensor(bbuf[:, 0:T].rearrange("p (r c) -> p r c", c=GRID_W), av,
                                      inv[:].rearrange("p (r c) -> p r c", c=GRID_W), ALU.mult)
                    dve.drain()
                    SD.done(dve.tensor_tensor(u_p[:, m, :], bbuf[:, 0:T], u_p[:, m, :], ALU.subtract), f"p{m}")
                    dve.drain()
                for m in range(4):
                    dve.wait_ge(act_step, SA.at(f"ph{m}", g))
                    SD.done(dve.tensor_tensor(yl_p[:, m, :], u_p[:, m, :], yh_p[:, m, :].bitcast(F32), ALU.subtract),
                            f"pl{m}")
                for m in range(4):
                    dve.wait_ge(unit_out, u + 9 + m + CREDIT)
                    SD.done(dve.tensor_tensor(u_p[:, m, :], u_p[:, m, :], ev_p[m % 2][:], ALU.mult), f"z{m}")
                for m in range(4):
                    dve.wait_ge(act_step, SA.at(f"yh{m}", g))
                    SD.done(dve.tensor_tensor(yl_p[:, m, :], u_p[:, m, :], yh_p[:, m, :].bitcast(F32), ALU.subtract),
                            f"yl{m}")
                add_up(dve, u + 12, ev_p, SD, g)

            dve.drain()
            for n in range(2):
                norm(st_n2[n], resid, n, HALF, m_t, m_h, m_rs, None, None, last=True)


def tables():
    t = np.arange(TF)[:, None].astype(np.float64)
    k = (RADIX * np.arange(TF)[None, :] + np.arange(RADIX)[:, None]).reshape(1, T)
    ang = 2 * np.pi * ((t * k) % T) / T
    norm = 1.0 / np.sqrt(T * DH)
    cidx = np.arange(DH)
    cang = 2 * np.pi * (np.outer(cidx, cidx) % DH) / DH
    s, q = np.arange(CHUNK)[:, None], np.arange(CHUNK)[None, :]
    mask = np.stack([np.where(s <= q, 0.0, BIG), np.where(s >= q, 0.0, BIG)], axis=1)
    inv = []
    for w in WINDOWS:
        def count(n):
            i = np.arange(n)
            return np.clip(i + w - w // 2, 0, n) - np.clip(i - w // 2, 0, n)
        inv.append(1.0 / np.outer(count(GRID_H), count(GRID_W)).reshape(-1))
    f = lambda a: np.ascontiguousarray(a, dtype=np.float32)
    return {"ident": f(np.eye(P)), "mask": f(mask), "ct": f(np.cos(ang) * norm), "ns": f(-np.sin(ang) * norm),
            "cc": f(np.cos(cang)), "cs": f(np.sin(cang)), "inv": f(np.stack(inv))}


_INS = ['x', 'c', 'ctx', 'c_ctx', 'ada_w', 'ada_b', 'norm_g', 'win_even', 'gate_b_even', 'conv_qk_even',
        'head_norm_even', 'fourier_w_even', 'wout_even', 'win_odd', 'pool_w_odd', 'pool_scale_odd', 'wout_odd',
        'final_g']
_OUT = ((1, 1024, 1024), 'float32')


def kernel(**inputs):
    import numpy as _np
    import concourse.bacc as _bacc
    from concourse import mybir as _mybir
    from concourse.bass_utils import run_bass_kernel_spmd as _run

    nc = _bacc.Bacc("TRN2", target_bir_lowering=False, num_devices=1)
    arrays, args = {}, []
    for name, a in [(n, inputs[n]) for n in _INS] + list(tables().items()):
        a = _np.ascontiguousarray(a)
        arrays[f"in_{name}_dram"] = a
        args.append(nc.dram_tensor(f"in_{name}_dram", a.shape, _mybir.dt.from_np(a.dtype), kind="ExternalInput").ap())
    args.append(nc.dram_tensor("out_0_dram", _OUT[0], _mybir.dt.from_np(_np.dtype(_OUT[1])),
                               kind="ExternalOutput").ap())
    program(nc, *args)
    r = _run(nc, [arrays], core_ids=[0])
    return r.results[0]["out_0_dram"]
```

```python
from contextlib import ExitStack

import numpy as np

import concourse.bass as bass
from concourse import mybir

F32 = mybir.dt.float32
F32R = mybir.dt.float32r
ALU = mybir.AluOpType
ACT = mybir.ActivationFunctionType

P = 128
D = 1024
KB = D // P
T = 1024
TC = 256
HALF = 512
HEADS = 4
DH = 256
GROUPS = 4
GRID_W = 64
GRID_H = T // GRID_W
WINDOWS = (2, 4, 8, 16)
EPS = 1e-6
CHUNK = 128
NCC, NCX = TC // CHUNK, T // CHUNK
NCH = NCC + NCX
BIG = 1e30
RADIX = 4
TF = T // RADIX

HEAD_UNITS = [1] * 10 + [4, 4]
FOUR_UNITS = [1] * 4 + [4, 4]
POOL_UNITS = [1] * 8 + [2, 2] + [2] * 4
ADA_CREDIT = 2
CREDIT = 8
STEP_CREDIT = 96


class Steps:

    def __init__(self, sem, base, names, times=1):
        self.sem, self.base, self.names, self.times = sem, base, list(names), times
        self.index = {n: i for i, n in enumerate(self.names)}
        assert len(self.index) == len(self.names)
        self.next = 0

    def at(self, name, i=0):
        return self.base + i * len(self.names) + self.index[name] + 1

    @property
    def end(self):
        return self.base + self.times * len(self.names)

    def done(self, ins, name):
        assert self.names[self.next % len(self.names)] == name, (name, self.names[self.next % len(self.names)])
        self.next += 1
        ins.then_inc(self.sem, 1)


def nat_chunk(direction, j):
    if direction == 0:
        return j
    return NCC - 1 - j if j < NCC else NCC + NCX - 1 - (j - NCC)


def program(nc, x, c, ctx_in, c_ctx, ada_w, ada_b, norm_g, win_even, gate_b, conv_qk, head_norm, fourier_w,
            wout_even, win_odd, pool_w, pool_scale, wout_odd, final_g, tab_ident, tab_mask, tab_ct, tab_ns,
            tab_cc, tab_cs, tab_inv, out):
    stack = ExitStack()
    with stack:
        def sem(name):
            return stack.enter_context(nc.semaphore(name))

        cursor = [-(-nc.sbuf_base // 64) * 64]

        def at(name, shape, dt, offset):
            return nc.alloc_sbuf_tensor_at(name, shape, dt, offset=offset)

        def size(shape):
            return -(-int(np.prod(shape[1:])) * 4 // 32) * 32

        def fixed(name, shape, dt=F32):
            t = at(name, shape, dt, cursor[0])
            cursor[0] += size(shape)
            return t

        class Region:
            def __init__(self, start):
                self.at = start

            def __call__(self, name, shape, dt=F32):
                t = at(name, shape, dt, self.at)
                self.at += size(shape)
                assert self.at <= nc.sbuf_usable_end, (name, self.at)
                return t

        ident = fixed("ident", [P, P])
        ones = fixed("ones", [P, P])
        mask = fixed("mask", [P, 2, CHUNK])
        zero = fixed("zero", [P, 1])
        eps = fixed("eps", [P, 1])
        seed = fixed("seed", [P, 5])
        vec = fixed("vec", [P, 176])
        mod = fixed("mod", [P, 2, 24, 2])
        gain = fixed("gain", [P, 3, KB])
        chunk_sc = fixed("chunk_sc", [P, 8, 2, NCH])
        w_raw = [fixed(f"w_raw{i}", [P, D]) for i in range(2)]
        w_hi = [fixed(f"w_hi{i}", [P, D], F32R) for i in range(2)]
        w_lo = [fixed(f"w_lo{i}", [P, D], F32R) for i in range(2)]
        h_hi = fixed("h_hi", [P, KB, T], F32R)
        h_lo = fixed("h_lo", [P, KB, T], F32R)
        resid = fixed("resid", [P, KB, T])
        arena = cursor[0]

        ADA_B, NORM_G, FINAL_G, HEAD_G, POOL_S, C_VEC, CONV = 0, 48, 64, 72, 80, 96, P

        r = Region(arena)
        hc_hi = r("hc_hi", [P, KB, TC], F32R)
        hc_lo = r("hc_lo", [P, KB, TC], F32R)
        cols = r("cols", [P, 3, NCH, 8])
        after_ctx = r.at
        tok = [r(f"tok{i}", [P, D]) for i in range(2)]
        xc_t = r("xc_t", [P, KB, TC])
        n_sq = [r(f"n_sq{i}", [P, HALF]) for i in range(2)]
        n_t = [r(f"n_t{i}", [P, HALF]) for i in range(3)]
        n_rs = r("n_rs", [P, HALF])
        ada_buf = [r(f"ada_buf{i}", [P, KB, HALF]) for i in range(2)]
        vrow = r("vrow", [P, 2, P])
        c_silu = r("c_silu", [P, KB, 2])
        r = Region(after_ctx)
        g_w = r("g_w", [P, KB, 2, P])
        g_wh = r("g_wh", [P, KB, 2, P], F32R)
        g_wl = r("g_wl", [P, KB, 2, P], F32R)
        g_in = r("g_in", [P, KB, 16])
        g_i = r("g_i", [64, TC + T])
        g_f = r("g_f", [64, TC + T])
        g_e = r("g_e", [64, TC + T])
        g_b = r("g_b", [64, TC + T])
        g_small = r("g_small", [64, 3, NCH])
        g_bias = r("g_bias", [64, 2])
        r = Region(after_ctx)
        g_g = r("g_g", [64, TC + T])
        g_d = r("g_d", [64, TC + T])
        g_nat = r("g_nat", [64, TC + T])
        g_s = r("g_s", [64, TC + T])
        assert r.at <= after_ctx + 3 * size([P, KB, 2, P])
        r = Region(after_ctx)
        q_t = r("q_t", [P, 2, T])
        kk = r.at
        k_t = r("k_t", [P, 2, TC + T])
        k_tok = r("k_tok", [P, NCH, DH])
        v_tok = r("v_tok", [P, NCH, DH + 1])
        cst = r("cst", [P, 2, 2, DH + 1])
        gg = r.at
        g_bc = r("g_bc", [P, 2, T])
        hh = r.at
        h_tok = r("h_tok", [P, NCX, DH])
        kw = [r(f"kw{d}", [P, DH]) for d in range(2)]
        qi = [r(f"qi{d}", [P, 2, CHUNK]) for d in range(2)]
        pr = [r(f"pr{d}", [P, CHUNK]) for d in range(2)]
        ee = [r(f"ee{d}", [P, CHUNK]) for d in range(2)]
        it = [r(f"it{d}", [P, CHUNK]) for d in range(2)]
        dn = r("dn", [P, 2, 4])
        r = Region(kk)
        yh2 = r("yh2", [P, 2, T], F32R)
        yl2 = r("yl2", [P, 2, T], F32R)
        r = Region(gg)
        ev_a = [r(f"ev_a{i}", [P, T]) for i in range(2)]
        r = Region(hh)
        cb = r("cb", [P, T + 2])
        cbc = r("cbc", [P, TC + 2])
        cv = r("cv", [P, TC + T])
        r = Region(arena)
        pq = r("pq", [P, 2, RADIX, 2 * DH])
        fd = r("fd", [P, 2, RADIX, TF])
        f_tmp = r("f_tmp", [P, 2, 2, TF])
        f_b = r("f_b", [P, 2 * DH])
        ct = r("ct", [P, 2, T])
        ns = r("ns", [P, 2, T])
        cfsf = r("cfsf", [P, 2, 2 * DH])
        ccs = r("ccs", [P, 2, 2, DH])
        fw = r("fw", [P, 2, DH])
        ev_f = [r(f"ev_f{i}", [P, T]) for i in range(2)]
        yh_f = r("yh_f", [P, 2, T], F32R)
        yl_f = r("yl_f", [P, 2, T], F32R)
        r = Region(arena)
        u_f = r("u_f", [P, 2, T])
        r = Region(arena + size([P, 2, RADIX, 2 * DH]))
        y_f = r("y_f", [P, 2, T])
        r = Region(arena)
        u_p = r("u_p", [P, 4, T])
        yh_p = r("yh_p", [P, 4, T], F32R)
        yl_p = r("yl_p", [P, 4, T], F32R)
        pt = [r(f"pt{i}", [P, (GRID_H + max(WINDOWS) - 1) * GRID_W]) for i in range(2)]
        inv = r("inv", [P, T])
        ev_p = [r(f"ev_p{i}", [P, T]) for i in range(4)]
        yh_g = at("yh_g", [P, 4, T], F32R, arena + 3 * size([P, 4, T]))
        yl_g = at("yl_g", [P, 4, T], F32R, arena)
        r = Region(arena)
        m_sq = [r(f"m_sq{i}", [P, HALF]) for i in range(2)]
        m_t = [r(f"m_t{i}", [P, HALF]) for i in range(3)]
        m_rs = r("m_rs", [P, HALF])
        o_tok = [r(f"o_tok{i}", [P, D]) for i in range(2)]

        ps = [stack.enter_context(nc.psum_tensor(f"ps{i}", [P, 2, HALF], F32)) for i in range(4)]

        g_dram = nc.dram_tensor("g_scratch", [8, TC + T], F32)
        s_dram = nc.dram_tensor("s_scratch", [8, 2 * NCH], F32)

        w_landed = [sem("w_landed0"), sem("w_landed1")]
        w_high = sem("w_high")
        w_ready = sem("w_ready")
        unit_done = sem("unit_done")
        unit_out = sem("unit_out")
        ctx_out = sem("ctx_out")
        pe_step, act_step, dve_step = sem("pe_step"), sem("act_step"), sem("dve_step")
        rows_clear = sem("rows_clear")
        bias_clear = sem("bias_clear")
        c_const = sem("c_const")
        c_vec = sem("c_vec")
        c_tok = [sem("c_tok0"), sem("c_tok1")]
        c_ada = [sem("c_ada0"), sem("c_ada1")]
        ada_used = sem("ada_used")
        c_gate = sem("c_gate")
        c_rows = sem("c_rows")
        c_bc = sem("c_bc")
        c_gbc = sem("c_gbc")
        c_four = sem("c_four")
        c_fw = sem("c_fw")
        c_inv = sem("c_inv")
        c_out = [sem("c_out0"), sem("c_out1")]

        DIRS = (0, 1)
        pos = {"pe": STEP_CREDIT, "act": STEP_CREDIT, "dve": STEP_CREDIT}
        sems = {"pe": pe_step, "act": act_step, "dve": dve_step}

        def stage(names, times=1):
            out_ = {}
            for e in ("pe", "act", "dve"):
                s = Steps(sems[e], pos[e], names.get(e, []), times)
                pos[e] = s.end
                out_[e] = s
            return out_

        NT = T // P
        st_vec = stage({"pe": ["vecT"], "act": ["silu_c"], "dve": ["vec"]})
        st_tok = stage({"pe": ["t0", "t1"], "act": ["c0", "c1"]}, NT // 2)
        st_tokc = stage({"pe": ["t0", "t1"], "act": ["c0", "c1"]})
        st_gain = stage({"dve": ["gain"]})

        def norm_stage(parts, last=False):
            a = [f"sq0{k}" for k in range(KB)] + ["std0"]
            for n in range(parts):
                for k in range(KB):
                    a += ([] if last else [f"hi{n}{k}"]) + ([f"sq{n + 1}{k}"] if n + 1 < parts else [])
                if n + 1 < parts:
                    a.append(f"std{n + 1}")
            v = [f"add{k}" for k in range(1, KB)]
            for n in range(parts):
                v.append(f"rs{n}")
                for k in range(KB):
                    v.append(f"t{n}{k}")
                    if k >= 1 and not last:
                        v.append(f"lo{n}{k - 1}")
                if not last:
                    v.append(f"lo{n}{KB - 1}")
            return stage({"pe": ["sum0"] + [f"s{n}{k}" for n in range(1, parts) for k in range(KB)],
                          "act": a, "dve": v})

        st_n0 = norm_stage(3)
        st_gate = stage({"pe": ["gates", "colsA", "colsW", "colsE"],
                         "act": ["ln", "w", "em"],
                         "dve": ["w_lo", "f", "G", "g_nat", "a_nat", "w_in", "w_nat", "e_in", "e_nat", "cols"]})

        head_act, head_dve, head_pe = [], [], []
        head_pe += ["vT0", "vT1"]
        for n in ("q0", "q1", "k0", "k1"):
            head_dve.append(f"conv_{n}")
            head_act.append(f"silu_{n}")
            if n == "k0":
                head_dve.append("vtok0")
            if n == "k1":
                head_dve.append("vtok1")
        head_pe += ["kT0", "kT1"]
        head_dve += ["ktok0", "ktok1"]
        SEQ = [(j, d) for j in range(NCH) for d in DIRS]
        for n, (j, d) in enumerate(SEQ):
            following = SEQ[n + 1] if n + 1 < len(SEQ) else (0, 0)
            if following[0] >= NCC:
                head_pe.append("S%d%d" % following)
                head_dve.append("E%d%d" % following)
                head_act += ["D%d%d" % following, "I%d%d" % following]
            if j >= NCC:
                head_dve += [f"P{j}{d}", f"Q{j}{d}"]
                head_pe.append(f"N{j}{d}")
            if j < NCH - 1:
                head_dve.append(f"kw{j}{d}")
                head_pe.append(f"U{j}{d}")
            for pj, pd in (SEQ[n - 1:n] if n else []) + ([(j, d)] if n == len(SEQ) - 1 else []):
                if pj >= NCC:
                    head_dve.append(f"h{pj}{pd}")
                if pj < NCH - 1:
                    head_dve.append(f"C{pj}{pd}")
        head_pe += ["hT0", "hT1"]
        head_dve += ["hf0", "hf1", "o0", "o1"]
        head_act += ["sq0", "sq1"]
        head_pe += ["hsum"]
        head_act += ["hstd"]
        head_dve += ["hrs", "z0", "z1"]
        head_act += ["yh0", "yh1"]
        head_dve += ["yl0", "yl1"] + [f"acc{m}" for m in range(KB)]
        st_head = stage({"pe": head_pe, "act": head_act, "dve": head_dve}, HEADS)

        st_four = stage({
            "pe": ["cf", "V0", "V1", "V2", "V3", "V4", "V5", "V6", "V7", "Y0", "Y1"],
            "act": ["cf", "y0", "y1", "yh0", "yh1"],
            "dve": ["fold", "V0", "V1", "V2", "V3", "V4", "V5", "V6", "V7", "z0", "z1", "yl0", "yl1"]
            + [f"acc{m}" for m in range(KB)]}, GROUPS)
        st_n1 = norm_stage(2)
        st_pool = stage({
            "act": [f"ph{m}" for m in range(4)] + [f"yh{m}" for m in range(4)],
            "dve": [f"p{m}" for m in range(4)] + [f"pl{m}" for m in range(4)] + ["z0", "z1", "yl0", "z2", "yl1", "z3", "yl2", "yl3"] + [f"acc{m}" for m in range(KB)]}, GROUPS)
        st_n2 = norm_stage(2, last=True)
        st_end = stage({"pe": ["t0", "t1"], "act": ["c0", "c1"]}, NT // 2)

        HU, FU, PU = sum(HEAD_UNITS), sum(FOUR_UNITS), sum(POOL_UNITS)
        U_FOUR = HEADS * HU
        U_POOL = U_FOUR + GROUPS * FU
        B_FOUR = HEADS * len(HEAD_UNITS)
        B_POOL = B_FOUR + GROUPS * len(FOUR_UNITS)

        we = win_even[0].rearrange("(k p) m -> p k m", p=P)
        wo = win_odd[0].rearrange("(k p) m -> p k m", p=P)
        woe = wout_even[0].rearrange("(k p) m -> p k m", p=P)
        woo = wout_odd[0].rearrange("(k p) m -> p k m", p=P)
        pw = pool_w[0].rearrange("g (k p) m -> p (g k) m", p=P)
        ada_v = ada_w.rearrange("l (k p) (b m) -> p l k b m", p=P, m=512)

        def bcast(dram, offset, n):
            a = dram[:].rearrange("a b -> (a b)")
            return a[bass.ds(offset, n)].partition_broadcast(P)

        def bcast_ap(dram, g):
            return dram.rearrange("a b -> (a b)")[bass.ds(g * T, T)].partition_broadcast(P)

        def accumulate(act, u, ev, layer, SD, i):
            for m in range(KB):
                act.wait_ge(unit_done, u + m + 1 + CREDIT)
                act.wait_ge(dve_step, SD.at(f"acc{m - 2}" if m >= 2 else f"z{m}", i))
                act.activation(ev[m % 2][:], ps[m % 2][:].rearrange("p a b -> p (a b)"), ACT.Identity,
                               scale=mod[:, layer, 16 + m, 0:1], bias=zero[:]).then_inc(unit_out, 1)

        def gather(dve, dst, i):
            for n, bank in enumerate((ps[2][:, 1, :], ps[3][:, 0, :], ps[3][:, 1, :])):
                cnt = min(4, NCH - 4 * n)
                ins = dve.tensor_copy(dst[:, 4 * n:4 * n + cnt, i * P:(i + 1) * P],
                                      bank[:, 0:cnt * P].rearrange("p (c f) -> p c f", f=P))
            return ins

        def add_up(dve, u, ev, SD, i):
            for m in range(KB):
                dve.wait_ge(unit_out, u + m + 1 + CREDIT)
                SD.done(dve.tensor_tensor(resid[:, m, :], resid[:, m, :], ev[m % 2][:], ALU.add), f"acc{m}")

        block = stack.enter_context(nc.Block())

        @block.sync
        def _(sp):
            sp.dma_start(ident[:], tab_ident).then_inc(c_const, 16)
            sp.dma_start(mask[:], tab_mask).then_inc(c_const, 16)
            sp.wait_ge(rows_clear, 1)
            rows = lambda a: a.rearrange("(k p) -> k p", p=P)
            for t, a0, n, src in ((0, ADA_B, 48, ada_b.rearrange("l (k p) -> (l k) p", p=P)),
                                  (0, NORM_G, 16, norm_g.rearrange("l (k p) -> (l k) p", p=P)),
                                  (0, FINAL_G, 8, rows(final_g)), (0, HEAD_G, 8, rows(head_norm[0])),
                                  (0, POOL_S, 16, rows(pool_scale[0])),
                                  (0, C_VEC, 8, rows(c[0])), (0, C_VEC + 8, 8, rows(c_ctx)),
                                  (1, 0, 48, conv_qk[0].rearrange("j (k p) -> (j k) p", p=P))):
                sp.dma_start(vrow[a0:a0 + n, t, :], src).then_inc(c_vec, 16)
            def ada(lay, i):
                for j in range(2):
                    sp.wait_ge(ada_used, 6 * lay + 2 * i + j - 1 + ADA_CREDIT)
                    sp.dma_start(ada_buf[j][:], ada_v[:, lay, :, bass.ds(2 * i + j, 1), :].rearrange(
                        "p k b m -> p k (b m)")).then_inc(c_ada[j], 16)

            def tokens(i):
                for j in range(2):
                    sp.wait_ge(pe_step, st_tok["pe"].at(f"t{j}", i - 1))
                    sp.dma_start(tok[j][:], x[0, bass.ds((2 * i + j) * P, P), :]).then_inc(c_tok[j], 16)

            with sp.Fori(0, 3) as i:
                tokens(i)
                ada(0, i)
            tokens(3)
            for j in range(2):
                sp.wait_ge(pe_step, st_tok["pe"].at(f"t{j}", NT // 2 - 1))
                sp.dma_start(tok[j][:], ctx_in[0, j * P:(j + 1) * P, :]).then_inc(c_tok[j], 16)
            with sp.Fori(0, 3) as i:
                ada(1, i)
            sp.wait_ge(dve_step, st_n0["dve"].end)
            sp.dma_start(g_in[:], we[:, :, 7 * D:7 * D + 16]).then_inc(c_gate, 16)
            sp.wait_ge(bias_clear, 1)
            for kind in range(2):
                for d in range(2):
                    row = 2 * d + kind
                    sp.dma_start(g_bias[32 * d:32 * d + 4, kind:kind + 1],
                                 gate_b[0, 4 * row:4 * row + 4].rearrange("(r o) -> r o", o=1)).then_inc(c_gate, 16)

            def load(b, j, src, k):
                sp.wait_ge(w_ready, b - 1 + CREDIT)
                sp.dma_start(w_raw[j % 2][:].rearrange("p (k m) -> p k m", k=k), src).then_inc(w_landed[j % 2], 16)

            with sp.Fori(0, HEADS) as h:
                b = h * len(HEAD_UNITS)
                for n, part in enumerate((0, 2, 1, 3, 4)):
                    for i in range(2):
                        load(b + 2 * n + i, i, we[:, :, bass.ds(h * DH + part * D + i * P, P)], KB)
                for i in range(2):
                    load(b + 10 + i, i, woe[:, bass.ds(2 * h, 2), i * 512:(i + 1) * 512], 2)
            with sp.Fori(0, GROUPS) as g:
                b = g * len(FOUR_UNITS) + B_FOUR
                for n, part in enumerate((5, 6)):
                    for i in range(2):
                        load(b + 2 * n + i, i, we[:, :, bass.ds(g * DH + part * D + i * P, P)], KB)
                for i in range(2):
                    load(b + 4 + i, i, woe[:, bass.ds(2 * g + 8, 2), i * 512:(i + 1) * 512], 2)
            with sp.Fori(0, GROUPS) as g:
                b = g * len(POOL_UNITS) + B_POOL
                for i in range(4):
                    load(b + i, i, wo[:, :, bass.ds(g * 512 + i * P, P)], KB)
                for i in range(4):
                    load(b + 4 + i, i, wo[:, :, bass.ds(g * 512 + 2 * D + i * P, P)], KB)
                for i in range(2):
                    load(b + 8 + i, i, pw[:, bass.ds(4 * g, 4), i * 256:(i + 1) * 256], 4)
                for i in range(4):
                    load(b + 10 + i, i, woo[:, bass.ds(4 * g, 4), i * 256:(i + 1) * 256], 4)
            for i in range(NT // 2):
                for j in range(2):
                    sp.wait_ge(act_step, st_end["act"].at(f"c{j}", i))
                    sp.dma_start(out[0, (2 * i + j) * P:(2 * i + j + 1) * P, :], o_tok[j][:]).then_inc(c_out[j], 16)
            for j in range(2):
                sp.wait_ge(c_out[j], 16 * (NT // 2))

        @block.gpsimd
        def _(pool):
            pool.memset(ones[:], 1.0).then_inc(act_step, STEP_CREDIT)
            pool.memset(eps[:], EPS).then_inc(dve_step, STEP_CREDIT)
            pool.memset(zero[:], 0.0).then_inc(unit_done, CREDIT)
            for n, (counter, start) in enumerate(((w_ready, CREDIT), (unit_out, CREDIT), (pe_step, STEP_CREDIT),
                                                  (ctx_out, 1), (ada_used, ADA_CREDIT))):
                pool.memset(seed[:, n:n + 1], 0.0).then_inc(counter, start)
            pool.drain()

            def split(base, i, units):
                ubase, bbase = base
                per, nb = sum(units), len(units)
                for j in range(nb):
                    before = sum(units[:j - 1]) if j >= 1 else -units[-1]
                    s = j % 2
                    pool.wait_ge(w_landed[s], 16 * (i * (nb // 2) + (bbase + j) // 2 + 1))
                    pool.wait_ge(unit_done, i * per + ubase + before + CREDIT)
                    pool.tensor_tensor(w_hi[s][:], w_raw[s][:], zero[:].to_broadcast([P, D]), ALU.add
                                       ).then_inc(w_high, 1)
                    pool.wait_ge(w_high, i * nb + bbase + j + 1)
                    pool.tensor_tensor(w_lo[s][:], w_raw[s][:], w_hi[s][:].bitcast(F32), ALU.subtract
                                       ).then_inc(w_ready, 1)

            with pool.Fori(0, HEADS) as i:
                split((0, 0), i, HEAD_UNITS)
            with pool.Fori(0, GROUPS) as i:
                split((U_FOUR, B_FOUR), i, FOUR_UNITS)
            with pool.Fori(0, GROUPS) as i:
                split((U_POOL, B_POOL), i, POOL_UNITS)

        @block.tensor
        def _(pe):
            def three(dst, ah, al, bh, bl, start, stop):
                pe.matmul(dst, ah, bh, start=start, stop=False)
                pe.matmul(dst, ah, bl, start=False, stop=False)
                return pe.matmul(dst, al, bh, start=False, stop=stop)

            pe.wait_ge(c_const, 32)
            pe.wait_ge(c_vec, 8 * 16)
            pe.transpose(ps[0][:, 0, 0:P], vrow[:, 0, :], ident[:])
            st_vec["pe"].done(pe.transpose(ps[0][:, 0, P:2 * P], vrow[:, 1, :], ident[:]), "vecT")

            def token_tile(st, i, j, landed):
                pe.wait_ge(c_tok[j], landed)
                pe.wait_ge(act_step, st["act"].at(f"c{j}", i - 1) if st is st_tok
                           else st_tok["act"].at(f"c{j}", NT // 2 - 1))
                for k in range(KB):
                    m = pe.transpose(ps[2 + j][:, k // 4, (k % 4) * P:(k % 4 + 1) * P],
                                     tok[j][:, k * P:(k + 1) * P], ident[:])
                st["pe"].done(m, f"t{j}")

            def modulation(lay, i):
                for j in range(2):
                    pe.wait_ge(c_ada[j], 16 * (3 * lay + i + 1))
                    for m4 in range(4):
                        for k in range(KB):
                            m = pe.matmul(ps[0][:, lay, bass.ds((2 * i + j) * 8 + 2 * m4, 2)],
                                          ada_buf[j][:, k, m4 * P:(m4 + 1) * P], c_silu[:, k, :],
                                          start=(k == 0), stop=(k == KB - 1))
                    m.then_inc(ada_used, 1)

            pe.wait_ge(act_step, st_vec["act"].at("silu_c"))
            with pe.Fori(0, 3) as i:
                for j in range(2):
                    token_tile(st_tok, i, j, 16 * i + 16)
                modulation(0, i)
            for j in range(2):
                token_tile(st_tok, 3, j, 16 * 3 + 16)
            for j in range(2):
                token_tile(st_tokc, 0, j, 16 * (NT // 2) + 16)

            def norm(st, widths, sq, total, between=None):
                for n, width in enumerate(widths):
                    bank = ps[2 + n // 2][:, n % 2, 0:width]
                    if n == 0:
                        pe.wait_ge(dve_step, st["dve"].at(f"add{KB - 1}"))
                        st["pe"].done(pe.matmul(bank, ones[:], total[:, 0:width], start=True, stop=True), "sum0")
                    else:
                        for k in range(KB):
                            pe.wait_ge(act_step, st["act"].at(f"sq{n}{k}"))
                            st["pe"].done(pe.matmul(bank, ones[:], sq[k % 2][:, 0:width],
                                                    start=(k == 0), stop=(k == KB - 1)), f"s{n}{k}")
                    if between:
                        between(n)

            norm(st_n0, (HALF, HALF, TC), n_sq, n_t[0], lambda n: modulation(1, n))

            pe.wait_ge(dve_step, st_gate["dve"].at("w_lo"))
            for kind, bank in ((0, ps[0]), (1, ps[1])):
                for half in range(2):
                    for k in range(KB):
                        s = slice(half * HALF, (half + 1) * HALF)
                        three(bank[:, half, :], g_wh[:, k, kind, :], g_wl[:, k, kind, :], h_hi[:, k, s], h_lo[:, k, s],
                              k == 0, k == KB - 1)
                for k in range(KB):
                    m = three(ps[3][:, kind, 0:TC], g_wh[:, k, kind, :], g_wl[:, k, kind, :], hc_hi[:, k, :],
                              hc_lo[:, k, :], k == 0, k == KB - 1)
            st_gate["pe"].done(m, "gates")
            for n, (name, src, want) in enumerate((("colsA", g_nat, "a_nat"), ("colsW", g_s, "w_nat"),
                                                   ("colsE", g_e, "e_nat"))):
                pe.wait_ge(dve_step, st_gate["dve"].at(want))
                for ch in range(NCH):
                    bank = (ps[0], ps[1], ps[3])[n]
                    m = pe.transpose(bank[:, ch // 8, (ch % 8) * 64:(ch % 8) * 64 + 64],
                                     src[:, ch * CHUNK:(ch + 1) * CHUNK], ident[0:64, 0:64])
                st_gate["pe"].done(m, name)

            def begin(b):
                pe.wait_ge(w_ready, b + 1 + CREDIT)

            def unit(s, u, lhs, rhs, ks, more=None):
                pe.wait_ge(unit_out, u - 1 + CREDIT)
                bank = ps[s]
                for half in range(2):
                    for k in ks:
                        m = three(bank[:, half, :], *lhs(k), rhs[0][:, k, half * HALF:(half + 1) * HALF],
                                  rhs[1][:, k, half * HALF:(half + 1) * HALF], k == ks[0], k == ks[-1])
                m.then_inc(unit_done, 1)

            def wide(s, m0, width):
                return lambda k: (w_hi[s][:, k * width + m0:k * width + m0 + P],
                                  w_lo[s][:, k * width + m0:k * width + m0 + P])

            pe.wait_ge(dve_step, st_gate["dve"].end)
            with pe.Fori(0, HEADS) as h:
                b, u = h * len(HEAD_UNITS), h * HU
                SA, SD, SP_ = st_head["act"], st_head["dve"], st_head["pe"]

                def project(n, context=None):
                    begin(b + n)
                    if context is not None:
                        pe.wait_ge(ctx_out, h * 4 + context + 1)
                        for k in range(KB):
                            three(ps[2][:, 0, 0:TC], *wide(n % 2, 0, P)(k), hc_hi[:, k, :], hc_lo[:, k, :],
                                  k == 0, k == KB - 1)
                    unit(n % 2, u + n, wide(n % 2, 0, P), (h_hi, h_lo), range(KB))

                pe.wait_ge(dve_step, SD.at("hrs", h - 1))
                project(0)
                project(1)
                project(2, 0)
                project(3, 1)
                project(4, 2)

                def turn(src, i, name):
                    for ch in range(NCH):
                        col = ch * P
                        bank = (ps[2][:, 1, :], ps[3][:, 0, :], ps[3][:, 1, :])[col // HALF]
                        m = pe.transpose(bank[:, col % HALF:col % HALF + P], src[:, i, ch * P:(ch + 1) * P], ident[:])
                    SP_.done(m, name)

                pe.wait_ge(ctx_out, h * 4 + 3)
                pe.wait_ge(unit_out, u + 4 + CREDIT)
                turn(k_t, 0, "vT0")
                project(5, 3)
                pe.wait_ge(dve_step, SD.at("vtok0", h))
                turn(k_t, 1, "vT1")
                pe.wait_ge(act_step, SA.at("silu_k1", h))
                pe.wait_ge(dve_step, SD.at("vtok1", h))
                turn(k_t, 0, "kT0")
                pe.wait_ge(dve_step, SD.at("ktok0", h))
                turn(k_t, 1, "kT1")
                pe.wait_ge(dve_step, SD.at("ktok1", h))
                def scores(j, d):
                    n = nat_chunk(d, j)
                    t = (n - NCC) * CHUNK
                    if j > NCC:
                        pe.wait_ge(dve_step, SD.at(f"P{j - 1}{d}", h))
                    else:
                        pe.wait_ge(unit_out, u + 6 + CREDIT)
                    for i in range(2):
                        m = pe.matmul(ps[0][:, d, 0:CHUNK], k_t[:, i, n * CHUNK:(n + 1) * CHUNK],
                                      q_t[:, i, t:t + CHUNK], start=(i == 0), stop=(i == 1))
                    SP_.done(m, f"S{j}{d}")

                for s, (j, d) in enumerate(SEQ):
                    if s + 1 < len(SEQ) and SEQ[s + 1][0] >= NCC:
                        scores(*SEQ[s + 1])
                    n = nat_chunk(d, j)
                    if j >= NCC:
                        n_b = ps[1][:, d, 0:DH + 1]
                        pe.wait_ge(dve_step, SD.at(f"Q{j}{d}", h))
                        pe.matmul(n_b, pr[d][:], v_tok[:, n, :], start=True, stop=False)
                        pe.matmul(n_b, qi[d][:, 0, :], cst[:, d, 0, :], start=False, stop=False)
                        SP_.done(pe.matmul(n_b, qi[d][:, 1, :], cst[:, d, 1, :], start=False, stop=True),
                                 f"N{j}{d}")
                    if j < NCH - 1:
                        pe.wait_ge(dve_step, SD.at(f"kw{j}{d}", h))
                        for i in range(2):
                            m = pe.matmul(ps[2 + d][:, i, 0:DH + 1], kw[d][:, i * P:(i + 1) * P], v_tok[:, n, :],
                                          start=True, stop=True)
                        SP_.done(m, f"U{j}{d}")
                for i in range(2):
                    pe.wait_ge(dve_step, SD.at(f"h{NCH - 1}1", h))
                    for n in range(NCX):
                        m = pe.transpose(ps[2 + i][:, n // 4, (n % 4) * P:(n % 4 + 1) * P],
                                         h_tok[:, n, i * P:(i + 1) * P], ident[:])
                    SP_.done(m, f"hT{i}")
                project(6)
                project(7)
                for half in range(2):
                    for i in range(2):
                        pe.wait_ge(act_step, SA.at(f"sq{i}", h))
                        if half == 0 and i == 0:
                            pe.wait_ge(dve_step, SD.at("hf1", h))
                        m = pe.matmul(ps[2][:, half, :], ones[:], k_t[:, i, half * HALF:(half + 1) * HALF],
                                      start=(i == 0), stop=(i == 1))
                SP_.done(m, "hsum")
                project(8)
                project(9)
                for n in range(2):
                    begin(b + 10 + n)
                    if n == 0:
                        pe.wait_ge(dve_step, SD.at("yl1", h))
                    for m4 in range(4):
                        unit(m4 % 2, u + 10 + 4 * n + m4, wide(n, m4 * P, 512), (yh2, yl2), range(2))

            with pe.Fori(0, GROUPS) as g:
                b, u = g * len(FOUR_UNITS) + B_FOUR, g * FU + U_FOUR
                SA, SD, SP_ = st_four["act"], st_four["dve"], st_four["pe"]
                pe.wait_ge(c_fw, 16 * g + 16)
                pe.wait_ge(c_four, 64)
                pe.wait_ge(dve_step, SD.at("V7", g - 1))
                pe.wait_ge(act_step, SA.at("y1", g - 1))
                for f in range(2):
                    for i in range(2):
                        for k in range(2):
                            m = pe.matmul(ps[2][:, i, f * DH:(f + 1) * DH], ccs[:, f, k, i * P:(i + 1) * P], fw[:, k, :],
                                          start=(k == 0), stop=(k == 1))
                SP_.done(m, "cf")
                for n in range(2):
                    begin(b + n)
                    unit(n, u + n, wide(n, 0, P), (h_hi, h_lo), range(KB))
                pe.wait_ge(dve_step, SD.at("fold", g))
                pe.wait_ge(act_step, SA.at("cf", g))
                for n, (arr, tb) in enumerate(((0, 0), (0, 1), (2, 0), (2, 1), (3, 0), (1, 0), (3, 1), (1, 1))):
                    bank = ps[2 + (n % 4) // 2][:, n % 2, :]
                    if n >= 4:
                        pe.wait_ge(dve_step, SD.at(f"V{n - 4}", g))
                    for ch in range(2):
                        m = pe.matmul(bank, fd[:, ch, arr, tb * P:(tb + 1) * P], cfsf[:, ch, :],
                                      start=(ch == 0), stop=(ch == 1))
                    SP_.done(m, f"V{n}")
                for i in range(2):
                    pe.wait_ge(dve_step, SD.at("V7", g))
                    for rr in range(RADIX):
                        dst = ps[2 + i][:, rr // 2, (rr % 2) * TF:(rr % 2 + 1) * TF]
                        for tb in range(2):
                            for z, tab in ((0, ct), (1, ns)):
                                m = pe.matmul(dst, pq[:, tb, rr, z * DH + i * P:z * DH + (i + 1) * P],
                                              tab[:, tb, rr * TF:(rr + 1) * TF], start=(tb == 0 and z == 0),
                                              stop=(tb == 1 and z == 1))
                    SP_.done(m, f"Y{i}")
                for n in range(2):
                    begin(b + 2 + n)
                    unit(n, u + 2 + n, wide(n, 0, P), (h_hi, h_lo), range(KB))
                for n in range(2):
                    begin(b + 4 + n)
                    if n == 0:
                        pe.wait_ge(dve_step, SD.at("yl1", g))
                    for m4 in range(4):
                        unit(m4 % 2, u + 4 + 4 * n + m4, wide(n, m4 * P, 512), (yh_f, yl_f), range(2))

            norm(st_n1, (HALF, HALF), m_sq, m_t[0])

            pe.wait_ge(dve_step, st_n1["dve"].end)
            with pe.Fori(0, GROUPS) as g:
                b, u = g * len(POOL_UNITS) + B_POOL, g * PU + U_POOL
                SA, SD = st_pool["act"], st_pool["dve"]
                for n in range(8):
                    begin(b + n)
                    unit(n % 2, u + n, wide(n % 2, 0, P), (h_hi, h_lo), range(KB))
                for n in range(2):
                    begin(b + 8 + n)
                    if n == 0:
                        pe.wait_ge(dve_step, SD.at("pl3", g))
                    for m2 in range(2):
                        unit(m2, u + 8 + 2 * n + m2, wide(n, m2 * P, 256), (yh_p, yl_p), range(4))
                for n in range(4):
                    begin(b + 10 + n)
                    if n == 0:
                        pe.wait_ge(dve_step, SD.at("yl3", g))
                    for m2 in range(2):
                        unit(m2, u + 12 + 2 * n + m2, wide(n % 2, m2 * P, 256), (yh_g, yl_g), range(4))

            norm(st_n2, (HALF, HALF), m_sq, m_t[0])
            pe.wait_ge(dve_step, st_n2["dve"].end)
            for i in range(NT // 2):
                for j in range(2):
                    pe.wait_ge(act_step, st_end["act"].at(f"c{j}", i - 1))
                    for k in range(KB):
                        m = pe.transpose(ps[2 + j][:, k // 4, (k % 4) * P:(k % 4 + 1) * P],
                                         resid[:, k, (2 * i + j) * P:(2 * i + j + 1) * P], ident[:])
                    st_end["pe"].done(m, f"t{j}")

        @block.scalar
        def _(act):
            def flat(bank):
                return bank[:].rearrange("p a b -> p (a b)")

            act.wait_ge(dve_step, st_vec["dve"].at("vec"))
            st_vec["act"].done(act.activation(c_silu[:].rearrange("p k s -> p s k"),
                                              vec[:, C_VEC:C_VEC + 16].rearrange("p (s k) -> p s k", s=2),
                                              ACT.Silu), "silu_c")
            with act.Fori(0, NT // 2) as i:
                for j in range(2):
                    act.wait_ge(pe_step, st_tok["pe"].at(f"t{j}", i))
                    st_tok["act"].done(act.copy(resid[:, :, bass.ds((2 * i + j) * P, P)],
                                                flat(ps[2 + j]).rearrange("p (k t) -> p k t", k=KB)), f"c{j}")
            for j in range(2):
                act.wait_ge(pe_step, st_tokc["pe"].at(f"t{j}"))
                st_tokc["act"].done(act.copy(xc_t[:, :, j * P:(j + 1) * P],
                                             flat(ps[2 + j]).rearrange("p (k t) -> p k t", k=KB)), f"c{j}")
            def norm(st, parts, sq, t_, rs):
                last = parts[0][4] is None

                def square(n, k):
                    src, t0, width = parts[n][:3]
                    if n == 0 and k >= 2:
                        act.wait_ge(dve_step, st["dve"].at(f"add{max(k - 2, 1)}"))
                    elif n and k >= 2:
                        act.wait_ge(pe_step, st["pe"].at(f"s{n}{k - 2}"))
                    elif n > 1:
                        act.wait_ge(pe_step, st["pe"].at(f"s{n - 1}{KB - 2 + k}"))
                    elif n:
                        act.wait_ge(dve_step, st["dve"].at(f"add{KB - 1}"))
                    st["act"].done(act.activation(sq[k % 2][:, 0:width], src[:, k, t0:t0 + width], ACT.Square),
                                   f"sq{n}{k}")

                def root(n):
                    act.wait_ge(pe_step, st["pe"].at(f"s{n}{KB - 1}" if n else "sum0"))
                    if n:
                        act.wait_ge(dve_step, st["dve"].at(f"t{n - 1}{KB - 1}"))
                    width = parts[n][2]
                    st["act"].done(act.activation(rs[:, 0:width], ps[2 + n // 2][:, n % 2, 0:width], ACT.Sqrt,
                                                  scale=1.0 / D, bias=eps[:]), f"std{n}")

                for k in range(KB):
                    square(0, k)
                root(0)
                for n, (src, t0, width, shift, hi) in enumerate(parts):
                    for k in range(KB):
                        if not last:
                            act.wait_ge(dve_step, st["dve"].at(f"t{n}{k}"))
                            st["act"].done(act.activation(hi[:, k, t0:t0 + width], t_[(n * KB + k) % 3][:, 0:width],
                                                          ACT.Identity, bias=shift(k)), f"hi{n}{k}")
                        if n + 1 < len(parts):
                            square(n + 1, k)
                    if n + 1 < len(parts):
                        root(n + 1)

            act.wait_ge(dve_step, st_gain["dve"].at("gain"))
            act.wait_ge(act_step, st_tokc["act"].end)
            norm(st_n0, [(resid, 0, HALF, lambda k: mod[:, 0, k, 0:1], h_hi),
                         (resid, HALF, HALF, lambda k: mod[:, 0, k, 0:1], h_hi),
                         (xc_t, 0, TC, lambda k: mod[:, 0, k, 1:2], hc_hi)], n_sq, n_t, n_rs)

            SG = st_gate
            act.wait_ge(dve_step, SG["dve"].at("f"))
            act.activation(g_e[:], g_f[:], ACT.Abs)
            act.drain()
            act.activation(g_e[:], g_e[:], ACT.Exp, scale=-1.0)
            act.drain()
            SG["act"].done(act.activation(g_e[:], g_e[:], ACT.Ln, bias=1.0), "ln")
            act.wait_ge(dve_step, SG["dve"].at("w_in"))
            SG["act"].done(act.activation(g_i[:], g_i[:], ACT.Exp), "w")
            act.wait_ge(dve_step, SG["dve"].at("e_in"))
            SG["act"].done(act.activation(g_f[:], g_f[:], ACT.Exp, scale=-1.0), "em")

            act.activation(g_small[:, 1, :], g_small[:, 1, :], ACT.Exp)
            act.drain()
            for d in range(2):
                act.dma_start(g_dram[4 * d:4 * d + 4, :], g_b[32 * d:32 * d + 4, :]).then_inc(c_rows, 16)
                act.dma_start(s_dram[4 * d:4 * d + 4, :], g_small[32 * d:32 * d + 4, 0:2, :]).then_inc(c_rows, 16)
            act.wait_ge(c_rows, 64)
            act.dma_start(chunk_sc[:].rearrange("p a b c -> p (a b c)"),
                          bcast(s_dram, 0, 16 * NCH)).then_inc(c_bc, 16)

            act.wait_ge(dve_step, SG["dve"].end)
            with act.Fori(0, HEADS) as h:
                u = h * HU
                SA, SD, SPE = st_head["act"], st_head["dve"], st_head["pe"]
                act.wait_ge(unit_done, u + CREDIT)
                act.wait_ge(dve_step, SD.at("acc7", h - 1))
                for d in range(2):
                    act.dma_start(g_bc[:, d, :], bcast(g_dram, (h + 4 * d) * (TC + T) + TC, T)).then_inc(c_gbc, 16)
                for n, name in enumerate(("q0", "q1", "v0", "v1", "k0", "k1")):
                    i = n % 2
                    act.wait_ge(unit_done, u + 1 + n + CREDIT)
                    if name[0] == "v":
                        act.copy(k_t[:, i, 0:TC], ps[2][:, 0, 0:TC]).then_inc(ctx_out, 1)
                        act.copy(k_t[:, i, TC:TC + T], flat(ps[i])).then_inc(unit_out, 1)
                        continue
                    before = {"q1": "q0", "k0": "q1", "k1": "k0"}.get(name)
                    if before:
                        act.wait_ge(dve_step, SD.at(f"conv_{before}", h))
                    if name[0] == "k":
                        act.copy(cbc[:, 1:TC + 1], ps[2][:, 0, 0:TC]).then_inc(ctx_out, 1)
                    act.copy(cb[:, 1:T + 1], flat(ps[i])).then_inc(unit_out, 1)
                    act.wait_ge(dve_step, SD.at(f"conv_{name}", h))
                    if name[0] == "q":
                        ins = act.activation(q_t[:, i, :], cv[:, TC:TC + T], ACT.Silu)
                    else:
                        act.wait_ge(pe_step, SPE.at(f"vT{i}", h))
                        ins = act.activation(k_t[:, i, :], cv[:], ACT.Silu)
                    SA.done(ins, f"silu_{name}")
                act.wait_ge(c_gbc, 32 * h + 32)
                act.wait_ge(c_bc, 16)
                for j in range(NCC, NCH):
                    for d in DIRS:
                        t = (nat_chunk(d, j) - NCC) * CHUNK
                        if j > NCC:
                            act.wait_ge(dve_step, SD.at(f"Q{j - 1}{d}", h))
                        act.wait_ge(dve_step, SD.at(f"E{j}{d}", h))
                        SA.done(act.activation(ee[d][:], ee[d][:], ACT.Exp, scale=-1.0), f"D{j}{d}")
                        SA.done(act.activation(it[d][:], g_bc[:, d, t:t + CHUNK], ACT.Exp, scale=-1.0,
                                               bias=chunk_sc[:, bass.ds(h + 4 * d, 1), 0, j:j + 1].rearrange(
                                                   "p a b -> p (a b)")), f"I{j}{d}")
                for i in range(2):
                    act.wait_ge(unit_done, u + 7 + i + CREDIT)
                    if i == 0:
                        act.wait_ge(act_step, SA.at(f"I{NCH - 1}1", h))
                    act.activation(ev_a[i][:], flat(ps[i]), ACT.Sigmoid).then_inc(unit_out, 1)
                for i in range(2):
                    act.wait_ge(dve_step, SD.at(f"o{i}", h))
                    SA.done(act.activation(k_t[:, i, 0:T], q_t[:, i, :], ACT.Square), f"sq{i}")
                act.wait_ge(pe_step, SPE.at("hsum", h))
                act.wait_ge(dve_step, SD.at("o1", h))
                SA.done(act.activation(ev_a[0][:], flat(ps[2]), ACT.Sqrt, scale=1.0 / DH, bias=eps[:]), "hstd")
                for i in range(2):
                    act.wait_ge(unit_done, u + 9 + i + CREDIT)
                    if i == 0:
                        act.wait_ge(dve_step, SD.at("hrs", h))
                    act.activation(ev_a[i][:], flat(ps[i]), ACT.Silu).then_inc(unit_out, 1)
                for i in range(2):
                    act.wait_ge(dve_step, SD.at(f"z{i}", h))
                    SA.done(act.activation(yh2[:, i, :], q_t[:, i, :], ACT.Copy), f"yh{i}")
                accumulate(act, u + 10, ev_a, 0, SD, h)

            act.wait_ge(dve_step, st_head["dve"].end)
            act.dma_start(ct[:], tab_ct.rearrange("(b p) m -> p b m", p=P)).then_inc(c_four, 16)
            act.dma_start(ns[:], tab_ns.rearrange("(b p) m -> p b m", p=P)).then_inc(c_four, 16)
            act.dma_start(ccs[:, 0], tab_cc.rearrange("(b p) m -> p b m", p=P)).then_inc(c_four, 16)
            act.dma_start(ccs[:, 1], tab_cs.rearrange("(b p) m -> p b m", p=P)).then_inc(c_four, 16)
            with act.Fori(0, GROUPS) as g:
                u = g * FU + U_FOUR
                SA, SD, SPE = st_four["act"], st_four["dve"], st_four["pe"]
                act.wait_ge(pe_step, SPE.at("cf", g - 1))
                act.dma_start(fw[:], fourier_w[0, bass.ds(g, 1)].rearrange("g (k p) m -> p (g k) m", p=P)
                              ).then_inc(c_fw, 16)
                act.wait_ge(pe_step, SPE.at("cf", g))
                SA.done(act.copy(cfsf[:], ps[2][:]), "cf")
                for i in range(2):
                    act.wait_ge(unit_done, u + 1 + i + CREDIT)
                    act.copy(u_f[:, i, :], flat(ps[i])).then_inc(unit_out, 1)
                for i in range(2):
                    act.wait_ge(pe_step, SPE.at(f"Y{i}", g))
                    SA.done(act.copy(y_f[:, i, :].rearrange("p (m r) -> p r m", r=RADIX),
                                     flat(ps[2 + i]).rearrange("p (r m) -> p r m", r=RADIX)), f"y{i}")
                for i in range(2):
                    act.wait_ge(unit_done, u + 3 + i + CREDIT)
                    if i == 0:
                        act.wait_ge(dve_step, SD.at("acc7", g - 1))
                    act.activation(ev_f[i][:], flat(ps[i]), ACT.Silu).then_inc(unit_out, 1)
                for i in range(2):
                    act.wait_ge(dve_step, SD.at(f"z{i}", g))
                    SA.done(act.activation(yh_f[:, i, :], y_f[:, i, :], ACT.Copy), f"yh{i}")
                accumulate(act, u + 4, ev_f, 0, SD, g)

            act.wait_ge(dve_step, st_four["dve"].end)
            norm(st_n1, [(resid, n * HALF, HALF, lambda k: mod[:, 1, k, 0:1], h_hi) for n in range(2)],
                 m_sq, m_t, m_rs)
            act.wait_ge(dve_step, st_n1["dve"].end)

            with act.Fori(0, GROUPS) as g:
                u = g * PU + U_POOL
                SA, SD = st_pool["act"], st_pool["dve"]
                act.wait_ge(dve_step, SD.at("acc7", g - 1))
                act.dma_start(inv[:], bcast_ap(tab_inv, g)).then_inc(c_inv, 16)
                for m in range(4):
                    act.wait_ge(unit_done, u + 1 + m + CREDIT)
                    act.copy(u_p[:, m, :], flat(ps[m % 2])).then_inc(unit_out, 1)
                def high(m):
                    act.wait_ge(dve_step, SD.at(f"p{m}", g))
                    SA.done(act.activation(yh_p[:, m, :], u_p[:, m, :], ACT.Copy), f"ph{m}")

                def gate(m):
                    act.wait_ge(unit_done, u + 5 + m + CREDIT)
                    act.activation(ev_p[m][:], flat(ps[m % 2]), ACT.Silu).then_inc(unit_out, 1)

                gate(0)
                high(0)
                gate(1)
                high(1)
                high(2)
                gate(2)
                high(3)
                gate(3)
                for m in range(5):
                    if m < 4:
                        act.wait_ge(unit_done, u + 9 + m + CREDIT)
                        if m == 0:
                            act.wait_ge(dve_step, SD.at("pl3", g))
                        act.activation(u_p[:, m, :], flat(ps[m % 2]), ACT.Identity,
                                       scale=vec[:, bass.ds(4 * g + POOL_S + m, 1)], bias=zero[:]).then_inc(unit_out, 1)
                    if m >= 1:
                        act.wait_ge(dve_step, SD.at(f"z{m - 1}", g))
                        SA.done(act.activation(yh_g[:, m - 1, :], u_p[:, m - 1, :], ACT.Copy), f"yh{m - 1}")
                accumulate(act, u + 12, ev_p, 1, SD, g)

            act.wait_ge(dve_step, st_pool["dve"].end)
            norm(st_n2, [(resid, n * HALF, HALF, None, None) for n in range(2)], m_sq, m_t, m_rs)
            for i in range(NT // 2):
                for j in range(2):
                    act.wait_ge(pe_step, st_end["pe"].at(f"t{j}", i))
                    if i:
                        act.wait_ge(c_out[j], 16 * i)
                    st_end["act"].done(act.copy(o_tok[j][:], flat(ps[2 + j])), f"c{j}")

        @block.vector
        def _(dve):
            def flat(bank):
                return bank[:].rearrange("p a b -> p (a b)")

            dve.memset(vrow[:], 0.0).then_inc(rows_clear, 1)
            dve.wait_ge(pe_step, st_vec["pe"].at("vecT"))
            st_vec["dve"].done(dve.tensor_copy(vec[:], ps[0][:, 0, 0:176]), "vec")

            def modulate(lay, blocks):
                dve.wait_ge(ada_used, blocks)
                for s in range(2):
                    dve.tensor_tensor(mod[:, lay, :, s], ps[0][:, lay, 0:48].rearrange("p (b s) -> p b s", s=2)[:, :, s],
                                      vec[:, ADA_B + 24 * lay:ADA_B + 24 * lay + 24], ALU.add)

            def gains(n, lay, s):
                return dve.scalar_tensor_tensor(gain[:, n, :], mod[:, lay, 8:16, s], 1.0,
                                                vec[:, NORM_G + 8 * lay:NORM_G + 8 * lay + 8], ALU.add, ALU.mult)

            modulate(0, 6 + ADA_CREDIT)
            dve.drain()
            gains(0, 0, 0)
            st_gain["dve"].done(gains(1, 0, 1), "gain")

            def norm(st, parts, sq, t_, rs):
                width = parts[0][2]
                for k in range(1, KB):
                    dve.wait_ge(act_step, st["act"].at(f"sq0{k}"))
                    st["dve"].done(dve.tensor_tensor(t_[0][:, 0:width], (sq[0] if k == 1 else t_[0])[:, 0:width],
                                                     sq[k % 2][:, 0:width], ALU.add), f"add{k}")
                    dve.drain()
                for n, (src, t0, width, gain_col, shift, hi, lo) in enumerate(parts):
                    dve.wait_ge(act_step, st["act"].at(f"std{n}"))
                    st["dve"].done(dve.reciprocal(rs[:, 0:width], rs[:, 0:width]), f"rs{n}")
                    dve.drain()

                    def low(k):
                        dve.wait_ge(act_step, st["act"].at(f"hi{n}{k}"))
                        st["dve"].done(dve.scalar_tensor_tensor(lo[:, k, t0:t0 + width],
                                                                t_[(n * KB + k) % 3][:, 0:width],
                                                                shift(k), hi[:, k, t0:t0 + width].bitcast(F32),
                                                                ALU.add, ALU.subtract), f"lo{n}{k}")

                    for k in range(KB):
                        cell = src[:, k, t0:t0 + width]
                        turn = n * KB + k
                        if hi is not None and turn >= 3:
                            dve.wait_ge(dve_step, st["dve"].at(f"lo{(turn - 3) // KB}{(turn - 3) % KB}"))
                        st["dve"].done(dve.scalar_tensor_tensor(cell if hi is None else t_[turn % 3][:, 0:width], cell,
                                                                gain_col(k), rs[:, 0:width], ALU.mult, ALU.mult),
                                       f"t{n}{k}")
                        if k >= 1 and hi is not None:
                            low(k - 1)
                    if hi is not None:
                        low(KB - 1)

            norm(st_n0, [(resid, 0, HALF, lambda k: gain[:, 0, k:k + 1], lambda k: mod[:, 0, k, 0:1], h_hi, h_lo),
                         (resid, HALF, HALF, lambda k: gain[:, 0, k:k + 1], lambda k: mod[:, 0, k, 0:1], h_hi, h_lo),
                         (xc_t, 0, TC, lambda k: gain[:, 1, k:k + 1], lambda k: mod[:, 0, k, 1:2], hc_hi, hc_lo)],
                 n_sq, n_t, n_rs)
            modulate(1, 12 + ADA_CREDIT)
            dve.drain()
            gains(2, 1, 0)

            SG = st_gate
            dve.wait_ge(dve_step, st_n0["dve"].end)
            dve.memset(g_bias[:], 0.0).then_inc(bias_clear, 1)
            dve.memset(g_w[:], 0.0)
            dve.wait_ge(c_gate, 16 * 5)
            dve.drain()
            for kind in range(2):
                for d in range(2):
                    row = 2 * d + kind
                    dve.tensor_copy(g_w[:, :, kind, 32 * d:32 * d + 4], g_in[:, :, 4 * row:4 * row + 4])
            dve.drain()
            dve.tensor_copy(g_wh[:], g_w[:])
            dve.drain()
            SG["dve"].done(dve.tensor_tensor(g_wl[:], g_w[:], g_wh[:].bitcast(F32), ALU.subtract), "w_lo")
            dve.wait_ge(pe_step, SG["pe"].at("gates"))
            for kind, dst, bank in ((0, g_i, ps[0]), (1, g_f, ps[1])):
                bc = slice(kind, kind + 1)
                dve.tensor_scalar(dst[0:32, 0:TC], ps[3][0:32, kind, 0:TC], g_bias[0:32, bc], None, ALU.add)
                dve.tensor_scalar(dst[0:32, TC:TC + T], flat(bank)[0:32], g_bias[0:32, bc], None, ALU.add)
                dve.tensor_scalar(dst[32:64, 0:TC], ps[3][32:64, kind, 0:TC][:, ::-1], g_bias[32:64, bc], None, ALU.add)
                ins = dve.tensor_scalar(dst[32:64, TC:TC + T], flat(bank)[32:64][:, ::-1], g_bias[32:64, bc], None,
                                        ALU.add)
            SG["dve"].done(ins, "f")
            dve.memset(g_s[:], 1.0)
            dve.memset(g_d[:], 0.0)
            dve.memset(g_small[:], 0.0)
            dve.drain()
            dve.memset(g_s[:, ::CHUNK], 0.0)
            dve.wait_ge(act_step, SG["act"].at("ln"))
            dve.scalar_tensor_tensor(g_f[:], g_f[:], 0.0, g_e[:], ALU.min, ALU.subtract)
            dve.drain()
            dve.tensor_tensor_scan(g_b[:], g_s[:], g_f[:], 0.0, ALU.mult, ALU.add)
            dve.drain()
            dve.tensor_tensor(g_i[:], g_i[:], g_b[:], ALU.subtract)
            dve.tensor_copy(g_d[:, CHUNK::CHUNK], g_b[:, CHUNK - 1:TC + T - CHUNK:CHUNK])
            dve.drain()
            SG["dve"].done(dve.tensor_tensor_scan(g_g[:], g_d[:], g_i[:], 0.0, ALU.add, ALU.max), "G")
            dve.wait_ge(dve_step, SG["dve"].at("G"))

            def natural(dst, src):
                dve.tensor_copy(dst[0:32, :], src[0:32, :])
                dve.tensor_copy(dst[32:64, 0:TC], src[32:64, 0:TC][:, ::-1])
                return dve.tensor_copy(dst[32:64, TC:TC + T], src[32:64, TC:TC + T][:, ::-1])

            ch = lambda a: a[:].rearrange("p (c t) -> p c t", t=CHUNK)
            SG["dve"].done(natural(g_nat, g_i), "g_nat")
            dve.tensor_tensor(g_small[:, 0, 1:NCH], g_g[:, CHUNK - 1:TC + T - CHUNK:CHUNK],
                              g_b[:, CHUNK - 1:TC + T - CHUNK:CHUNK], ALU.add)
            dve.tensor_copy(g_small[:, 2, :], g_g[:, CHUNK - 1::CHUNK])
            dve.drain()
            SG["dve"].done(dve.tensor_tensor(g_small[:, 1, :], g_small[:, 0, :], g_small[:, 2, :], ALU.subtract),
                           "a_nat")
            SG["dve"].done(dve.tensor_tensor(ch(g_i), ch(g_i),
                                             g_small[:, 2, :].unsqueeze(2).to_broadcast([64, NCH, CHUNK]),
                                             ALU.subtract), "w_in")
            dve.tensor_tensor(g_f[:], g_b[:], g_g[:], ALU.add)
            dve.drain()
            dve.wait_ge(act_step, SG["act"].at("w"))
            SG["dve"].done(natural(g_s, g_i), "w_nat")
            SG["dve"].done(natural(g_b, g_g), "e_in")
            dve.wait_ge(act_step, SG["act"].at("em"))
            SG["dve"].done(natural(g_e, g_f), "e_nat")
            dve.wait_ge(c_bc, 16)
            dve.drain()
            for n, (name, bank) in enumerate((("colsA", ps[0]), ("colsW", ps[1]), ("colsE", ps[3]))):
                dve.wait_ge(pe_step, SG["pe"].at(name))
                for lo_, hi_ in ((0, 8), (8, NCH)):
                    dve.tensor_copy(
                        cols[:, n, lo_:hi_, :].rearrange("p c (d r) -> p c d r", d=2),
                        bank[:, lo_ // 8, 0:(hi_ - lo_) * 64].rearrange("p (c d r) -> p c d r", d=2, r=32)[:, :, :, 0:4])
            dve.drain()
            dve.tensor_scalar(cols[:, 1], cols[:, 1], float(DH) ** -0.5, None, ALU.mult)
            SG["dve"].done(dve.tensor_copy(dn[:, 0, 0:1], zero[:]), "cols")
            dve.drain()

            dve.wait_ge(c_const, 32)
            with dve.Fori(0, HEADS) as h:
                u = h * HU
                SA, SD, SPE = st_head["act"], st_head["dve"], st_head["pe"]
                sc = float(DH) ** -0.5
                dve.memset(cb[:, 0:T + 2:T + 1], 0.0)
                dve.memset(cbc[:, 0:TC + 2:TC + 1], 0.0)
                for n, name in enumerate(("q0", "q1", "k0", "k1")):
                    if n == 0:
                        dve.drain()
                    wcol = lambda tap: vec[:, bass.ds(2 * h + (CONV + 16 * tap + 8 * (n // 2) + n % 2), 1)]
                    dve.wait_ge(unit_out, u + (1, 2, 5, 6)[n] + CREDIT)
                    if n:
                        dve.wait_ge(act_step, SA.at(f"silu_{('q0', 'q1', 'k0')[n - 1]}", h))
                    parts = [(cb, T, slice(TC, TC + T))]
                    if n >= 2:
                        parts.append((cbc, TC, slice(0, TC)))
                    for src, w, dst in parts:
                        dve.tensor_scalar(cv[:, dst], src[:, 0:w], wcol(0), None, ALU.mult)
                    dve.drain()
                    for src, w, dst in parts:
                        dve.scalar_tensor_tensor(cv[:, dst], src[:, 1:w + 1], wcol(1), cv[:, dst], ALU.mult, ALU.add)
                    dve.drain()
                    for src, w, dst in parts:
                        ins = dve.scalar_tensor_tensor(cv[:, dst], src[:, 2:w + 2], wcol(2), cv[:, dst], ALU.mult,
                                                       ALU.add)
                    SD.done(ins, f"conv_{name}")
                    if n >= 2:
                        dve.wait_ge(pe_step, SPE.at(f"vT{n - 2}", h))
                        SD.done(gather(dve, v_tok, n - 2), f"vtok{n - 2}")
                dve.memset(v_tok[:, :, DH:DH + 1], 1.0)
                dve.memset(cst[:], 0.0)
                for i in range(2):
                    dve.wait_ge(pe_step, SPE.at(f"kT{i}", h))
                    SD.done(gather(dve, k_tok, i), f"ktok{i}")
                dve.wait_ge(c_gbc, 32 * h + 32)
                dve.wait_ge(dve_step, SD.at("ktok1", h))
                col = lambda arr, n, d: cols[:, arr, n, bass.ds(h + 4 * d, 1)]

                def exponent(j, d):
                    n = nat_chunk(d, j)
                    t = (n - NCC) * CHUNK
                    SD.done(dve.scalar_tensor_tensor(ee[d][:], g_bc[:, d, t:t + CHUNK], col(0, n, d),
                                                     mask[:, d, :], ALU.subtract, ALU.add), f"E{j}{d}")

                def front(j, d):
                    n = nat_chunk(d, j)
                    t = (n - NCC) * CHUNK
                    if j >= NCC:
                        dve.wait_ge(pe_step, SPE.at(f"S{j}{d}", h))
                        dve.wait_ge(act_step, SA.at(f"D{j}{d}", h))
                        SD.done(dve.scalar_tensor_tensor(pr[d][:], ps[0][:, d, 0:CHUNK], sc, ee[d][:], ALU.mult,
                                                         ALU.mult), f"P{j}{d}")
                        dve.wait_ge(act_step, SA.at(f"I{j}{d}", h))
                        SD.done(dve.tensor_tensor(qi[d][:], q_t[:, :, t:t + CHUNK],
                                                  it[d][:].unsqueeze(1).to_broadcast([P, 2, CHUNK]), ALU.mult),
                                f"Q{j}{d}")
                    if j < NCH - 1:
                        SD.done(dve.tensor_scalar(kw[d][:], k_tok[:, n, :], col(1, n, d), None, ALU.mult),
                                f"kw{j}{d}")

                def back(j, d):
                    n = nat_chunk(d, j)
                    if j >= NCC:
                        nb = ps[1][:, d, :]
                        dve.wait_ge(pe_step, SPE.at(f"N{j}{d}", h))
                        den = nb[:, DH:DH + 1]
                        dve.tensor_scalar(dn[:, d, 0:1], den, -1.0, col(2, n, d), ALU.mult, ALU.max)
                        dve.drain()
                        dve.tensor_tensor(dn[:, d, 1:2], dn[:, d, 0:1], den, ALU.max)
                        dve.drain()
                        dve.reciprocal(dn[:, d, 2:3], dn[:, d, 1:2])
                        dve.drain()
                        hs = h_tok[:, n - NCC, :]
                        if j - NCC < NCX // 2:
                            ins = dve.tensor_scalar(hs, nb[:, 0:DH], dn[:, d, 2:3], None, ALU.mult)
                        else:
                            ins = dve.scalar_tensor_tensor(hs, nb[:, 0:DH], dn[:, d, 2:3], hs, ALU.mult, ALU.add)
                        SD.done(ins, f"h{j}{d}")
                    if j < NCH - 1:
                        dve.wait_ge(pe_step, SPE.at(f"U{j}{d}", h))
                        dec = chunk_sc[:, bass.ds(h + 4 * d, 1), 1, j:j + 1].rearrange("p a b -> p (a b)")
                        for i in range(2):
                            ins = dve.scalar_tensor_tensor(cst[:, d, i, :], cst[:, d, i, :], dec,
                                                           ps[2 + d][:, i, 0:DH + 1], ALU.mult, ALU.add)
                        SD.done(ins, f"C{j}{d}")

                for s, (j, d) in enumerate(SEQ):
                    if s + 1 < len(SEQ) and SEQ[s + 1][0] >= NCC:
                        exponent(*SEQ[s + 1])
                    front(j, d)
                    if s:
                        back(*SEQ[s - 1])
                    dve.drain()
                back(*SEQ[-1])
                for i in range(2):
                    dve.wait_ge(pe_step, SPE.at(f"hT{i}", h))
                    SD.done(dve.tensor_copy(q_t[:, i, :], flat(ps[2 + i])), f"hf{i}")
                dve.wait_ge(dve_step, SD.at("hf1", h))
                for i in range(2):
                    dve.wait_ge(unit_out, u + 7 + i + CREDIT)
                    SD.done(dve.tensor_tensor(q_t[:, i, :], q_t[:, i, :], ev_a[i][:], ALU.mult), f"o{i}")
                dve.wait_ge(act_step, SA.at("hstd", h))
                dve.reciprocal(ev_a[0][:], ev_a[0][:])
                dve.drain()
                for i in range(2):
                    ins = dve.tensor_tensor(q_t[:, i, :], q_t[:, i, :], ev_a[0][:], ALU.mult)
                SD.done(ins, "hrs")
                dve.wait_ge(dve_step, SD.at("hrs", h))
                for i in range(2):
                    dve.wait_ge(unit_out, u + 9 + i + CREDIT)
                    SD.done(dve.scalar_tensor_tensor(q_t[:, i, :], q_t[:, i, :],
                                                     vec[:, bass.ds(2 * h + HEAD_G + i, 1)], ev_a[i][:],
                                                     ALU.mult, ALU.mult), f"z{i}")
                for i in range(2):
                    dve.wait_ge(act_step, SA.at(f"yh{i}", h))
                    SD.done(dve.tensor_tensor(yl2[:, i, :], q_t[:, i, :], yh2[:, i, :].bitcast(F32), ALU.subtract),
                            f"yl{i}")
                add_up(dve, u + 10, ev_a, SD, h)

            with dve.Fori(0, GROUPS) as g:
                u = g * FU + U_FOUR
                SA, SD, SPE = st_four["act"], st_four["dve"], st_four["pe"]
                dve.wait_ge(unit_out, u + 2 + CREDIT)
                uq = lambda q: u_f[:].rearrange("p c (q t) -> p c q t", q=RADIX)[:, :, q, :]
                dve.tensor_tensor(f_tmp[:, :, 0, :], uq(0), uq(2), ALU.add)
                dve.tensor_tensor(f_tmp[:, :, 1, :], uq(1), uq(3), ALU.add)
                dve.tensor_tensor(fd[:, :, 1, :], uq(0), uq(2), ALU.subtract)
                dve.tensor_tensor(fd[:, :, 3, :], uq(1), uq(3), ALU.subtract)
                dve.drain()
                dve.tensor_tensor(fd[:, :, 0, :], f_tmp[:, :, 0, :], f_tmp[:, :, 1, :], ALU.add)
                SD.done(dve.tensor_tensor(fd[:, :, 2, :], f_tmp[:, :, 0, :], f_tmp[:, :, 1, :], ALU.subtract), "fold")
                lo_, hi_ = slice(0, DH), slice(DH, 2 * DH)
                for n, (arr, tb) in enumerate(((0, 0), (0, 1), (2, 0), (2, 1), (3, 0), (1, 0), (3, 1), (1, 1))):
                    bank = ps[2 + (n % 4) // 2][:, n % 2, :]
                    if n > 4:
                        dve.drain()
                    dve.wait_ge(pe_step, SPE.at(f"V{n}", g))
                    if arr in (0, 2):
                        ins = dve.tensor_copy(pq[:, tb, arr, :], bank)
                    elif arr == 3:
                        ins = dve.tensor_copy(f_b[:], bank)
                    else:
                        dve.tensor_tensor(pq[:, tb, 1, lo_], bank[:, lo_], f_b[:, hi_], ALU.subtract)
                        dve.tensor_tensor(pq[:, tb, 1, hi_], bank[:, hi_], f_b[:, lo_], ALU.add)
                        dve.tensor_tensor(pq[:, tb, 3, lo_], bank[:, lo_], f_b[:, hi_], ALU.add)
                        ins = dve.tensor_tensor(pq[:, tb, 3, hi_], bank[:, hi_], f_b[:, lo_], ALU.subtract)
                    SD.done(ins, f"V{n}")
                for i in range(2):
                    dve.wait_ge(unit_out, u + 4 + i - 1 + CREDIT)
                    dve.wait_ge(act_step, SA.at(f"y{i}", g))
                    SD.done(dve.tensor_tensor(y_f[:, i, :], y_f[:, i, :], ev_f[i][:], ALU.mult), f"z{i}")
                for i in range(2):
                    dve.wait_ge(act_step, SA.at(f"yh{i}", g))
                    SD.done(dve.tensor_tensor(yl_f[:, i, :], y_f[:, i, :], yh_f[:, i, :].bitcast(F32), ALU.subtract),
                            f"yl{i}")
                add_up(dve, u + 4, ev_f, SD, g)

            dve.drain()
            norm(st_n1, [(resid, n * HALF, HALF, lambda k: gain[:, 2, k:k + 1], lambda k: mod[:, 1, k, 0:1],
                          h_hi, h_lo) for n in range(2)], m_sq, m_t, m_rs)
            dve.drain()

            for g, win in enumerate(WINDOWS):
                u = g * PU + U_POOL
                SA, SD = st_pool["act"], st_pool["dve"]
                half = win // 2
                for m in range(4):
                    dve.wait_ge(unit_out, u + 1 + m + CREDIT)
                    if m == 0:
                        dve.wait_ge(c_inv, 16 * g + 16)
                    rows_n = GRID_H + win - 1
                    a, bbuf = pt[0], pt[1]
                    rv = lambda t_: t_[:, 0:rows_n * GRID_W]
                    dve.memset(a[:, 0:half * GRID_W], 0.0)
                    if win - 1 - half:
                        dve.memset(a[:, (half + GRID_H) * GRID_W:rows_n * GRID_W], 0.0)
                    dve.tensor_copy(a[:, half * GRID_W:half * GRID_W + T], u_p[:, m, :])
                    dve.drain()
                    step, left = 1, rows_n
                    while step < win:
                        left -= step
                        dve.tensor_tensor(bbuf[:, 0:left * GRID_W], a[:, 0:left * GRID_W],
                                          a[:, step * GRID_W:(step + left) * GRID_W], ALU.add)
                        dve.drain()
                        a, bbuf = bbuf, a
                        step *= 2
                    assert left == GRID_H
                    cw = GRID_W + win - 1
                    bv = bbuf[:, 0:GRID_H * cw].rearrange("p (r c) -> p r c", c=cw)
                    dve.memset(bv[:, :, 0:half], 0.0)
                    if win - 1 - half:
                        dve.memset(bv[:, :, half + GRID_W:cw], 0.0)
                    dve.tensor_copy(bv[:, :, half:half + GRID_W],
                                    a[:, 0:T].rearrange("p (r c) -> p r c", c=GRID_W))
                    dve.drain()
                    a, bbuf = bbuf, a
                    step, left = 1, cw
                    while step < win:
                        left -= step
                        av = a[:, 0:GRID_H * cw].rearrange("p (r c) -> p r c", c=cw)
                        ov = bbuf[:, 0:GRID_H * cw].rearrange("p (r c) -> p r c", c=cw)
                        dve.tensor_tensor(ov[:, :, 0:left], av[:, :, 0:left], av[:, :, step:step + left], ALU.add)
                        dve.drain()
                        a, bbuf = bbuf, a
                        step *= 2
                    av = a[:, 0:GRID_H * cw].rearrange("p (r c) -> p r c", c=cw)[:, :, 0:GRID_W]
                    dve.tensor_tensor(bbuf[:, 0:T].rearrange("p (r c) -> p r c", c=GRID_W), av,
                                      inv[:].rearrange("p (r c) -> p r c", c=GRID_W), ALU.mult)
                    dve.drain()
                    SD.done(dve.tensor_tensor(u_p[:, m, :], bbuf[:, 0:T], u_p[:, m, :], ALU.subtract), f"p{m}")
                    dve.drain()
                for m in range(4):
                    dve.wait_ge(act_step, SA.at(f"ph{m}", g))
                    SD.done(dve.tensor_tensor(yl_p[:, m, :], u_p[:, m, :], yh_p[:, m, :].bitcast(F32), ALU.subtract),
                            f"pl{m}")
                for m in range(5):
                    if m < 4:
                        dve.wait_ge(unit_out, u + 9 + m + CREDIT)
                        SD.done(dve.tensor_tensor(u_p[:, m, :], u_p[:, m, :], ev_p[m][:], ALU.mult), f"z{m}")
                    if m >= 1:
                        dve.wait_ge(act_step, SA.at(f"yh{m - 1}", g))
                        SD.done(dve.tensor_tensor(yl_g[:, m - 1, :], u_p[:, m - 1, :],
                                                  yh_g[:, m - 1, :].bitcast(F32), ALU.subtract), f"yl{m - 1}")
                add_up(dve, u + 12, ev_p, SD, g)

            dve.drain()
            norm(st_n2, [(resid, n * HALF, HALF, lambda k: vec[:, FINAL_G + k:FINAL_G + k + 1], None, None, None)
                         for n in range(2)], m_sq, m_t, m_rs)


def tables():
    t = np.arange(TF)[:, None].astype(np.float64)
    k = (RADIX * np.arange(TF)[None, :] + np.arange(RADIX)[:, None]).reshape(1, T)
    ang = 2 * np.pi * ((t * k) % T) / T
    norm = 1.0 / np.sqrt(T * DH)
    cidx = np.arange(DH)
    cang = 2 * np.pi * (np.outer(cidx, cidx) % DH) / DH
    s, q = np.arange(CHUNK)[:, None], np.arange(CHUNK)[None, :]
    mask = np.stack([np.where(s <= q, 0.0, BIG), np.where(s >= q, 0.0, BIG)], axis=1)
    inv = []
    for w in WINDOWS:
        def count(n):
            i = np.arange(n)
            return np.clip(i + w - w // 2, 0, n) - np.clip(i - w // 2, 0, n)
        inv.append(1.0 / np.outer(count(GRID_H), count(GRID_W)).reshape(-1))
    f = lambda a: np.ascontiguousarray(a, dtype=np.float32)
    return {"ident": f(np.eye(P)), "mask": f(mask), "ct": f(np.cos(ang) * norm), "ns": f(-np.sin(ang) * norm),
            "cc": f(np.cos(cang)), "cs": f(np.sin(cang)), "inv": f(np.stack(inv))}


_INS = ['x', 'c', 'ctx', 'c_ctx', 'ada_w', 'ada_b', 'norm_g', 'win_even', 'gate_b_even', 'conv_qk_even',
        'head_norm_even', 'fourier_w_even', 'wout_even', 'win_odd', 'pool_w_odd', 'pool_scale_odd', 'wout_odd',
        'final_g']
_OUT = ((1, 1024, 1024), 'float32')


def kernel(**inputs):
    import numpy as _np
    import concourse.bacc as _bacc
    from concourse import mybir as _mybir
    from concourse.bass_utils import run_bass_kernel_spmd as _run

    nc = _bacc.Bacc("TRN2", target_bir_lowering=False, num_devices=1)
    arrays, args = {}, []
    for name, a in [(n, inputs[n]) for n in _INS] + list(tables().items()):
        a = _np.ascontiguousarray(a)
        arrays[f"in_{name}_dram"] = a
        args.append(nc.dram_tensor(f"in_{name}_dram", a.shape, _mybir.dt.from_np(a.dtype), kind="ExternalInput").ap())
    args.append(nc.dram_tensor("out_0_dram", _OUT[0], _mybir.dt.from_np(_np.dtype(_OUT[1])),
                               kind="ExternalOutput").ap())
    program(nc, *args)
    r = _run(nc, [arrays], core_ids=[0])
    return r.results[0]["out_0_dram"]
```

```python
from contextlib import ExitStack

import numpy as np

import concourse.bass as bass
from concourse import mybir

F32 = mybir.dt.float32
F32R = mybir.dt.float32r
ALU = mybir.AluOpType
ACT = mybir.ActivationFunctionType

P = 128
D = 1024
KB = D // P
T = 1024
TC = 256
HALF = 512
HEADS = 4
DH = 256
GROUPS = 4
GRID_W = 64
GRID_H = T // GRID_W
WINDOWS = (2, 4, 8, 16)
EPS = 1e-6
CHUNK = 128
NCC, NCX = TC // CHUNK, T // CHUNK
NCH = NCC + NCX
BIG = 1e30
RADIX = 4
TF = T // RADIX

HEAD_UNITS = [1] * 10 + [4, 4]
FOUR_UNITS = [1] * 4 + [4, 4]
POOL_UNITS = [1] * 8 + [2, 2] + [2] * 4
EARLY = 2
CREDIT = 8
STEP_CREDIT = 96


class Steps:

    def __init__(self, sem, base, names, times=1):
        self.sem, self.base, self.names, self.times = sem, base, list(names), times
        self.index = {n: i for i, n in enumerate(self.names)}
        assert len(self.index) == len(self.names)
        self.next = 0

    def at(self, name, i=0):
        return self.base + i * len(self.names) + self.index[name] + 1

    @property
    def end(self):
        return self.base + self.times * len(self.names)

    def done(self, ins, name):
        assert self.names[self.next % len(self.names)] == name, (name, self.names[self.next % len(self.names)])
        self.next += 1
        ins.then_inc(self.sem, 1)


def nat_chunk(direction, j):
    if direction == 0:
        return j
    return NCC - 1 - j if j < NCC else NCC + NCX - 1 - (j - NCC)


def program(nc, x, c, ctx_in, c_ctx, ada_w, ada_b, norm_g, win_even, gate_b, conv_qk, head_norm, fourier_w,
            wout_even, win_odd, pool_w, pool_scale, wout_odd, final_g, tab_ident, tab_mask, tab_ct, tab_ns,
            tab_cc, tab_cs, tab_inv, out):
    stack = ExitStack()
    with stack:
        def sem(name):
            return stack.enter_context(nc.semaphore(name))

        cursor = [-(-nc.sbuf_base // 64) * 64]

        def at(name, shape, dt, offset):
            return nc.alloc_sbuf_tensor_at(name, shape, dt, offset=offset)

        def size(shape):
            return -(-int(np.prod(shape[1:])) * 4 // 32) * 32

        def fixed(name, shape, dt=F32):
            t = at(name, shape, dt, cursor[0])
            cursor[0] += size(shape)
            return t

        class Region:
            def __init__(self, start):
                self.at = start

            def __call__(self, name, shape, dt=F32):
                t = at(name, shape, dt, self.at)
                self.at += size(shape)
                assert self.at <= nc.sbuf_usable_end, (name, self.at)
                return t

        ident = fixed("ident", [P, P])
        ones = fixed("ones", [P, P])
        mask = fixed("mask", [P, 2, CHUNK])
        zero = fixed("zero", [P, 1])
        eps = fixed("eps", [P, 1])
        p_scale = fixed("p_scale", [P, 4])
        seed = fixed("seed", [P, 9])
        vec = fixed("vec", [P, 176])
        mod = fixed("mod", [P, 2, 24, 2])
        gain = fixed("gain", [P, 3, KB])
        chunk_sc = fixed("chunk_sc", [P, 8, 2, NCH])
        w_raw = [fixed(f"w_raw{i}", [P, D]) for i in range(2)]
        w_hi = [fixed(f"w_hi{i}", [P, D], F32R) for i in range(2)]
        mrow = [at(f"mrow{i}", [2, HALF], F32, cursor[0] + i * size([P, D])) for i in range(2)]
        w_lo = [fixed(f"w_lo{i}", [P, D], F32R) for i in range(2)]
        h_hi = fixed("h_hi", [P, KB, T], F32R)
        h_lo = fixed("h_lo", [P, KB, T], F32R)
        resid = fixed("resid", [P, KB, T])
        arena = cursor[0]

        ADA_B, NORM_G, FINAL_G, HEAD_G, POOL_S, C_VEC, CONV = 0, 48, 64, 72, 80, 96, P

        r = Region(arena)
        hc_hi = r("hc_hi", [P, KB, TC], F32R)
        hc_lo = r("hc_lo", [P, KB, TC], F32R)
        cols = r("cols", [P, 3, NCH, 8])
        after_ctx = r.at
        g_in = r("g_in", [P, KB, 16])
        g_bias = r("g_bias", [P, 1])
        c_silu = r("c_silu", [P, KB, 2])
        before_tok = r.at
        tok = [r(f"tok{i}", [P, D]) for i in range(2)]
        vrow = r("vrow", [P, 2, P])
        r.at = max(r.at, before_tok + 3 * size([P, KB, P]))
        after_tok = r.at
        xc_t = r("xc_t", [P, KB, TC])
        n_sq = [r(f"n_sq{i}", [P, HALF]) for i in range(2)]
        n_t = [r(f"n_t{i}", [P, HALF]) for i in range(3)]
        n_rs = r("n_rs", [P, HALF])
        ada_buf = [r(f"ada_buf{i}", [P, KB, HALF]) for i in range(2)]
        ada_end = r.at
        r = Region(before_tok)
        g_w = r("g_w", [P, KB, P])
        g_wh = r("g_wh", [P, KB, P], F32R)
        g_wl = r("g_wl", [P, KB, P], F32R)
        r = Region(after_tok)
        g_i = r("g_i", [64, TC + T])
        g_f = r("g_f", [64, TC + T])
        g_e = r("g_e", [64, TC + T])
        g_b = r("g_b", [64, TC + T])
        g_g = r("g_g", [64, TC + T])
        g_d = r("g_d", [64, TC + T])
        g_s = r("g_s", [64, TC + T])
        g_nat = at("g_nat", [64, TC + T], F32, r.at - 2 * size([64, TC + T]))
        g_small = r("g_small", [64, 3, NCH])
        assert r.at <= ada_end - size([P, KB, HALF])
        r = Region(after_ctx)
        q_t = r("q_t", [P, 2, T])
        kk = r.at
        k_t = r("k_t", [P, 2, TC + T])
        k_tok = r("k_tok", [P, NCH, DH])
        v_tok = r("v_tok", [P, NCH, DH + 1])
        cst = r("cst", [P, 2, 2, DH + 1])
        gg = r.at
        g_bc = r("g_bc", [P, 2, T])
        hh = r.at
        h_tok = r("h_tok", [P, NCX, DH])
        kw = [r(f"kw{d}", [P, DH]) for d in range(2)]
        qi = [r(f"qi{d}", [P, 2, CHUNK]) for d in range(2)]
        pr = [r(f"pr{d}", [P, CHUNK]) for d in range(2)]
        ee = [r(f"ee{d}", [P, CHUNK]) for d in range(2)]
        it = [r(f"it{d}", [P, CHUNK]) for d in range(2)]
        dn = r("dn", [P, 2, 4])
        r = Region(max(r.at, hh + size([P, T + 2]) + size([P, TC + 2]) + 2 * size([P, TC + T])))
        h_cols = r("h_cols", [P, 3, NCH, 2])
        h_sc = r("h_sc", [P, 2, 2, NCH])
        r = Region(kk)
        yh2 = r("yh2", [P, 2, T], F32R)
        yl2 = r("yl2", [P, 2, T], F32R)
        r = Region(gg)
        ev_a = [r(f"ev_a{i}", [P, T]) for i in range(2)]
        r = Region(hh)
        cb = r("cb", [P, T + 2])
        cbc = r("cbc", [P, TC + 2])
        cv = r("cv", [P, TC + T])
        v_raw = [r("v_raw0", [P, TC + T]), at("v_raw1", [P, TC + T], F32, hh)]
        assert size([P, TC + T]) <= size([P, T + 2]) + size([P, TC + 2])
        r = Region(arena)
        pq = r("pq", [P, 2, RADIX, 2 * DH])
        fd = r("fd", [P, 2, RADIX, TF])
        f_tmp = r("f_tmp", [P, 2, 2, TF])
        f_b = r("f_b", [P, 2 * DH])
        ct = r("ct", [P, 2, T])
        ns = r("ns", [P, 2, T])
        cfsf = r("cfsf", [P, 2, 2 * DH])
        ccs = r("ccs", [P, 2, 2, DH])
        fw = r("fw", [P, 2, DH])
        ev_f = [r(f"ev_f{i}", [P, T]) for i in range(2)]
        yh_f = r("yh_f", [P, 2, T], F32R)
        yl_f = r("yl_f", [P, 2, T], F32R)
        r = Region(arena)
        u_f = r("u_f", [P, 2, T])
        r = Region(arena + size([P, 2, RADIX, 2 * DH]))
        y_f = r("y_f", [P, 2, T])
        r = Region(arena)
        u_p = r("u_p", [P, 4, T])
        yh_p = r("yh_p", [P, 4, T], F32R)
        yl_p = r("yl_p", [P, 4, T], F32R)
        pt = [r(f"pt{i}", [P, (GRID_H + max(WINDOWS) - 1) * GRID_W]) for i in range(2)]
        inv = r("inv", [P, T])
        ev_p = [r(f"ev_p{i}", [P, T]) for i in range(4)]
        yh_g = at("yh_g", [P, 4, T], F32R, arena + 3 * size([P, 4, T]))
        yl_g = at("yl_g", [P, 4, T], F32R, arena)
        r = Region(arena)
        m_sq = [r(f"m_sq{i}", [P, HALF]) for i in range(2)]
        m_t = [r(f"m_t{i}", [P, HALF]) for i in range(3)]
        m_rs = r("m_rs", [P, HALF])
        o_tok = [r(f"o_tok{i}", [P, D]) for i in range(2)]

        ps = [stack.enter_context(nc.psum_tensor(f"ps{i}", [P, 2, HALF], F32)) for i in range(4)]

        g_dram = nc.dram_tensor("g_scratch", [8, TC + T], F32)
        s_dram = nc.dram_tensor("s_scratch", [8, 2 * NCH], F32)

        w_landed = [sem("w_landed0"), sem("w_landed1")]
        w_high = sem("w_high")
        w_ready = sem("w_ready")
        unit_done = sem("unit_done")
        unit_out = sem("unit_out")
        ctx_out = sem("ctx_out")
        pe_step, act_step, dve_step = sem("pe_step"), sem("act_step"), sem("dve_step")
        rows_clear = sem("rows_clear")
        c_const = sem("c_const")
        c_vec = sem("c_vec")
        c_tok = [sem("c_tok0"), sem("c_tok1")]
        c_ada = [sem("c_ada0"), sem("c_ada1")]
        ada_used = sem("ada_used")
        ada_row = sem("ada_row")
        tile_turned = sem("tile_turned")
        tile_out = sem("tile_out")
        ada_col = sem("ada_col")
        c_gate = sem("c_gate")
        c_rows = sem("c_rows")
        c_bc = sem("c_bc")
        c_gbc = sem("c_gbc")
        c_four = sem("c_four")
        c_fw = sem("c_fw")
        c_inv = sem("c_inv")
        c_out = [sem("c_out0"), sem("c_out1")]

        DIRS = (0, 1)
        pos = {"pe": STEP_CREDIT, "act": STEP_CREDIT, "dve": STEP_CREDIT}
        sems = {"pe": pe_step, "act": act_step, "dve": dve_step}

        def stage(names, times=1):
            out_ = {}
            for e in ("pe", "act", "dve"):
                s = Steps(sems[e], pos[e], names.get(e, []), times)
                pos[e] = s.end
                out_[e] = s
            return out_

        NT, NTC = T // P, TC // P
        st_vec = stage({"pe": ["vecT"], "act": ["silu_c"], "dve": ["vec"]})

        def norm_stage(parts, last=False):
            a = [f"sq0{k}" for k in range(KB)] + ["std0"]
            for n in range(parts):
                for k in range(KB):
                    a += ([] if last else [f"hi{n}{k}"]) + ([f"sq{n + 1}{k}"] if n + 1 < parts else [])
                if n + 1 < parts:
                    a.append(f"std{n + 1}")
            v = [f"add{k}" for k in range(1, KB)]
            for n in range(parts):
                v.append(f"rs{n}")
                for k in range(KB):
                    v.append(f"t{n}{k}")
                    if k >= 1 and not last:
                        v.append(f"lo{n}{k - 1}")
                if not last:
                    v.append(f"lo{n}{KB - 1}")
            return stage({"pe": ["sum0"] + [f"s{n}{k}" for n in range(1, parts) for k in range(KB)],
                          "act": a, "dve": v})

        st_n0 = norm_stage(3)
        st_gate = stage({"pe": ["gates", "colsA", "colsW", "colsE"],
                         "act": ["ln", "w", "em"],
                         "dve": ["f", "G", "g_nat", "a_nat", "w_in", "w_nat", "e_in", "e_nat", "cols"]})

        head_act, head_dve, head_pe = [], [], []
        for n in ("q0", "q1", "k0", "k1"):
            head_dve.append(f"conv_{n}")
            head_act.append(f"silu_{n}")
        for n in ("k", "v"):
            head_pe += [f"{n}T0", f"{n}T1"]
            head_dve += [f"{n}tok0", f"{n}tok1"]
        SEQ = [(j, d) for j in range(NCH) for d in DIRS]
        for n, (j, d) in enumerate(SEQ):
            following = SEQ[n + 1] if n + 1 < len(SEQ) else (0, 0)
            if following[0] >= NCC:
                head_pe.append("S%d%d" % following)
                head_dve.append("E%d%d" % following)
            if j >= NCC:
                head_dve += [f"P{j}{d}", f"Q{j}{d}"]
                head_pe.append(f"N{j}{d}")
            if j < NCH - 1:
                head_act.append(f"kw{j}{d}")
                head_pe.append(f"U{j}{d}")
            if following[0] >= NCC:
                head_act += ["D%d%d" % following, "I%d%d" % following]
            for pj, pd in (SEQ[n - 1:n] if n else []) + ([(j, d)] if n == len(SEQ) - 1 else []):
                if pj >= NCC:
                    head_dve.append(f"h{pj}{pd}")
                if pj < NCH - 1:
                    head_dve.append(f"C{pj}{pd}")
        head_pe += ["hT0", "hT1"]
        head_dve += ["hf0", "hf1", "o0", "o1"]
        head_act += ["sq0", "sq1", "hstd"]
        head_pe += ["hsum", "half"]
        head_dve += ["hrs", "z0", "yl0", "z1a", "yl1a", "z1b", "yl1b"] + [f"acc{m}" for m in range(KB)]
        head_act += ["yh0", "silu_a", "yh1a", "yh1b"]
        st_head = stage({"pe": head_pe, "act": head_act, "dve": head_dve}, HEADS)

        st_four = stage({
            "pe": ["cf", "V0", "V1", "V2", "V3", "V4", "V5", "V6", "V7", "Y0", "Y1", "half"],
            "act": ["cf", "y0", "y1", "yh0", "silu_a", "yh1a", "yh1b"],
            "dve": ["fold", "V0", "V1", "V2", "V3", "V4", "V5", "V6", "V7", "z0", "yl0", "z1a", "yl1a", "z1b", "yl1b"]
            + [f"acc{m}" for m in range(KB)]}, GROUPS)
        st_n1 = norm_stage(2)
        st_pool = stage({
            "pe": ["half"],
            "act": [f"ph{m}" for m in range(4)] + ["yh0", "yh1", "scale_a", "yh2", "yh3a", "yh3b"],
            "dve": [f"p{m}" for m in range(4)] + [f"pl{m}" for m in range(4)]
            + ["z0", "z1", "yl0", "z2", "yl1", "z3a", "yl2", "z3b", "yl3a", "yl3b"]
            + [f"acc{m}" for m in range(KB)]}, GROUPS)
        st_n2 = norm_stage(2, last=True)
        st_end = stage({"pe": ["t0", "t1"], "act": ["c0", "c1"]}, NT // 2)

        HU, FU, PU = sum(HEAD_UNITS), sum(FOUR_UNITS), sum(POOL_UNITS)
        U_FOUR = HEADS * HU
        U_POOL = U_FOUR + GROUPS * FU
        B_FOUR = HEADS * len(HEAD_UNITS)
        B_POOL = B_FOUR + GROUPS * len(FOUR_UNITS)

        we = win_even[0].rearrange("(k p) m -> p k m", p=P)
        wo = win_odd[0].rearrange("(k p) m -> p k m", p=P)
        woe = wout_even[0].rearrange("(k p) m -> p k m", p=P)
        woo = wout_odd[0].rearrange("(k p) m -> p k m", p=P)
        pw = pool_w[0].rearrange("g (k p) m -> p (g k) m", p=P)
        ada_v = ada_w.rearrange("l (k p) (b m) -> p l k b m", p=P, m=512)

        def bcast(dram, offset, n):
            a = dram[:].rearrange("a b -> (a b)")
            return a[bass.ds(offset, n)].partition_broadcast(P)

        def pool_counts(g):
            return tab_inv.rearrange("a b -> (a b)")[bass.ds(g * T, T)].partition_broadcast(P)

        def accumulate(act, u, ev, layer, SD, i, last=1):
            for m in range(KB):
                act.wait_ge(unit_done, u + m + 1 + CREDIT)
                act.wait_ge(dve_step, SD.at(f"acc{m - 2}" if m >= 2 else f"z{m}" if m < last else f"z{m}b", i))
                act.activation(ev[m % 2][:], ps[m % 2][:].rearrange("p a b -> p (a b)"), ACT.Identity,
                               scale=mod[:, layer, 16 + m, 0:1], bias=zero[:]).then_inc(unit_out, 1)

        def gather(dve, dst, i):
            for n, bank in enumerate((ps[2][:, 1, :], ps[3][:, 0, :], ps[3][:, 1, :])):
                cnt = min(4, NCH - 4 * n)
                ins = dve.tensor_copy(dst[:, 4 * n:4 * n + cnt, i * P:(i + 1) * P],
                                      bank[:, 0:cnt * P].rearrange("p (c f) -> p c f", f=P))
            return ins

        def add_up(dve, u, ev, SD, i):
            for m in range(KB):
                dve.wait_ge(unit_out, u + m + 1 + CREDIT)
                SD.done(dve.tensor_tensor(resid[:, m, :], resid[:, m, :], ev[m % 2][:], ALU.add), f"acc{m}")

        block = stack.enter_context(nc.Block())

        @block.sync
        def _(sp):
            sp.dma_start(ident[:], tab_ident).then_inc(c_const, 16)
            sp.dma_start(mask[:], tab_mask).then_inc(c_const, 16)
            sp.wait_ge(rows_clear, 1)
            rows = lambda a: a.rearrange("(k p) -> k p", p=P)
            for t, a0, n, src in ((0, ADA_B, 48, ada_b.rearrange("l (k p) -> (l k) p", p=P)),
                                  (0, NORM_G, 16, norm_g.rearrange("l (k p) -> (l k) p", p=P)),
                                  (0, FINAL_G, 8, rows(final_g)), (0, HEAD_G, 8, rows(head_norm[0])),
                                  (0, POOL_S, 16, rows(pool_scale[0])),
                                  (0, C_VEC, 8, rows(c[0])), (0, C_VEC + 8, 8, rows(c_ctx)),
                                  (1, 0, 48, conv_qk[0].rearrange("j (k p) -> (j k) p", p=P))):
                sp.dma_start(vrow[a0:a0 + n, t, :], src).then_inc(c_vec, 16)
            def ada(lay, i):
                for j in range(2):
                    sp.wait_ge(ada_used, 6 * lay + 2 * i + j - 1 + EARLY)
                    sp.dma_start(ada_buf[j][:], ada_v[:, lay, :, bass.ds(2 * i + j, 1), :].rearrange(
                        "p k b m -> p k (b m)")).then_inc(c_ada[j], 16)

            def tokens(i):
                for j in range(2):
                    sp.wait_ge(tile_turned, 2 * i + j - 1 + EARLY)
                    sp.dma_start(tok[j][:], x[0, bass.ds((2 * i + j) * P, P), :]).then_inc(c_tok[j], 16)

            with sp.Fori(0, 2) as i:
                ada(0, i)
                tokens(i)
            ada(0, 2)
            tokens(2)
            tokens(3)
            sp.dma_start(g_in[:], we[:, :, 7 * D:7 * D + 16]).then_inc(c_gate, 16)
            for kind in range(2):
                for d in range(2):
                    row = 2 * d + kind
                    sp.dma_start(g_bias[64 * kind + 32 * d:64 * kind + 32 * d + 4, 0:1],
                                 gate_b[0, 4 * row:4 * row + 4].rearrange("(r o) -> r o", o=1)).then_inc(c_gate, 16)
            for j in range(2):
                sp.wait_ge(tile_turned, NT + j - 1 + EARLY)
                sp.dma_start(tok[j][:], ctx_in[0, j * P:(j + 1) * P, :]).then_inc(c_tok[j], 16)
            with sp.Fori(0, 3) as i:
                ada(1, i)
            def load(b, j, src, k):
                sp.wait_ge(w_ready, b - 1 + CREDIT)
                sp.dma_start(w_raw[j % 2][:].rearrange("p (k m) -> p k m", k=k), src).then_inc(w_landed[j % 2], 16)

            with sp.Fori(0, HEADS) as h:
                b = h * len(HEAD_UNITS)
                for n, part in enumerate((0, 1, 2, 3, 4)):
                    for i in range(2):
                        load(b + 2 * n + i, i, we[:, :, bass.ds(h * DH + part * D + i * P, P)], KB)
                for i in range(2):
                    load(b + 10 + i, i, woe[:, bass.ds(2 * h, 2), i * 512:(i + 1) * 512], 2)
            with sp.Fori(0, GROUPS) as g:
                b = g * len(FOUR_UNITS) + B_FOUR
                for n, part in enumerate((5, 6)):
                    for i in range(2):
                        load(b + 2 * n + i, i, we[:, :, bass.ds(g * DH + part * D + i * P, P)], KB)
                    if n == 0:
                        sp.wait_ge(pe_step, st_four["pe"].at("cf", g - 1))
                        sp.dma_start(fw[:], fourier_w[0, bass.ds(g, 1)].rearrange("g (k p) m -> p (g k) m", p=P)
                                     ).then_inc(c_fw, 16)
                for i in range(2):
                    load(b + 4 + i, i, woe[:, bass.ds(2 * g + 8, 2), i * 512:(i + 1) * 512], 2)
            with sp.Fori(0, GROUPS) as g:
                b = g * len(POOL_UNITS) + B_POOL
                for i in range(4):
                    load(b + i, i, wo[:, :, bass.ds(g * 512 + i * P, P)], KB)
                for i in range(4):
                    load(b + 4 + i, i, wo[:, :, bass.ds(g * 512 + 2 * D + i * P, P)], KB)
                for i in range(2):
                    load(b + 8 + i, i, pw[:, bass.ds(4 * g, 4), i * 256:(i + 1) * 256], 4)
                for i in range(4):
                    load(b + 10 + i, i, woo[:, bass.ds(4 * g, 4), i * 256:(i + 1) * 256], 4)
            for i in range(NT // 2):
                for j in range(2):
                    sp.wait_ge(act_step, st_end["act"].at(f"c{j}", i))
                    sp.dma_start(out[0, (2 * i + j) * P:(2 * i + j + 1) * P, :], o_tok[j][:]).then_inc(c_out[j], 16)
            for j in range(2):
                sp.wait_ge(c_out[j], 16 * (NT // 2))

        @block.gpsimd
        def _(pool):
            pool.memset(ones[:], 1.0).then_inc(act_step, STEP_CREDIT)
            pool.memset(eps[:], EPS).then_inc(dve_step, STEP_CREDIT)
            pool.memset(zero[:], 0.0).then_inc(unit_done, CREDIT)
            for n, (counter, start) in enumerate(((w_ready, CREDIT), (unit_out, CREDIT), (pe_step, STEP_CREDIT),
                                                  (ctx_out, 1), (ada_used, EARLY), (ada_row, EARLY),
                                                  (ada_col, EARLY), (tile_turned, EARLY), (tile_out, EARLY))):
                pool.memset(seed[:, n:n + 1], 0.0).then_inc(counter, start)
            pool.drain()

            def split(base, i, units):
                ubase, bbase = base
                per, nb = sum(units), len(units)
                for j in range(nb):
                    before = sum(units[:j - 1]) if j >= 1 else -units[-1]
                    s = j % 2
                    pool.wait_ge(w_landed[s], 16 * (i * (nb // 2) + (bbase + j) // 2 + 1))
                    pool.wait_ge(unit_done, i * per + ubase + before + CREDIT)
                    pool.tensor_tensor(w_hi[s][:], w_raw[s][:], zero[:].to_broadcast([P, D]), ALU.add
                                       ).then_inc(w_high, 1)
                    pool.wait_ge(w_high, i * nb + bbase + j + 1)
                    pool.tensor_tensor(w_lo[s][:], w_raw[s][:], w_hi[s][:].bitcast(F32), ALU.subtract
                                       ).then_inc(w_ready, 1)

            pool.wait_ge(ada_col, 12 + EARLY)
            with pool.Fori(0, HEADS) as i:
                split((0, 0), i, HEAD_UNITS)
            with pool.Fori(0, GROUPS) as i:
                split((U_FOUR, B_FOUR), i, FOUR_UNITS)
            with pool.Fori(0, GROUPS) as i:
                split((U_POOL, B_POOL), i, POOL_UNITS)

        @block.tensor
        def _(pe):
            def three(dst, ah, al, bh, bl, start, stop):
                pe.matmul(dst, ah, bh, start=start, stop=False)
                pe.matmul(dst, ah, bl, start=False, stop=False)
                return pe.matmul(dst, al, bh, start=False, stop=stop)

            pe.wait_ge(c_const, 32)
            pe.wait_ge(c_vec, 8 * 16)
            pe.transpose(ps[0][:, 0, 0:P], vrow[:, 0, :], ident[:])
            st_vec["pe"].done(pe.transpose(ps[0][:, 0, P:2 * P], vrow[:, 1, :], ident[:]), "vecT")

            def tokens(i):
                for j in range(2):
                    pe.wait_ge(c_tok[j], 16 * i + 16)
                    pe.wait_ge(tile_out, 2 * i + j - 1 + EARLY)
                    for k in range(KB):
                        m = pe.transpose(ps[2 + j][:, k // 4, (k % 4) * P:(k % 4 + 1) * P],
                                         tok[j][:, k * P:(k + 1) * P], ident[:])
                    m.then_inc(tile_turned, 1)

            def sums(i, j, bank=None, free=True):
                pe.wait_ge(c_ada[j], 16 * i + 16)
                if free:
                    pe.wait_ge(ada_row, 2 * i + j - 1 + EARLY)
                for k in range(KB):
                    m = pe.matmul((ps[0][:, j] if bank is None else bank)[0:2, :], c_silu[:, k, :],
                                  ada_buf[j][:, k, :], start=(k == 0), stop=(k == KB - 1))
                m.then_inc(ada_used, 1)

            def columns(lay, i, j):
                pe.wait_ge(ada_row, 2 * i + j + 1 + EARLY)
                for n in range(4):
                    m = pe.matmul(ps[1][:, lay, bass.ds((2 * i + j - 6 * lay) * 8 + 2 * n, 2)],
                                  mrow[j][:, n * P:(n + 1) * P], ident[0:2, 0:2], start=True, stop=True)
                m.then_inc(ada_col, 1)

            pe.wait_ge(act_step, st_vec["act"].at("silu_c"))
            with pe.Fori(0, 2) as i:
                sums(i, 0)
                sums(i, 1)
                columns(0, i, 0)
                tokens(i)
                columns(0, i, 1)
            sums(2, 0)
            sums(2, 1)

            def between(n):
                if n == 0:
                    columns(0, 2, 0)
                    columns(0, 2, 1)
                    pe.wait_ge(act_step, st_n0["act"].at("std0"))
                    for i in range(2, (NT + NTC) // 2):
                        tokens(i)
                elif n == 1:
                    sums(3, 0)
                    sums(3, 1)
                elif n == 2:
                    columns(1, 3, 0)
                    columns(1, 3, 1)
                    sums(4, 0)
                    sums(4, 1)
                    sums(5, 0, bank=ps[3][:, 1], free=False)

            def norm(st, widths, sq, total, between=None):
                for n, width in enumerate(widths):
                    bank = ps[2 + n // 2][:, n % 2, 0:width]
                    if n == 0:
                        pe.wait_ge(dve_step, st["dve"].at(f"add{KB - 1}"))
                        st["pe"].done(pe.matmul(bank, ones[:], total[:, 0:width], start=True, stop=True), "sum0")
                    else:
                        for k in range(KB):
                            pe.wait_ge(act_step, st["act"].at(f"sq{n}{k}"))
                            st["pe"].done(pe.matmul(bank, ones[:], sq[k % 2][:, 0:width],
                                                    start=(k == 0), stop=(k == KB - 1)), f"s{n}{k}")
                    if between:
                        between(n)

            norm(st_n0, (HALF, HALF, TC), n_sq, n_t[0], between)

            pe.wait_ge(dve_step, st_n0["dve"].end)
            for half in range(2):
                for k in range(KB):
                    s = slice(half * HALF, (half + 1) * HALF)
                    three(ps[2][:, half, :], g_wh[:, k, :], g_wl[:, k, :], h_hi[:, k, s], h_lo[:, k, s],
                          k == 0, k == KB - 1)
            for k in range(KB):
                m = three(ps[3][:, 0, 0:TC], g_wh[:, k, :], g_wl[:, k, :], hc_hi[:, k, :], hc_lo[:, k, :],
                          k == 0, k == KB - 1)
            st_gate["pe"].done(m, "gates")
            columns(1, 4, 0)
            columns(1, 4, 1)
            sums(5, 1)
            columns(1, 5, 0)
            columns(1, 5, 1)
            for n, (name, src, want) in enumerate((("colsA", g_nat, "a_nat"), ("colsW", g_s, "w_nat"),
                                                   ("colsE", g_e, "e_nat"))):
                pe.wait_ge(dve_step, st_gate["dve"].at(want))
                for ch in range(NCH):
                    bank = (ps[0], ps[2], ps[3])[n]
                    m = pe.transpose(bank[:, ch // 8, (ch % 8) * 64:(ch % 8) * 64 + 64],
                                     src[:, ch * CHUNK:(ch + 1) * CHUNK], ident[0:64, 0:64])
                st_gate["pe"].done(m, name)

            def begin(b):
                pe.wait_ge(w_ready, b + 1 + CREDIT)

            def unit(s, u, lhs, rhs, ks, ready=None, after_half=None):
                pe.wait_ge(unit_out, u - 1 + CREDIT)
                bank = ps[s]
                for half in range(2):
                    if ready:
                        pe.wait_ge(dve_step, ready[half])
                    for k in ks:
                        m = three(bank[:, half, :], *lhs(k), rhs[0][:, k, half * HALF:(half + 1) * HALF],
                                  rhs[1][:, k, half * HALF:(half + 1) * HALF], k == ks[0], k == ks[-1])
                    if half == 0 and after_half:
                        after_half(m)
                m.then_inc(unit_done, 1)

            def wide(s, m0, width):
                return lambda k: (w_hi[s][:, k * width + m0:k * width + m0 + P],
                                  w_lo[s][:, k * width + m0:k * width + m0 + P])

            pe.wait_ge(dve_step, st_gate["dve"].end)
            with pe.Fori(0, HEADS) as h:
                b, u = h * len(HEAD_UNITS), h * HU
                SA, SD, SP_ = st_head["act"], st_head["dve"], st_head["pe"]

                def project(n, context=None, after_half=None):
                    begin(b + n)
                    if context is not None:
                        pe.wait_ge(ctx_out, h * 4 + context + 1)
                        for k in range(KB):
                            three(ps[2][:, 0, 0:TC], *wide(n % 2, 0, P)(k), hc_hi[:, k, :], hc_lo[:, k, :],
                                  k == 0, k == KB - 1)
                    unit(n % 2, u + n, wide(n % 2, 0, P), (h_hi, h_lo), range(KB), after_half=after_half)

                pe.wait_ge(dve_step, SD.at("hrs", h - 1))
                project(0)
                project(1)
                project(2, 0)
                project(3, 1)
                project(4, 2)

                def turn(src, name):
                    for ch in range(NCH):
                        col = ch * P
                        bank = (ps[2][:, 1, :], ps[3][:, 0, :], ps[3][:, 1, :])[col // HALF]
                        m = pe.transpose(bank[:, col % HALF:col % HALF + P], src[:, ch * P:(ch + 1) * P], ident[:])
                    SP_.done(m, name)

                def second_keys(_):
                    pe.wait_ge(act_step, SA.at("silu_k1", h))
                    pe.wait_ge(dve_step, SD.at("ktok0", h))
                    turn(k_t[:, 1, :], "kT1")

                pe.wait_ge(act_step, SA.at("silu_k0", h))
                turn(k_t[:, 0, :], "kT0")
                project(5, 3, after_half=second_keys)
                pe.wait_ge(ctx_out, h * 4 + 4)
                pe.wait_ge(unit_out, u + 5 + CREDIT)
                pe.wait_ge(dve_step, SD.at("ktok1", h))
                turn(v_raw[0][:], "vT0")
                pe.wait_ge(ctx_out, h * 4 + 5)
                pe.wait_ge(unit_out, u + 6 + CREDIT)
                pe.wait_ge(dve_step, SD.at("vtok0", h))
                turn(v_raw[1][:], "vT1")
                pe.wait_ge(dve_step, SD.at("vtok1", h))

                def scores(j, d):
                    n = nat_chunk(d, j)
                    t = (n - NCC) * CHUNK
                    if j > NCC:
                        pe.wait_ge(dve_step, SD.at(f"P{j - 1}{d}", h))
                    else:
                        pe.wait_ge(unit_out, u + 6 + CREDIT)
                    for i in range(2):
                        m = pe.matmul(ps[0][:, d, 0:CHUNK], k_t[:, i, n * CHUNK:(n + 1) * CHUNK],
                                      q_t[:, i, t:t + CHUNK], start=(i == 0), stop=(i == 1))
                    SP_.done(m, f"S{j}{d}")

                for s, (j, d) in enumerate(SEQ):
                    if s + 1 < len(SEQ) and SEQ[s + 1][0] >= NCC:
                        scores(*SEQ[s + 1])
                    n = nat_chunk(d, j)
                    if j >= NCC:
                        n_b = ps[1][:, d, 0:DH + 1]
                        pe.wait_ge(dve_step, SD.at(f"Q{j}{d}", h))
                        pe.matmul(n_b, pr[d][:], v_tok[:, n, :], start=True, stop=False)
                        pe.matmul(n_b, qi[d][:, 0, :], cst[:, d, 0, :], start=False, stop=False)
                        SP_.done(pe.matmul(n_b, qi[d][:, 1, :], cst[:, d, 1, :], start=False, stop=True),
                                 f"N{j}{d}")
                    if j < NCH - 1:
                        pe.wait_ge(act_step, SA.at(f"kw{j}{d}", h))
                        if j > 0:
                            pe.wait_ge(dve_step, SD.at(f"C{j - 1}{d}", h))
                        for i in range(2):
                            m = pe.matmul(ps[2 + d][:, i, 0:DH + 1], kw[d][:, i * P:(i + 1) * P], v_tok[:, n, :],
                                          start=True, stop=True)
                        SP_.done(m, f"U{j}{d}")
                project(6)
                for i in range(2):
                    pe.wait_ge(dve_step, SD.at(f"h{NCH - 1}1", h))
                    for n in range(NCX):
                        m = pe.transpose(ps[2 + i][:, n // 4, (n % 4) * P:(n % 4 + 1) * P],
                                         h_tok[:, n, i * P:(i + 1) * P], ident[:])
                    SP_.done(m, f"hT{i}")
                project(7)

                def sum_squares(_):
                    for i in range(2):
                        pe.wait_ge(act_step, SA.at(f"sq{i}", h))
                    for half in range(2):
                        for i in range(2):
                            m = pe.matmul(ps[2][:, half, :], ones[:], k_t[:, i, half * HALF:(half + 1) * HALF],
                                          start=(i == 0), stop=(i == 1))
                    SP_.done(m, "hsum")

                project(8, after_half=sum_squares)
                project(9, after_half=lambda m: SP_.done(m, "half"))
                for n in range(2):
                    begin(b + 10 + n)
                    for m4 in range(4):
                        unit(m4 % 2, u + 10 + 4 * n + m4, wide(n, m4 * P, 512), (yh2, yl2), range(2),
                             ready=[SD.at(f"yl1{x}", h) for x in "ab"] if n == m4 == 0 else None)

            with pe.Fori(0, GROUPS) as g:
                b, u = g * len(FOUR_UNITS) + B_FOUR, g * FU + U_FOUR
                SA, SD, SP_ = st_four["act"], st_four["dve"], st_four["pe"]
                for n in range(2):
                    begin(b + n)
                    unit(n, u + n, wide(n, 0, P), (h_hi, h_lo), range(KB))
                pe.wait_ge(c_fw, 16 * g + 16)
                pe.wait_ge(c_four, 64)
                pe.wait_ge(act_step, SA.at("y1", g - 1))
                for f in range(2):
                    for i in range(2):
                        for k in range(2):
                            m = pe.matmul(ps[2][:, i, f * DH:(f + 1) * DH], ccs[:, f, k, i * P:(i + 1) * P],
                                          fw[:, k, :], start=(k == 0), stop=(k == 1))
                SP_.done(m, "cf")
                begin(b + 2)
                unit(0, u + 2, wide(0, 0, P), (h_hi, h_lo), range(KB))
                pe.wait_ge(dve_step, SD.at("fold", g))
                pe.wait_ge(act_step, SA.at("cf", g))
                for n, (arr, tb) in enumerate(((0, 0), (0, 1), (2, 0), (2, 1), (3, 0), (1, 0), (3, 1), (1, 1))):
                    bank = ps[2 + (n % 4) // 2][:, n % 2, :]
                    if n >= 4:
                        pe.wait_ge(dve_step, SD.at(f"V{n - 4}", g))
                    for ch in range(2):
                        m = pe.matmul(bank, fd[:, ch, arr, tb * P:(tb + 1) * P], cfsf[:, ch, :],
                                      start=(ch == 0), stop=(ch == 1))
                    SP_.done(m, f"V{n}")
                for i in range(2):
                    pe.wait_ge(dve_step, SD.at("V7", g))
                    for rr in range(RADIX):
                        dst = ps[2 + i][:, rr // 2, (rr % 2) * TF:(rr % 2 + 1) * TF]
                        for tb in range(2):
                            for z, tab in ((0, ct), (1, ns)):
                                m = pe.matmul(dst, pq[:, tb, rr, z * DH + i * P:z * DH + (i + 1) * P],
                                              tab[:, tb, rr * TF:(rr + 1) * TF], start=(tb == 0 and z == 0),
                                              stop=(tb == 1 and z == 1))
                    SP_.done(m, f"Y{i}")
                begin(b + 3)
                unit(1, u + 3, wide(1, 0, P), (h_hi, h_lo), range(KB), after_half=lambda m: SP_.done(m, "half"))
                for n in range(2):
                    begin(b + 4 + n)
                    for m4 in range(4):
                        unit(m4 % 2, u + 4 + 4 * n + m4, wide(n, m4 * P, 512), (yh_f, yl_f), range(2),
                             ready=[SD.at(f"yl1{x}", g) for x in "ab"] if n == m4 == 0 else None)

            norm(st_n1, (HALF, HALF), m_sq, m_t[0])

            with pe.Fori(0, GROUPS) as g:
                b, u = g * len(POOL_UNITS) + B_POOL, g * PU + U_POOL
                SA, SD = st_pool["act"], st_pool["dve"]
                for n in range(8):
                    begin(b + n)
                    unit(n % 2, u + n, wide(n % 2, 0, P), (h_hi, h_lo), range(KB),
                         ready=[st_n1["dve"].at(f"lo{half}{KB - 1}") for half in range(2)] if n == 0 else None)
                for n in range(2):
                    begin(b + 8 + n)
                    if n == 0:
                        pe.wait_ge(dve_step, SD.at("pl3", g))
                    for m2 in range(2):
                        unit(m2, u + 8 + 2 * n + m2, wide(n, m2 * P, 256), (yh_p, yl_p), range(4),
                             after_half=(lambda m: st_pool["pe"].done(m, "half")) if n == m2 == 1 else None)
                for n in range(4):
                    begin(b + 10 + n)
                    for m2 in range(2):
                        unit(m2, u + 12 + 2 * n + m2, wide(n % 2, m2 * P, 256), (yh_g, yl_g), range(4),
                             ready=[SD.at(f"yl3{x}", g) for x in "ab"] if n == m2 == 0 else None)

            norm(st_n2, (HALF, HALF), m_sq, m_t[0])
            for i in range(NT // 2):
                for j in range(2):
                    pe.wait_ge(dve_step, st_n2["dve"].at(f"t{i // (NT // 4)}{KB - 1}"))
                    pe.wait_ge(act_step, st_end["act"].at(f"c{j}", i - 1))
                    for k in range(KB):
                        m = pe.transpose(ps[j][:, k // 4, (k % 4) * P:(k % 4 + 1) * P],
                                         resid[:, k, (2 * i + j) * P:(2 * i + j + 1) * P], ident[:])
                    st_end["pe"].done(m, f"t{j}")

        @block.scalar
        def _(act):
            def flat(bank):
                return bank[:].rearrange("p a b -> p (a b)")

            act.wait_ge(dve_step, st_vec["dve"].at("vec"))
            st_vec["act"].done(act.activation(c_silu[:].rearrange("p k s -> p s k"),
                                              vec[:, C_VEC:C_VEC + 16].rearrange("p (s k) -> p s k", s=2),
                                              ACT.Silu), "silu_c")
            def tokens(i):
                for j in range(2):
                    act.wait_ge(tile_turned, 2 * i + j + 1 + EARLY)
                    if isinstance(i, int) and i == NT // 2:
                        dst = xc_t[:, :, j * P:(j + 1) * P]
                    else:
                        dst = resid[:, :, bass.ds((2 * i + j) * P, P)]
                    act.copy(dst, flat(ps[2 + j]).rearrange("p (k t) -> p k t", k=KB)).then_inc(tile_out, 1)

            with act.Fori(0, 2) as i:
                tokens(i)

            def rest():
                for i in range(2, (NT + NTC) // 2):
                    tokens(i)
                act.wait_ge(tile_out, NT + NTC + EARLY)

            def norm(st, parts, sq, t_, rs, after_root=None):
                last = parts[0][4] is None

                def square(n, k):
                    src, t0, width = parts[n][:3]
                    if n == 0 and k >= 2:
                        act.wait_ge(dve_step, st["dve"].at(f"add{max(k - 2, 1)}"))
                    elif n and k >= 2:
                        act.wait_ge(pe_step, st["pe"].at(f"s{n}{k - 2}"))
                    elif n > 1:
                        act.wait_ge(pe_step, st["pe"].at(f"s{n - 1}{KB - 2 + k}"))
                    elif n:
                        act.wait_ge(dve_step, st["dve"].at(f"add{KB - 1}"))
                    st["act"].done(act.activation(sq[k % 2][:, 0:width], src[:, k, t0:t0 + width], ACT.Square),
                                   f"sq{n}{k}")

                def root(n):
                    act.wait_ge(pe_step, st["pe"].at(f"s{n}{KB - 1}" if n else "sum0"))
                    if n:
                        act.wait_ge(dve_step, st["dve"].at(f"t{n - 1}{KB - 1}"))
                    width = parts[n][2]
                    st["act"].done(act.activation(rs[:, 0:width], ps[2 + n // 2][:, n % 2, 0:width], ACT.Sqrt,
                                                  scale=1.0 / D, bias=eps[:]), f"std{n}")

                for k in range(KB):
                    square(0, k)
                root(0)
                if after_root:
                    after_root()
                for n, (src, t0, width, shift, hi) in enumerate(parts):
                    for k in range(KB):
                        if not last:
                            act.wait_ge(dve_step, st["dve"].at(f"t{n}{k}"))
                            st["act"].done(act.activation(hi[:, k, t0:t0 + width], t_[(n * KB + k) % 3][:, 0:width],
                                                          ACT.Identity, bias=shift(k)), f"hi{n}{k}")
                        if n + 1 < len(parts):
                            square(n + 1, k)
                    if n + 1 < len(parts):
                        root(n + 1)

            act.wait_ge(tile_out, NT // 2 + EARLY)
            norm(st_n0, [(resid, 0, HALF, lambda k: mod[:, 0, k, 0:1], h_hi),
                         (resid, HALF, HALF, lambda k: mod[:, 0, k, 0:1], h_hi),
                         (xc_t, 0, TC, lambda k: mod[:, 0, k, 1:2], hc_hi)], n_sq, n_t, n_rs, rest)

            SG = st_gate
            act.wait_ge(dve_step, SG["dve"].at("f"))
            act.activation(g_e[:], g_f[:], ACT.Abs)
            act.drain()
            act.activation(g_e[:], g_e[:], ACT.Exp, scale=-1.0)
            act.drain()
            SG["act"].done(act.activation(g_e[:], g_e[:], ACT.Ln, bias=1.0), "ln")
            act.wait_ge(dve_step, SG["dve"].at("w_in"))
            SG["act"].done(act.activation(g_i[:], g_i[:], ACT.Exp), "w")
            act.wait_ge(dve_step, SG["dve"].at("e_in"))
            SG["act"].done(act.activation(g_f[:], g_f[:], ACT.Exp, scale=-1.0), "em")

            act.activation(g_small[:, 1, :], g_small[:, 1, :], ACT.Exp)
            act.drain()
            for d in range(2):
                act.dma_start(g_dram[4 * d:4 * d + 4, :], g_b[32 * d:32 * d + 4, :]).then_inc(c_rows, 16)
                act.dma_start(s_dram[4 * d:4 * d + 4, :], g_small[32 * d:32 * d + 4, 0:2, :]).then_inc(c_rows, 16)
            act.wait_ge(c_rows, 64)
            act.dma_start(chunk_sc[:].rearrange("p a b c -> p (a b c)"),
                          bcast(s_dram, 0, 16 * NCH)).then_inc(c_bc, 16)

            def gated_parts(act, SA, SD, SPE, i, y, yh, ev, done):
                act.wait_ge(dve_step, SD.at("z0", i))
                SA.done(act.activation(yh[:, 0, :], y[:, 0, :], ACT.Copy), "yh0")
                a, b = slice(0, HALF), slice(HALF, T)
                act.wait_ge(pe_step, SPE.at("half", i))
                SA.done(act.activation(ev[:, a], ps[1][:, 0, :], ACT.Silu), "silu_a")
                act.wait_ge(dve_step, SD.at("z1a", i))
                SA.done(act.activation(yh[:, 1, a], y[:, 1, a], ACT.Copy), "yh1a")
                act.wait_ge(unit_done, done + CREDIT)
                act.activation(ev[:, b], ps[1][:, 1, :], ACT.Silu).then_inc(unit_out, 1)
                act.wait_ge(dve_step, SD.at("z1b", i))
                SA.done(act.activation(yh[:, 1, b], y[:, 1, b], ACT.Copy), "yh1b")

            act.wait_ge(dve_step, SG["dve"].end)
            with act.Fori(0, HEADS) as h:
                u = h * HU
                SA, SD, SPE = st_head["act"], st_head["dve"], st_head["pe"]
                act.wait_ge(unit_done, u + CREDIT)
                act.wait_ge(dve_step, SD.at("acc7", h - 1))
                for d in range(2):
                    act.dma_start(g_bc[:, d, :], bcast(g_dram, (h + 4 * d) * (TC + T) + TC, T)).then_inc(c_gbc, 16)
                for n, name in enumerate(("q0", "q1", "k0", "k1", "v0", "v1")):
                    i = n % 2
                    act.wait_ge(unit_done, u + 1 + n + CREDIT)
                    if name[0] == "v":
                        act.copy(v_raw[i][:, 0:TC], ps[2][:, 0, 0:TC]).then_inc(ctx_out, 1)
                        act.copy(v_raw[i][:, TC:TC + T], flat(ps[i])).then_inc(unit_out, 1)
                        continue
                    before = {"q1": "q0", "k0": "q1", "k1": "k0"}.get(name)
                    if before:
                        act.wait_ge(dve_step, SD.at(f"conv_{before}", h))
                    if name[0] == "k":
                        act.copy(cbc[:, 1:TC + 1], ps[2][:, 0, 0:TC]).then_inc(ctx_out, 1)
                    act.copy(cb[:, 1:T + 1], flat(ps[i])).then_inc(unit_out, 1)
                    act.wait_ge(dve_step, SD.at(f"conv_{name}", h))
                    if name[0] == "q":
                        ins = act.activation(q_t[:, i, :], cv[:, TC:TC + T], ACT.Silu)
                    else:
                        ins = act.activation(k_t[:, i, :], cv[:], ACT.Silu)
                    SA.done(ins, f"silu_{name}")
                act.wait_ge(c_gbc, 32 * h + 32)
                act.wait_ge(c_bc, 16)
                act.wait_ge(dve_step, SD.at("vtok1", h))
                for s, (j, d) in enumerate(SEQ):
                    if j < NCH - 1:
                        if j > 0:
                            act.wait_ge(pe_step, SPE.at(f"U{j - 1}{d}", h))
                        SA.done(act.activation(kw[d][:], k_tok[:, nat_chunk(d, j), :], ACT.Copy,
                                               scale=h_cols[:, 1, nat_chunk(d, j), d:d + 1]), f"kw{j}{d}")
                    if s + 1 == len(SEQ) or SEQ[s + 1][0] < NCC:
                        continue
                    j, d = SEQ[s + 1]
                    t = (nat_chunk(d, j) - NCC) * CHUNK
                    if j > NCC:
                        act.wait_ge(dve_step, SD.at(f"Q{j - 1}{d}", h))
                    act.wait_ge(dve_step, SD.at(f"E{j}{d}", h))
                    SA.done(act.activation(ee[d][:], ee[d][:], ACT.Exp, scale=-1.0), f"D{j}{d}")
                    SA.done(act.activation(it[d][:], g_bc[:, d, t:t + CHUNK], ACT.Exp, scale=-1.0,
                                           bias=h_sc[:, d, 0, j:j + 1]), f"I{j}{d}")
                for i in range(2):
                    act.wait_ge(unit_done, u + 7 + i + CREDIT)
                    if i == 0:
                        act.wait_ge(act_step, SA.at(f"I{NCH - 1}1", h))
                    act.activation(ev_a[i][:], flat(ps[i]), ACT.Sigmoid).then_inc(unit_out, 1)
                for i in range(2):
                    act.wait_ge(dve_step, SD.at(f"o{i}", h))
                    SA.done(act.activation(k_t[:, i, 0:T], q_t[:, i, :], ACT.Square), f"sq{i}")
                act.wait_ge(pe_step, SPE.at("hsum", h))
                SA.done(act.activation(cv[:, 0:T], flat(ps[2]), ACT.Sqrt, scale=1.0 / DH, bias=eps[:]), "hstd")
                act.wait_ge(unit_done, u + 9 + CREDIT)
                act.activation(ev_a[0][:], flat(ps[0]), ACT.Silu).then_inc(unit_out, 1)
                gated_parts(act, SA, SD, SPE, h, q_t, yh2, ev_a[1], u + 10)
                accumulate(act, u + 10, ev_a, 0, SD, h)

            act.wait_ge(dve_step, st_head["dve"].end)
            act.dma_start(ct[:], tab_ct.rearrange("(b p) m -> p b m", p=P)).then_inc(c_four, 16)
            act.dma_start(ns[:], tab_ns.rearrange("(b p) m -> p b m", p=P)).then_inc(c_four, 16)
            act.dma_start(ccs[:, 0], tab_cc.rearrange("(b p) m -> p b m", p=P)).then_inc(c_four, 16)
            act.dma_start(ccs[:, 1], tab_cs.rearrange("(b p) m -> p b m", p=P)).then_inc(c_four, 16)
            with act.Fori(0, GROUPS) as g:
                u = g * FU + U_FOUR
                SA, SD, SPE = st_four["act"], st_four["dve"], st_four["pe"]
                for i in range(2):
                    act.wait_ge(unit_done, u + 1 + i + CREDIT)
                    act.copy(u_f[:, i, :], flat(ps[i])).then_inc(unit_out, 1)
                act.wait_ge(pe_step, SPE.at("cf", g))
                SA.done(act.copy(cfsf[:], ps[2][:]), "cf")
                act.wait_ge(unit_done, u + 3 + CREDIT)
                act.wait_ge(dve_step, SD.at("acc7", g - 1))
                act.activation(ev_f[0][:], flat(ps[0]), ACT.Silu).then_inc(unit_out, 1)
                for i in range(2):
                    act.wait_ge(pe_step, SPE.at(f"Y{i}", g))
                    SA.done(act.copy(y_f[:, i, :].rearrange("p (m r) -> p r m", r=RADIX),
                                     flat(ps[2 + i]).rearrange("p (r m) -> p r m", r=RADIX)), f"y{i}")
                gated_parts(act, SA, SD, SPE, g, y_f, yh_f, ev_f[1], u + 4)
                accumulate(act, u + 4, ev_f, 0, SD, g)

            act.wait_ge(dve_step, st_four["dve"].end)
            norm(st_n1, [(resid, n * HALF, HALF, lambda k: mod[:, 1, k, 0:1], h_hi) for n in range(2)],
                 m_sq, m_t, m_rs)
            act.wait_ge(dve_step, st_n1["dve"].end)

            with act.Fori(0, GROUPS) as g:
                u = g * PU + U_POOL
                SA, SD = st_pool["act"], st_pool["dve"]
                act.wait_ge(dve_step, SD.at("acc7", g - 1))
                act.dma_start(inv[:], pool_counts(g)).then_inc(c_inv, 16)
                act.copy(p_scale[:], vec[:, bass.ds(4 * g + POOL_S, 4)])
                act.drain()
                for m in range(4):
                    act.wait_ge(unit_done, u + 1 + m + CREDIT)
                    act.copy(u_p[:, m, :], flat(ps[m % 2])).then_inc(unit_out, 1)
                def high(m):
                    act.wait_ge(dve_step, SD.at(f"p{m}", g))
                    SA.done(act.activation(yh_p[:, m, :], u_p[:, m, :], ACT.Copy), f"ph{m}")

                def gate(m):
                    act.wait_ge(unit_done, u + 5 + m + CREDIT)
                    act.activation(ev_p[m][:], flat(ps[m % 2]), ACT.Silu).then_inc(unit_out, 1)

                gate(0)
                high(0)
                gate(1)
                high(1)
                high(2)
                gate(2)
                high(3)
                gate(3)
                a, b = slice(0, HALF), slice(HALF, T)
                for m in range(3):
                    act.wait_ge(unit_done, u + 9 + m + CREDIT)
                    if m == 0:
                        act.wait_ge(dve_step, SD.at("pl3", g))
                    act.activation(u_p[:, m, :], flat(ps[m % 2]), ACT.Identity, scale=p_scale[:, m:m + 1],
                                   bias=zero[:]).then_inc(unit_out, 1)
                    if m >= 1:
                        act.wait_ge(dve_step, SD.at(f"z{m - 1}", g))
                        SA.done(act.activation(yh_g[:, m - 1, :], u_p[:, m - 1, :], ACT.Copy), f"yh{m - 1}")
                act.wait_ge(pe_step, st_pool["pe"].at("half", g))
                SA.done(act.activation(u_p[:, 3, a], ps[1][:, 0, :], ACT.Identity, scale=p_scale[:, 3:4],
                                       bias=zero[:]), "scale_a")
                act.wait_ge(dve_step, SD.at("z2", g))
                SA.done(act.activation(yh_g[:, 2, :], u_p[:, 2, :], ACT.Copy), "yh2")
                act.wait_ge(unit_done, u + 12 + CREDIT)
                act.activation(u_p[:, 3, b], ps[1][:, 1, :], ACT.Identity, scale=p_scale[:, 3:4],
                               bias=zero[:]).then_inc(unit_out, 1)
                for x, half in (("a", a), ("b", b)):
                    act.wait_ge(dve_step, SD.at(f"z3{x}", g))
                    SA.done(act.activation(yh_g[:, 3, half], u_p[:, 3, half], ACT.Copy), f"yh3{x}")
                accumulate(act, u + 12, ev_p, 1, SD, g, last=3)

            act.wait_ge(dve_step, st_pool["dve"].end)
            norm(st_n2, [(resid, n * HALF, HALF, None, None) for n in range(2)], m_sq, m_t, m_rs)
            for i in range(NT // 2):
                for j in range(2):
                    act.wait_ge(pe_step, st_end["pe"].at(f"t{j}", i))
                    if i:
                        act.wait_ge(c_out[j], 16 * i)
                    st_end["act"].done(act.copy(o_tok[j][:], flat(ps[j])), f"c{j}")

        @block.vector
        def _(dve):
            def flat(bank):
                return bank[:].rearrange("p a b -> p (a b)")

            dve.memset(g_bias[:], 0.0)
            dve.memset(vrow[:], 0.0).then_inc(rows_clear, 1)
            dve.wait_ge(pe_step, st_vec["pe"].at("vecT"))
            st_vec["dve"].done(dve.tensor_copy(vec[:], ps[0][:, 0, 0:176]), "vec")

            def rows(i, j, bank=None):
                dve.wait_ge(ada_used, 2 * i + j + 1 + EARLY)
                dve.wait_ge(ada_col, 2 * i + j - 1 + EARLY)
                dve.tensor_copy(mrow[j][:], (ps[0][:, j] if bank is None else bank)[0:2, :]).then_inc(ada_row, 1)

            with dve.Fori(0, 2) as i:
                rows(i, 0)
                rows(i, 1)

            def modulate(lay, blocks):
                dve.wait_ge(ada_col, blocks)
                for s in range(2):
                    dve.tensor_tensor(mod[:, lay, :, s],
                                      ps[1][:, lay, 0:48].rearrange("p (b s) -> p b s", s=2)[:, :, s],
                                      vec[:, ADA_B + 24 * lay:ADA_B + 24 * lay + 24], ALU.add)

            def gains(n, lay, s):
                return dve.scalar_tensor_tensor(gain[:, n, :], mod[:, lay, 8:16, s], 1.0,
                                                vec[:, NORM_G + 8 * lay:NORM_G + 8 * lay + 8], ALU.add, ALU.mult)

            def first_layer():
                rows(2, 0)
                rows(2, 1)
                modulate(0, 6 + EARLY)
                dve.drain()
                gains(0, 0, 0)
                gains(1, 0, 1)

            def gate_weights():
                dve.wait_ge(tile_turned, NT + NTC + EARLY)
                dve.memset(g_w[:], 0.0)
                dve.wait_ge(c_gate, 16 * 5)
                dve.drain()
                for kind in range(2):
                    for d in range(2):
                        row = 2 * d + kind
                        dve.tensor_copy(g_w[:, :, 64 * kind + 32 * d:64 * kind + 32 * d + 4],
                                        g_in[:, :, 4 * row:4 * row + 4])
                dve.drain()
                dve.tensor_copy(g_wh[:], g_w[:])
                dve.drain()
                dve.tensor_tensor(g_wl[:], g_w[:], g_wh[:].bitcast(F32), ALU.subtract)

            def after_part(n):
                if n == 0:
                    gate_weights()
                else:
                    rows(n + 2, 0)
                    rows(n + 2, 1)

            def norm(st, parts, sq, t_, rs, meanwhile=None, between=None):
                width = parts[0][2]
                for k in range(1, KB):
                    dve.wait_ge(act_step, st["act"].at(f"sq0{k}"))
                    st["dve"].done(dve.tensor_tensor(t_[0][:, 0:width], (sq[0] if k == 1 else t_[0])[:, 0:width],
                                                     sq[k % 2][:, 0:width], ALU.add), f"add{k}")
                    dve.drain()
                if meanwhile:
                    meanwhile()
                for n, (src, t0, width, gain_col, shift, hi, lo) in enumerate(parts):
                    dve.wait_ge(act_step, st["act"].at(f"std{n}"))
                    st["dve"].done(dve.reciprocal(rs[:, 0:width], rs[:, 0:width]), f"rs{n}")
                    dve.drain()

                    def low(k):
                        dve.wait_ge(act_step, st["act"].at(f"hi{n}{k}"))
                        st["dve"].done(dve.scalar_tensor_tensor(lo[:, k, t0:t0 + width],
                                                                t_[(n * KB + k) % 3][:, 0:width],
                                                                shift(k), hi[:, k, t0:t0 + width].bitcast(F32),
                                                                ALU.add, ALU.subtract), f"lo{n}{k}")

                    for k in range(KB):
                        cell = src[:, k, t0:t0 + width]
                        turn = n * KB + k
                        if hi is not None and turn >= 3:
                            dve.wait_ge(dve_step, st["dve"].at(f"lo{(turn - 3) // KB}{(turn - 3) % KB}"))
                        st["dve"].done(dve.scalar_tensor_tensor(cell if hi is None else t_[turn % 3][:, 0:width], cell,
                                                                gain_col(k), rs[:, 0:width], ALU.mult, ALU.mult),
                                       f"t{n}{k}")
                        if k >= 1 and hi is not None:
                            low(k - 1)
                    if hi is not None:
                        low(KB - 1)
                    if between:
                        between(n)

            norm(st_n0, [(resid, 0, HALF, lambda k: gain[:, 0, k:k + 1], lambda k: mod[:, 0, k, 0:1], h_hi, h_lo),
                         (resid, HALF, HALF, lambda k: gain[:, 0, k:k + 1], lambda k: mod[:, 0, k, 0:1], h_hi, h_lo),
                         (xc_t, 0, TC, lambda k: gain[:, 1, k:k + 1], lambda k: mod[:, 0, k, 1:2], hc_hi, hc_lo)],
                 n_sq, n_t, n_rs, first_layer, after_part)
            def gated_parts(SA, SD, i, gated, y, yh, yl, silu):
                dve.wait_ge(unit_out, silu + CREDIT)
                SD.done(gated(0, slice(0, T)), "z0")
                dve.wait_ge(act_step, SA.at("yh0", i))
                SD.done(dve.tensor_tensor(yl[:, 0, :], y[:, 0, :], yh[:, 0, :].bitcast(F32), ALU.subtract), "yl0")
                for x, half in (("a", slice(0, HALF)), ("b", slice(HALF, T))):
                    if x == "a":
                        dve.wait_ge(act_step, SA.at("silu_a", i))
                    else:
                        dve.wait_ge(unit_out, silu + 1 + CREDIT)
                    SD.done(gated(1, half), f"z1{x}")
                    dve.wait_ge(act_step, SA.at(f"yh1{x}", i))
                    SD.done(dve.tensor_tensor(yl[:, 1, half], y[:, 1, half], yh[:, 1, half].bitcast(F32),
                                              ALU.subtract), f"yl1{x}")

            SG = st_gate
            dve.wait_ge(ada_used, 11 + EARLY)
            dve.memset(g_s[:], 1.0)
            dve.memset(g_d[:], 0.0)
            dve.memset(g_small[:], 0.0)
            dve.wait_ge(pe_step, SG["pe"].at("gates"))
            for kind, dst in ((1, g_f), (0, g_i)):
                r0, r1, r2 = 64 * kind, 64 * kind + 32, 64 * kind + 64
                dve.tensor_scalar(dst[0:32, 0:TC], ps[3][r0:r1, 0, 0:TC], g_bias[r0:r1], None, ALU.add)
                dve.tensor_scalar(dst[0:32, TC:TC + T], flat(ps[2])[r0:r1], g_bias[r0:r1], None, ALU.add)
                dve.tensor_scalar(dst[32:64, 0:TC], ps[3][r1:r2, 0, 0:TC][:, ::-1], g_bias[r1:r2], None, ALU.add)
                ins = dve.tensor_scalar(dst[32:64, TC:TC + T], flat(ps[2])[r1:r2][:, ::-1], g_bias[r1:r2], None,
                                        ALU.add)
                if kind == 1:
                    SG["dve"].done(ins, "f")
            dve.drain()
            dve.memset(g_s[:, ::CHUNK], 0.0)
            rows(5, 0, bank=ps[3][:, 1])
            rows(5, 1)
            dve.wait_ge(act_step, SG["act"].at("ln"))
            dve.scalar_tensor_tensor(g_f[:], g_f[:], 0.0, g_e[:], ALU.min, ALU.subtract)
            dve.drain()
            dve.tensor_tensor_scan(g_b[:], g_s[:], g_f[:], 0.0, ALU.mult, ALU.add)
            dve.drain()
            dve.tensor_tensor(g_i[:], g_i[:], g_b[:], ALU.subtract)
            dve.tensor_copy(g_d[:, CHUNK::CHUNK], g_b[:, CHUNK - 1:TC + T - CHUNK:CHUNK])
            dve.drain()
            SG["dve"].done(dve.tensor_tensor_scan(g_g[:], g_d[:], g_i[:], 0.0, ALU.add, ALU.max), "G")
            dve.wait_ge(dve_step, SG["dve"].at("G"))

            def natural(dst, src):
                dve.tensor_copy(dst[0:32, :], src[0:32, :])
                dve.tensor_copy(dst[32:64, 0:TC], src[32:64, 0:TC][:, ::-1])
                return dve.tensor_copy(dst[32:64, TC:TC + T], src[32:64, TC:TC + T][:, ::-1])

            ch = lambda a: a[:].rearrange("p (c t) -> p c t", t=CHUNK)
            SG["dve"].done(natural(g_nat, g_i), "g_nat")
            dve.tensor_tensor(g_small[:, 0, 1:NCH], g_g[:, CHUNK - 1:TC + T - CHUNK:CHUNK],
                              g_b[:, CHUNK - 1:TC + T - CHUNK:CHUNK], ALU.add)
            dve.tensor_copy(g_small[:, 2, :], g_g[:, CHUNK - 1::CHUNK])
            dve.drain()
            SG["dve"].done(dve.tensor_tensor(g_small[:, 1, :], g_small[:, 0, :], g_small[:, 2, :], ALU.subtract),
                           "a_nat")
            SG["dve"].done(dve.tensor_tensor(ch(g_i), ch(g_i),
                                             g_small[:, 2, :].unsqueeze(2).to_broadcast([64, NCH, CHUNK]),
                                             ALU.subtract), "w_in")
            dve.tensor_tensor(g_f[:], g_b[:], g_g[:], ALU.add)
            dve.drain()
            dve.wait_ge(act_step, SG["act"].at("w"))
            SG["dve"].done(natural(g_s, g_i), "w_nat")
            SG["dve"].done(natural(g_b, g_g), "e_in")
            dve.wait_ge(act_step, SG["act"].at("em"))
            SG["dve"].done(natural(g_e, g_f), "e_nat")
            dve.drain()
            for n, (name, bank) in enumerate((("colsA", ps[0]), ("colsW", ps[2]), ("colsE", ps[3]))):
                dve.wait_ge(pe_step, SG["pe"].at(name))
                for lo_, hi_ in ((0, 8), (8, NCH)):
                    dve.tensor_copy(
                        cols[:, n, lo_:hi_, :].rearrange("p c (d r) -> p c d r", d=2),
                        bank[:, lo_ // 8, 0:(hi_ - lo_) * 64].rearrange("p (c d r) -> p c d r", d=2, r=32)[:, :, :, 0:4])
            dve.drain()
            dve.tensor_scalar(cols[:, 1], cols[:, 1], float(DH) ** -0.5, None, ALU.mult)
            modulate(1, 12 + EARLY)
            dve.drain()
            SG["dve"].done(gains(2, 1, 0), "cols")
            dve.drain()

            dve.wait_ge(c_const, 32)
            with dve.Fori(0, HEADS) as h:
                u = h * HU
                SA, SD, SPE = st_head["act"], st_head["dve"], st_head["pe"]
                sc = float(DH) ** -0.5
                for d in DIRS:
                    dve.tensor_copy(h_cols[:, :, :, d:d + 1], cols[:, :, :, bass.ds(h + 4 * d, 1)])
                dve.memset(cb[:, 0:T + 2:T + 1], 0.0)
                dve.memset(cbc[:, 0:TC + 2:TC + 1], 0.0)
                for n, name in enumerate(("q0", "q1", "k0", "k1")):
                    if n == 0:
                        dve.drain()
                    wcol = lambda tap: vec[:, bass.ds(2 * h + (CONV + 16 * tap + 8 * (n // 2) + n % 2), 1)]
                    dve.wait_ge(unit_out, u + n + 1 + CREDIT)
                    if n:
                        dve.wait_ge(act_step, SA.at(f"silu_{('q0', 'q1', 'k0')[n - 1]}", h))
                    parts = [(cb, T, slice(TC, TC + T))]
                    if n >= 2:
                        parts.append((cbc, TC, slice(0, TC)))
                    for src, w, dst in parts:
                        dve.tensor_scalar(cv[:, dst], src[:, 0:w], wcol(0), None, ALU.mult)
                    dve.drain()
                    for src, w, dst in parts:
                        dve.scalar_tensor_tensor(cv[:, dst], src[:, 1:w + 1], wcol(1), cv[:, dst], ALU.mult, ALU.add)
                    dve.drain()
                    for src, w, dst in parts:
                        ins = dve.scalar_tensor_tensor(cv[:, dst], src[:, 2:w + 2], wcol(2), cv[:, dst], ALU.mult,
                                                       ALU.add)
                    SD.done(ins, f"conv_{name}")
                dve.wait_ge(c_bc, 16)
                for d in DIRS:
                    dve.tensor_copy(h_sc[:, d:d + 1], chunk_sc[:, bass.ds(h + 4 * d, 1)])
                dve.memset(v_tok[:, :, DH:DH + 1], 1.0)
                dve.memset(cst[:], 0.0)
                for name, dst in (("k", k_tok), ("v", v_tok)):
                    for i in range(2):
                        dve.wait_ge(pe_step, SPE.at(f"{name}T{i}", h))
                        SD.done(gather(dve, dst, i), f"{name}tok{i}")
                dve.wait_ge(c_gbc, 32 * h + 32)
                dve.wait_ge(dve_step, SD.at("vtok1", h))
                col = lambda arr, n, d: h_cols[:, arr, n, d:d + 1]

                def exponent(j, d):
                    n = nat_chunk(d, j)
                    t = (n - NCC) * CHUNK
                    SD.done(dve.scalar_tensor_tensor(ee[d][:], g_bc[:, d, t:t + CHUNK], col(0, n, d),
                                                     mask[:, d, :], ALU.subtract, ALU.add), f"E{j}{d}")

                def front(j, d):
                    n = nat_chunk(d, j)
                    t = (n - NCC) * CHUNK
                    if j >= NCC:
                        dve.wait_ge(pe_step, SPE.at(f"S{j}{d}", h))
                        dve.wait_ge(act_step, SA.at(f"D{j}{d}", h))
                        SD.done(dve.scalar_tensor_tensor(pr[d][:], ps[0][:, d, 0:CHUNK], sc, ee[d][:], ALU.mult,
                                                         ALU.mult), f"P{j}{d}")
                        dve.wait_ge(act_step, SA.at(f"I{j}{d}", h))
                        SD.done(dve.tensor_tensor(qi[d][:], q_t[:, :, t:t + CHUNK],
                                                  it[d][:].unsqueeze(1).to_broadcast([P, 2, CHUNK]), ALU.mult),
                                f"Q{j}{d}")

                def back(j, d):
                    n = nat_chunk(d, j)
                    if j >= NCC:
                        nb = ps[1][:, d, :]
                        dve.wait_ge(pe_step, SPE.at(f"N{j}{d}", h))
                        den = nb[:, DH:DH + 1]
                        dve.tensor_scalar(dn[:, d, 0:1], den, -1.0, col(2, n, d), ALU.mult, ALU.max)
                        dve.drain()
                        dve.tensor_tensor(dn[:, d, 1:2], dn[:, d, 0:1], den, ALU.max)
                        dve.drain()
                        dve.reciprocal(dn[:, d, 2:3], dn[:, d, 1:2])
                        dve.drain()
                        hs = h_tok[:, n - NCC, :]
                        if j - NCC < NCX // 2:
                            ins = dve.tensor_scalar(hs, nb[:, 0:DH], dn[:, d, 2:3], None, ALU.mult)
                        else:
                            ins = dve.scalar_tensor_tensor(hs, nb[:, 0:DH], dn[:, d, 2:3], hs, ALU.mult, ALU.add)
                        SD.done(ins, f"h{j}{d}")
                    if j < NCH - 1:
                        dve.wait_ge(pe_step, SPE.at(f"U{j}{d}", h))
                        dec = h_sc[:, d, 1, j:j + 1]
                        for i in range(2):
                            ins = dve.scalar_tensor_tensor(cst[:, d, i, :], cst[:, d, i, :], dec,
                                                           ps[2 + d][:, i, 0:DH + 1], ALU.mult, ALU.add)
                        SD.done(ins, f"C{j}{d}")

                for s, (j, d) in enumerate(SEQ):
                    if s + 1 < len(SEQ) and SEQ[s + 1][0] >= NCC:
                        exponent(*SEQ[s + 1])
                    front(j, d)
                    if s:
                        back(*SEQ[s - 1])
                        dve.drain()
                back(*SEQ[-1])
                for i in range(2):
                    dve.wait_ge(pe_step, SPE.at(f"hT{i}", h))
                    SD.done(dve.tensor_copy(q_t[:, i, :], flat(ps[2 + i])), f"hf{i}")
                dve.wait_ge(dve_step, SD.at("hf1", h))
                for i in range(2):
                    dve.wait_ge(unit_out, u + 7 + i + CREDIT)
                    SD.done(dve.tensor_tensor(q_t[:, i, :], q_t[:, i, :], ev_a[i][:], ALU.mult), f"o{i}")
                dve.wait_ge(act_step, SA.at("hstd", h))
                dve.reciprocal(cv[:, 0:T], cv[:, 0:T])
                dve.drain()
                for i in range(2):
                    ins = dve.tensor_tensor(q_t[:, i, :], q_t[:, i, :], cv[:, 0:T], ALU.mult)
                SD.done(ins, "hrs")
                dve.wait_ge(dve_step, SD.at("hrs", h))

                def gated(i, s):
                    return dve.scalar_tensor_tensor(q_t[:, i, s], q_t[:, i, s],
                                                    vec[:, bass.ds(2 * h + HEAD_G + i, 1)], ev_a[i][:, s],
                                                    ALU.mult, ALU.mult)

                gated_parts(SA, SD, h, gated, q_t, yh2, yl2, u + 9)
                add_up(dve, u + 10, ev_a, SD, h)

            with dve.Fori(0, GROUPS) as g:
                u = g * FU + U_FOUR
                SA, SD, SPE = st_four["act"], st_four["dve"], st_four["pe"]
                dve.wait_ge(unit_out, u + 2 + CREDIT)
                uq = lambda q: u_f[:].rearrange("p c (q t) -> p c q t", q=RADIX)[:, :, q, :]
                dve.tensor_tensor(f_tmp[:, :, 0, :], uq(0), uq(2), ALU.add)
                dve.tensor_tensor(f_tmp[:, :, 1, :], uq(1), uq(3), ALU.add)
                dve.tensor_tensor(fd[:, :, 1, :], uq(0), uq(2), ALU.subtract)
                dve.tensor_tensor(fd[:, :, 3, :], uq(1), uq(3), ALU.subtract)
                dve.drain()
                dve.tensor_tensor(fd[:, :, 0, :], f_tmp[:, :, 0, :], f_tmp[:, :, 1, :], ALU.add)
                SD.done(dve.tensor_tensor(fd[:, :, 2, :], f_tmp[:, :, 0, :], f_tmp[:, :, 1, :], ALU.subtract), "fold")
                lo_, hi_ = slice(0, DH), slice(DH, 2 * DH)
                for n, (arr, tb) in enumerate(((0, 0), (0, 1), (2, 0), (2, 1), (3, 0), (1, 0), (3, 1), (1, 1))):
                    bank = ps[2 + (n % 4) // 2][:, n % 2, :]
                    if n > 4:
                        dve.drain()
                    dve.wait_ge(pe_step, SPE.at(f"V{n}", g))
                    if arr in (0, 2):
                        ins = dve.tensor_copy(pq[:, tb, arr, :], bank)
                    elif arr == 3:
                        ins = dve.tensor_copy(f_b[:], bank)
                    else:
                        dve.tensor_tensor(pq[:, tb, 1, lo_], bank[:, lo_], f_b[:, hi_], ALU.subtract)
                        dve.tensor_tensor(pq[:, tb, 1, hi_], bank[:, hi_], f_b[:, lo_], ALU.add)
                        dve.tensor_tensor(pq[:, tb, 3, lo_], bank[:, lo_], f_b[:, hi_], ALU.add)
                        ins = dve.tensor_tensor(pq[:, tb, 3, hi_], bank[:, hi_], f_b[:, lo_], ALU.subtract)
                    SD.done(ins, f"V{n}")
                dve.wait_ge(act_step, SA.at("y1", g))
                gated_parts(SA, SD, g, lambda i, s: dve.tensor_tensor(y_f[:, i, s], y_f[:, i, s], ev_f[i][:, s],
                                                                      ALU.mult), y_f, yh_f, yl_f, u + 3)
                add_up(dve, u + 4, ev_f, SD, g)

            dve.drain()
            norm(st_n1, [(resid, n * HALF, HALF, lambda k: gain[:, 2, k:k + 1], lambda k: mod[:, 1, k, 0:1],
                          h_hi, h_lo) for n in range(2)], m_sq, m_t, m_rs)
            dve.drain()

            for g, win in enumerate(WINDOWS):
                u = g * PU + U_POOL
                SA, SD = st_pool["act"], st_pool["dve"]
                half = win // 2
                for m in range(4):
                    dve.wait_ge(unit_out, u + 1 + m + CREDIT)
                    if m == 0:
                        dve.wait_ge(c_inv, 16 * g + 16)
                    rows_n = GRID_H + win - 1
                    a, bbuf = pt[0], pt[1]
                    dve.memset(a[:, 0:half * GRID_W], 0.0)
                    if win - 1 - half:
                        dve.memset(a[:, (half + GRID_H) * GRID_W:rows_n * GRID_W], 0.0)
                    dve.tensor_copy(a[:, half * GRID_W:half * GRID_W + T], u_p[:, m, :])
                    dve.drain()
                    step, left = 1, rows_n
                    while step < win:
                        left -= step
                        dve.tensor_tensor(bbuf[:, 0:left * GRID_W], a[:, 0:left * GRID_W],
                                          a[:, step * GRID_W:(step + left) * GRID_W], ALU.add)
                        dve.drain()
                        a, bbuf = bbuf, a
                        step *= 2
                    assert left == GRID_H
                    cw = GRID_W + win - 1
                    bv = bbuf[:, 0:GRID_H * cw].rearrange("p (r c) -> p r c", c=cw)
                    dve.memset(bv[:, :, 0:half], 0.0)
                    if win - 1 - half:
                        dve.memset(bv[:, :, half + GRID_W:cw], 0.0)
                    dve.tensor_copy(bv[:, :, half:half + GRID_W],
                                    a[:, 0:T].rearrange("p (r c) -> p r c", c=GRID_W))
                    dve.drain()
                    a, bbuf = bbuf, a
                    step, left = 1, cw
                    while step < win:
                        left -= step
                        av = a[:, 0:GRID_H * cw].rearrange("p (r c) -> p r c", c=cw)
                        ov = bbuf[:, 0:GRID_H * cw].rearrange("p (r c) -> p r c", c=cw)
                        dve.tensor_tensor(ov[:, :, 0:left], av[:, :, 0:left], av[:, :, step:step + left], ALU.add)
                        dve.drain()
                        a, bbuf = bbuf, a
                        step *= 2
                    av = a[:, 0:GRID_H * cw].rearrange("p (r c) -> p r c", c=cw)[:, :, 0:GRID_W]
                    dve.tensor_tensor(bbuf[:, 0:T].rearrange("p (r c) -> p r c", c=GRID_W), av,
                                      inv[:].rearrange("p (r c) -> p r c", c=GRID_W), ALU.mult)
                    dve.drain()
                    SD.done(dve.tensor_tensor(u_p[:, m, :], bbuf[:, 0:T], u_p[:, m, :], ALU.subtract), f"p{m}")
                    dve.drain()
                for m in range(4):
                    dve.wait_ge(act_step, SA.at(f"ph{m}", g))
                    SD.done(dve.tensor_tensor(yl_p[:, m, :], u_p[:, m, :], yh_p[:, m, :].bitcast(F32), ALU.subtract),
                            f"pl{m}")
                def gated(m, s):
                    return dve.tensor_tensor(u_p[:, m, s], u_p[:, m, s], ev_p[m][:, s], ALU.mult)

                def low(m, s, x=""):
                    dve.wait_ge(act_step, SA.at(f"yh{m}{x}", g))
                    SD.done(dve.tensor_tensor(yl_g[:, m, s], u_p[:, m, s], yh_g[:, m, s].bitcast(F32),
                                              ALU.subtract), f"yl{m}{x}")

                full, a, b = slice(0, T), slice(0, HALF), slice(HALF, T)
                for m in range(3):
                    dve.wait_ge(unit_out, u + 9 + m + CREDIT)
                    SD.done(gated(m, full), f"z{m}")
                    if m >= 1:
                        low(m - 1, full)
                dve.wait_ge(act_step, SA.at("scale_a", g))
                SD.done(gated(3, a), "z3a")
                low(2, full)
                dve.wait_ge(unit_out, u + 12 + CREDIT)
                SD.done(gated(3, b), "z3b")
                low(3, a, "a")
                low(3, b, "b")
                add_up(dve, u + 12, ev_p, SD, g)

            dve.drain()
            norm(st_n2, [(resid, n * HALF, HALF, lambda k: vec[:, FINAL_G + k:FINAL_G + k + 1], None, None, None)
                         for n in range(2)], m_sq, m_t, m_rs)


def tables():
    t = np.arange(TF)[:, None].astype(np.float64)
    k = (RADIX * np.arange(TF)[None, :] + np.arange(RADIX)[:, None]).reshape(1, T)
    ang = 2 * np.pi * ((t * k) % T) / T
    norm = 1.0 / np.sqrt(T * DH)
    cidx = np.arange(DH)
    cang = 2 * np.pi * (np.outer(cidx, cidx) % DH) / DH
    s, q = np.arange(CHUNK)[:, None], np.arange(CHUNK)[None, :]
    mask = np.stack([np.where(s <= q, 0.0, BIG), np.where(s >= q, 0.0, BIG)], axis=1)
    inv = []
    for w in WINDOWS:
        def count(n):
            i = np.arange(n)
            return np.clip(i + w - w // 2, 0, n) - np.clip(i - w // 2, 0, n)
        inv.append(1.0 / np.outer(count(GRID_H), count(GRID_W)).reshape(-1))
    f = lambda a: np.ascontiguousarray(a, dtype=np.float32)
    return {"ident": f(np.eye(P)), "mask": f(mask), "ct": f(np.cos(ang) * norm), "ns": f(-np.sin(ang) * norm),
            "cc": f(np.cos(cang)), "cs": f(np.sin(cang)), "inv": f(np.stack(inv))}


_INS = ['x', 'c', 'ctx', 'c_ctx', 'ada_w', 'ada_b', 'norm_g', 'win_even', 'gate_b_even', 'conv_qk_even',
        'head_norm_even', 'fourier_w_even', 'wout_even', 'win_odd', 'pool_w_odd', 'pool_scale_odd', 'wout_odd',
        'final_g']
_OUT = ((1, 1024, 1024), 'float32')


def kernel(**inputs):
    import numpy as _np
    import concourse.bacc as _bacc
    from concourse import mybir as _mybir
    from concourse.bass_utils import run_bass_kernel_spmd as _run

    nc = _bacc.Bacc("TRN2", target_bir_lowering=False, num_devices=1)
    arrays, args = {}, []
    for name, a in [(n, inputs[n]) for n in _INS] + list(tables().items()):
        a = _np.ascontiguousarray(a)
        arrays[f"in_{name}_dram"] = a
        args.append(nc.dram_tensor(f"in_{name}_dram", a.shape, _mybir.dt.from_np(a.dtype), kind="ExternalInput").ap())
    args.append(nc.dram_tensor("out_0_dram", _OUT[0], _mybir.dt.from_np(_np.dtype(_OUT[1])),
                               kind="ExternalOutput").ap())
    program(nc, *args)
    r = _run(nc, [arrays], core_ids=[0])
    return r.results[0]["out_0_dram"]
```
